# Optimizing a Trainium2 kernel written in Bass

```python
import math
import jax, jax.numpy as jnp
from jax import lax
import numpy as np

D_MODEL = 1024
BATCH = 1
SEQ = 256
DEPTH = 2

N_ATTN_HEADS = 8
HEAD_DIM = 64
ATTN_WIDTH = N_ATTN_HEADS * HEAD_DIM
CONV_WIDTH = D_MODEL - ATTN_WIDTH
CONV_GROUPS = 8
MIX_WIDTH = ATTN_WIDTH + CONV_WIDTH
CONV_KERNEL = 31
IDX_HEADS = 8
IDX_DIM = 64
TOPK_KEYS = 256
ROPE_THETA = 500000.0
ROPE_DIM = HEAD_DIM // 4
Q_BLOCK = 128
PEER_HEADS = 8
PEER_KEYS = 128
PEER_EXPERTS = PEER_KEYS * PEER_KEYS
PEER_QDIM = 256
PEER_TOPK = 16
PEER_BLOCK = 128
NORM_EPS = 1e-6
IN_SIZES = (ATTN_WIDTH, ATTN_WIDTH, ATTN_WIDTH, IDX_HEADS * IDX_DIM, IDX_DIM, IDX_HEADS, 2 * CONV_WIDTH)
IN_COLS = 3 * ATTN_WIDTH + IDX_HEADS * IDX_DIM + IDX_DIM + IDX_HEADS + 2 * CONV_WIDTH

kernel_name = "hymba_dsa_conformer_peer_trunk"

F32 = jnp.float32

def rms_norm(x, gain=None, eps=NORM_EPS):
    xf = x.astype(F32)
    y = xf * lax.rsqrt(jnp.mean(xf * xf, axis=-1, keepdims=True) + eps)
    if gain is not None:
        y = y * gain.astype(F32)
    return y.astype(x.dtype)

def layer_norm(x, gain, bias, eps=NORM_EPS):
    xf = x.astype(F32)
    mu = jnp.mean(xf, axis=-1, keepdims=True)
    var = jnp.mean(jnp.square(xf - mu), axis=-1, keepdims=True)
    y = (xf - mu) * lax.rsqrt(var + eps) * gain.astype(F32) + bias.astype(F32)
    return y.astype(x.dtype)

def rope_tables(positions):
    inv_freq = jnp.power(jnp.float32(ROPE_THETA), -jnp.arange(0, ROPE_DIM, 2, dtype=F32) / ROPE_DIM)
    ang = positions.astype(F32)[..., None] * inv_freq
    return jnp.cos(ang)[:, :, None, :], jnp.sin(ang)[:, :, None, :]

def partial_rope(x, cos, sin):
    half = ROPE_DIM // 2
    x1, x2, xp = x[..., :half], x[..., half:ROPE_DIM], x[..., ROPE_DIM:]
    c = cos.astype(x.dtype)
    s = sin.astype(x.dtype)
    return jnp.concatenate([x1 * c - x2 * s, x2 * c + x1 * s, xp], axis=-1)

def split_offsets():
    return [int(v) for v in np.cumsum(np.array(IN_SIZES))[:-1]]

def dsa_attention(q, k, v, q_idx, k_idx, w_idx):
    B, T = q.shape[0], q.shape[1]
    n_sel = min(TOPK_KEYS, T // 4)
    nb = T // Q_BLOCK

    def to_blocks(a):
        return jnp.swapaxes(a.reshape((B, nb, Q_BLOCK) + a.shape[2:]), 0, 1)

    starts = jnp.arange(nb, dtype=jnp.int32) * Q_BLOCK
    kpos = jnp.arange(T, dtype=jnp.int32)
    idx_scale = IDX_DIM ** -0.5
    w_scale = IDX_HEADS ** -0.5
    attn_scale = HEAD_DIM ** -0.5
    k_idx_f = k_idx.astype(F32)

    def block(args):
        qb, qib, wb, start = args
        qpos = start + jnp.arange(Q_BLOCK, dtype=jnp.int32)
        causal = kpos[None, :] <= qpos[:, None]
        dots = jnp.einsum('bqhd,bkd->bqhk', qib.astype(F32), k_idx_f) * idx_scale
        score = jnp.einsum('bqh,bqhk->bqk', wb.astype(F32) * w_scale, jax.nn.relu(dots))
        score = jnp.where(causal[None], score, -jnp.inf)
        _, sel = lax.top_k(score, n_sel)
        valid = sel <= qpos[None, :, None]
        kg = jax.vmap(lambda kb, ib: kb[ib])(k, sel)
        vg = jax.vmap(lambda vb, ib: vb[ib])(v, sel)
        logits = jnp.einsum('bqhd,bqnhd->bhqn', qb.astype(F32), kg.astype(F32)) * attn_scale
        logits = jnp.where(valid[:, None], logits, -jnp.inf)
        p = jax.nn.softmax(logits, axis=-1)
        o = jnp.einsum('bhqn,bqnhd->bqhd', p, vg.astype(F32))
        return o.astype(q.dtype)

    out = lax.map(block, (to_blocks(q), to_blocks(q_idx), to_blocks(w_idx), starts))
    return jnp.swapaxes(out, 0, 1).reshape(B, T, N_ATTN_HEADS, HEAD_DIM)

def conformer_conv(u, w_dw, b_dw, ln_g, ln_b):
    a, g = jnp.split(u, 2, axis=-1)
    h = a * jax.nn.sigmoid(g)
    h = lax.conv_general_dilated(
        h, w_dw[:, None, :].astype(h.dtype), window_strides=(1,),
        padding=((CONV_KERNEL - 1, 0),), dimension_numbers=('NWC', 'WIO', 'NWC'),
        feature_group_count=CONV_WIDTH) + b_dw.astype(h.dtype)
    h = layer_norm(h, ln_g, ln_b)
    return jax.nn.silu(h)

def peer_ffn(h, w_q, sub_keys, exp_u, exp_v):
    B, T, D = h.shape
    nb = T // PEER_BLOCK
    half = PEER_QDIM // 2
    hb = jnp.swapaxes(h.reshape(B, nb, PEER_BLOCK, D), 0, 1)

    def block(xb):
        q = (xb @ w_q).reshape(B, PEER_BLOCK, PEER_HEADS, 2, half)
        s = jnp.einsum('bthpd,hpnd->bthpn', q.astype(F32), sub_keys.astype(F32))
        s1, i1 = lax.top_k(s[..., 0, :], PEER_TOPK)
        s2, i2 = lax.top_k(s[..., 1, :], PEER_TOPK)
        cand = (s1[..., :, None] + s2[..., None, :]).reshape(B, PEER_BLOCK, PEER_HEADS, PEER_TOPK * PEER_TOPK)
        cand_idx = (i1[..., :, None] * PEER_KEYS + i2[..., None, :]).reshape(B, PEER_BLOCK, PEER_HEADS, PEER_TOPK * PEER_TOPK)
        top_s, pos = lax.top_k(cand, PEER_TOPK)
        e = jnp.take_along_axis(cand_idx, pos, axis=-1)
        g = jax.nn.softmax(top_s, axis=-1)
        u = exp_u[e]
        act = jax.nn.gelu(jnp.einsum('btd,bthkd->bthk', xb.astype(F32), u.astype(F32)), approximate=False)
        coef = (g * act).astype(xb.dtype)
        vv = exp_v[e]
        return jnp.einsum('bthk,bthkd->btd', coef, vv)

    out = lax.map(block, hb)
    return jnp.swapaxes(out, 0, 1).reshape(B, T, D)

def setup_inputs(seed: int = 0) -> dict:
    key = jax.random.key(seed)
    ks = jax.random.split(key, 24)
    n = jax.random.normal
    L, D = DEPTH, D_MODEL
    x = n(ks[0], (BATCH, SEQ, D), F32)
    c = n(ks[1], (BATCH, D), F32)
    positions = jnp.broadcast_to(jnp.arange(SEQ, dtype=jnp.int32)[None, :], (BATCH, SEQ))
    w_ada = n(ks[2], (L, D, 6 * D), F32) * (0.5 * D ** -0.5)
    b_ada = n(ks[3], (L, 6 * D), F32) * 0.02
    w_in = n(ks[4], (L, D, IN_COLS), F32) * D ** -0.5
    q_norm_g = 1.0 + 0.02 * n(ks[5], (L, HEAD_DIM), F32)
    k_norm_g = 1.0 + 0.02 * n(ks[6], (L, HEAD_DIM), F32)
    idx_k_ln_g = 1.0 + 0.02 * n(ks[7], (L, IDX_DIM), F32)
    idx_k_ln_b = 0.02 * n(ks[8], (L, IDX_DIM), F32)
    conv_dw = n(ks[9], (L, CONV_KERNEL, CONV_WIDTH), F32) * CONV_KERNEL ** -0.5
    conv_b = 0.02 * n(ks[10], (L, CONV_WIDTH), F32)
    conv_ln_g = 1.0 + 0.02 * n(ks[11], (L, CONV_WIDTH), F32)
    conv_ln_b = 0.02 * n(ks[12], (L, CONV_WIDTH), F32)
    out_g_attn = 1.0 + 0.02 * n(ks[13], (L, ATTN_WIDTH), F32)
    out_g_conv = 1.0 + 0.02 * n(ks[14], (L, CONV_WIDTH), F32)
    w_out = n(ks[15], (L, MIX_WIDTH, D), F32) * MIX_WIDTH ** -0.5
    peer_wq = n(ks[16], (L, D, PEER_HEADS * PEER_QDIM), F32) * D ** -0.5
    peer_sub_keys = n(ks[17], (L, PEER_HEADS, 2, PEER_KEYS, PEER_QDIM // 2), F32) * (PEER_QDIM // 2) ** -0.5
    peer_u = n(ks[18], (L, PEER_EXPERTS, D), F32) * D ** -0.5
    peer_v = n(ks[19], (L, PEER_EXPERTS, D), F32) * PEER_HEADS ** -0.5
    return {"x": x, "c": c, "positions": positions, "w_ada": w_ada, "b_ada": b_ada,
            "w_in": w_in, "q_norm_g": q_norm_g, "k_norm_g": k_norm_g,
            "idx_k_ln_g": idx_k_ln_g, "idx_k_ln_b": idx_k_ln_b, "conv_dw": conv_dw,
            "conv_b": conv_b, "conv_ln_g": conv_ln_g, "conv_ln_b": conv_ln_b,
            "out_g_attn": out_g_attn, "out_g_conv": out_g_conv, "w_out": w_out,
            "peer_wq": peer_wq, "peer_sub_keys": peer_sub_keys, "peer_u": peer_u,
            "peer_v": peer_v}

def reference(x, c, positions, w_ada, b_ada, w_in, q_norm_g, k_norm_g, idx_k_ln_g,
              idx_k_ln_b, conv_dw, conv_b, conv_ln_g, conv_ln_b, out_g_attn, out_g_conv,
              w_out, peer_wq, peer_sub_keys, peer_u, peer_v):
    B, T, D = x.shape
    cos, sin = rope_tables(positions)
    c_act = jax.nn.silu(c)
    offs = split_offsets()
    for l in range(DEPTH):
        mod = (c_act @ w_ada[l] + b_ada[l])[:, None, :]
        sh1, sc1, g1, sh2, sc2, g2 = jnp.split(mod, 6, axis=-1)
        h = rms_norm(x) * (1.0 + sc1) + sh1
        proj = h @ w_in[l]
        q, k, v, qi, ki, wi, cu = jnp.split(proj, offs, axis=-1)
        q = partial_rope(rms_norm(q.reshape(B, T, N_ATTN_HEADS, HEAD_DIM), q_norm_g[l]), cos, sin)
        k = partial_rope(rms_norm(k.reshape(B, T, N_ATTN_HEADS, HEAD_DIM), k_norm_g[l]), cos, sin)
        v = v.reshape(B, T, N_ATTN_HEADS, HEAD_DIM)
        qi = partial_rope(qi.reshape(B, T, IDX_HEADS, IDX_DIM), cos, sin)
        ki = partial_rope(layer_norm(ki, idx_k_ln_g[l], idx_k_ln_b[l])[:, :, None, :], cos, sin)[:, :, 0, :]
        attn = dsa_attention(q, k, v, qi, ki, wi).reshape(B, T, ATTN_WIDTH)
        conv = conformer_conv(cu, conv_dw[l], conv_b[l], conv_ln_g[l], conv_ln_b[l])
        mixed = jnp.concatenate([rms_norm(attn, out_g_attn[l]), rms_norm(conv, out_g_conv[l])], axis=-1)
        x = x + g1 * (mixed @ w_out[l])
        h2 = rms_norm(x) * (1.0 + sc2) + sh2
        x = x + g2 * peer_ffn(h2, peer_wq[l], peer_sub_keys[l], peer_u[l], peer_v[l])
    return x


_drawn_inputs = setup_inputs


def setup_inputs(seed=0):
    import zlib

    import numpy as np

    out = dict(_drawn_inputs(seed))
    spreads = {}
    factors = {'q_norm_g': 6.37,
     'k_norm_g': 6.756,
     'idx_k_ln_g': 2.854,
     'idx_k_ln_b': 3.391,
     'conv_b': 3.435,
     'conv_ln_g': 4.477,
     'conv_ln_b': 4.922,
     'out_g_attn': 5.047,
     'out_g_conv': 4.95}
    for name, (base, spread) in spreads.items():
        noise = np.random.default_rng([zlib.crc32(name.encode()), seed]).standard_normal(out[name].shape)
        drawn = base * np.exp(spread * noise) if base else spread * noise
        out[name] = __import__('jax').numpy.asarray(drawn.astype(out[name].dtype))
    for name, factor in factors.items():
        out[name] = (out[name] * factor).astype(out[name].dtype)
    return out
```

```python
from contextlib import ExitStack

import numpy as np

import concourse.bass as bass
from concourse import mybir

F32 = mybir.dt.float32
F32R = mybir.dt.float32r
I32 = mybir.dt.int32
U32 = mybir.dt.uint32
ALU = mybir.AluOpType
ACT = mybir.ActivationFunctionType
AX = mybir.AxisListType

P = 128
NORM_EPS = 1e-6
ROPE_THETA = 500000.0
PEER_TOPK = 16
NEG = -1.0e30
TAKEN = -3.0e38
RING = 7
WSLOTS = 3


class Chain:

    def __init__(self, eng, step_sem):
        self.eng, self.step_sem, self.count = eng, step_sem, {}
        self.i, self.per, self.start = None, {}, {}

    def __call__(self, ins, sem=None, wait=True):
        s = self.step_sem if sem is None else sem
        n = self.count.get(s, 0) + 1
        self.count[s] = n
        ins.then_inc(s, 1)
        if wait:
            self.eng.wait_ge(s, n if self.i is None else n + self.i * self.per[s])

    def enter(self, i, per):
        self.i, self.per, self.start = i, per, dict(self.count)

    def leave(self, iterations):
        for s, n in self.per.items():
            assert self.count.get(s, 0) - self.start.get(s, 0) == n
            self.count[s] = self.start.get(s, 0) + n * iterations
        self.i = None


def plan(depth):
    seq = []

    def block(*name):
        seq.append(("block", name))

    def job(*name):
        seq.append(("job", name))

    def ada(items):
        for layer, blk in items:
            block("ada", layer, blk)
            job("ada", layer, blk)

    for l in range(depth):
        more = l == 0 and depth > 1
        if l == 0:
            ada([(0, b) for b in range(4)])
        job("wT", l)
        for t in range(2):
            for q in range(2):
                job("hT", l, t, q)
        for name in ("qi", "ki"):
            block(name, l)
            for t in range(2):
                job(name, l, t)
        block("cu0", l)
        job("cv", l, 0)
        job("cv", l, 1)
        job("iT", l, 0)
        job("iT", l, 1)
        job("kiT", l)
        block("cu1", l)
        job("cv", l, 2)
        job("cv", l, 3)
        for n in range(6):
            job("dot", l, n)
        for name in ("q", "k", "v"):
            block(name, l)
            for t in range(2):
                job(name, l, t)
        for t in range(2):
            for name in ("qT", "kT"):
                job(name, l, t)
        for t in range(2):
            job("cT", l, t)
        job("S", l, 0)
        for n in range(6):
            if n < 5:
                job("S", l, n + 1)
            if l == 0:
                ada([(0, 4 + n)])
            job("PT", l, n)
        for t in range(2):
            for q in range(2):
                job("mT", l, t, q)
        for b in range(2):
            block("out", l, b)
            for t in range(2):
                job("out", l, b, t)
        block("sk", l)
        for n in range(4):
            job("skT", l, n)
        for t in range(2):
            for q in range(2):
                job("h2T", l, t, q)
        mid = ADA_MID if l == 0 else [[], [], [], []]
        for b in range(4):
            block("wq", l, b)
            job("qp", l, b, 0)
            job("qp", l, b, 1)
            ada(mid[b] if more or l else [])
            if b:
                job("s", l, b - 1, 0)
                job("s", l, b - 1, 1)
        job("s", l, 3, 0)
        job("s", l, 3, 1)
        if more:
            ada(ADA_TAIL)
        job("eT", l, 0)
        job("eT", l, 1)
    return seq


ADA_MID = [[(0, 10)], [(0, 11), (1, 0)], [(1, 1), (1, 2)], [(1, 3)]]
ADA_TAIL = [(1, b) for b in range(4, 12)]


def trunk(nc, x, c, positions, w_ada, b_ada, w_in, q_norm_g, k_norm_g, idx_k_ln_g, idx_k_ln_b,
          conv_dw, conv_b, conv_ln_g, conv_ln_b, out_g_attn, out_g_conv, w_out, peer_wq,
          peer_sub_keys, peer_u, peer_v, out):
    _, T, D = x.shape
    L = w_ada.shape[0]
    DH = q_norm_g.shape[1]
    TAPS, CW = conv_dw.shape[1:]
    AW = out_g_attn.shape[1]
    NH = AW // DH
    NI = NH
    ROT = DH // 4
    HALF = ROT // 2
    KT = D // P
    CT = CW // P
    HP = peer_sub_keys.shape[1]
    NK = peer_sub_keys.shape[3]
    SEL = min(256, T // 4)
    CU0 = 3 * AW + NI * DH + DH + NI
    assert (T, D, NH, DH, CW, NK, HP) == (256, 1024, 8, 64, 512, 128, 8) and L == 2

    seq = plan(L)
    blocks = [n for kind, n in seq if kind == "block"]
    jobs = [n for kind, n in seq if kind == "job"]
    job_at = {n: i for i, n in enumerate(jobs)}
    block_at = {n: i for i, n in enumerate(blocks)}
    last_job, cur = {}, None
    for kind, n in seq:
        if kind == "block":
            cur = n
        elif cur is not None and (n[0] == cur[0] or (cur[0][:2] == "cu" and n[0] == "cv")
                                  or (cur[0], n[0]) in (("sk", "skT"), ("wq", "qp"))):
            last_job[cur] = n

    scratch = nc.dram_tensor("mod_rows", [L, 6 * D], F32, kind="Internal").ap()

    with ExitStack() as ctx:
        def sb(name, shape, dt=F32):
            return ctx.enter_context(nc.sbuf_tensor(name, shape, dt))

        def sem(name):
            return ctx.enter_context(nc.semaphore(name))

        xs = sb("xs", [P, 2, D])
        h2hi = sb("h2hi", [P, KT, T], F32R)
        h2lo = sb("h2lo", [P, KT, T], F32R)
        u_raw = sb("u_raw", [P, 2, D])
        v_raw = sb("v_raw", [P, 2, D])
        uT_hi = sb("uT_hi", [P, KT, P], F32R)
        uT_lo = sb("uT_lo", [P, KT, P], F32R)
        v_hi = sb("v_hi", [P, 2, D], F32R)
        v_lo = sb("v_lo", [P, 2, D], F32R)
        c_hi = sb("c_hi", [P, 2, T], F32R)
        c_lo = sb("c_lo", [P, 2, T], F32R)
        gel = sb("gel", [P, 2, T])
        ident = sb("ident", [P, P])
        iota = sb("iota", [P, P])
        tri = sb("tri", [P, P])
        selT = sb("selT", [P, 3, T])
        bias = sb("bias", [P, 2, T])
        cwT = sb("cwT", [P, CT, TAPS + 1])
        gain_small = sb("gain_small", [P, 4, DH])
        rope = sb("rope", [P, 2, 2, HALF])
        ropek = sb("ropek", [P, 2, 2, HALF])
        invf = sb("invf", [P, HALF])
        posi = sb("posi", [P, 2], I32)
        posf = sb("posf", [P, 2])
        ccol = sb("ccol", [P, KT])
        cact = sb("cact", [P, KT])
        wis = sb("wis", [P, 2, NI])
        rs = sb("rs", [P, 32])
        neghalf = sb("neghalf", [P, 32])
        bn6 = sb("bn6", [P, 2, 6])
        mv = sb("mv", [P, 2, 2])
        m8 = sb("m8", [P, 8])
        negm = sb("negm", [P, 2, 4])
        rsum = sb("rsum", [P, 2, NH])
        rinv = sb("rinv", [P, 2, NH])
        gmx = sb("gmx", [P, 2, 4])

        arena = sb("arena", [P, P * T])
        gates = arena[:, :].rearrange("p (i t) -> p i t", t=T)
        top = [0]

        def cut(n, at=None):
            a = top[0] if at is None else at
            if at is None:
                top[0] = a + n
            assert a + n <= P * T
            return arena[:, a:a + n]

        wring = cut(WSLOTS * 8 * 512).rearrange("p (s n) -> p s n", s=WSLOTS)
        MODA = top[0]
        moda = cut(2 * D).rearrange("p (a n) -> p a n", a=2)
        ln_gb = moda[:, 0, :].rearrange("p (a n) -> p a n", a=2)
        out_g = moda[:, 1, :]
        eq = cut(2 * D, MODA)
        GM0 = top[0]
        gmod = cut(D)
        HT0 = top[0]
        hT = cut(KT * T).rearrange("p (k t) -> p k t", k=KT)
        HB0 = top[0]
        hb = cut(2 * D).rearrange("p (a n) -> p a n", a=2)
        cand = cut(2 * D, HB0)
        P0 = top[0]
        PW = 34 * DH
        pj = cut(2 * PW).rearrange("p (a n) -> p a n", a=2)
        pjh = pj.rearrange("p a (h d) -> p a h d", d=DH)
        sc = cut(2 * 16 * NK, P0).rearrange("p (a g n) -> p a g n", a=2, g=16)
        QK0 = top[0]
        qT = cut(4 * T).rearrange("p (j t) -> p j t", j=4)
        kT = cut(4 * T).rearrange("p (j t) -> p j t", j=4)
        qiT = cut(4 * T).rearrange("p (j t) -> p j t", j=4)
        kiT = cut(T)
        skT = cut(16 * NK, QK0).rearrange("p (g n) -> p g n", g=16)
        CV0 = top[0]
        HCW = TAPS - 1 + T
        hc = cut(CT * HCW).rearrange("p (j t) -> p j t", j=CT)
        acc = cut(CT * T).rearrange("p (j t) -> p j t", j=CT)
        modb = cut(2 * D, CV0).rearrange("p (a n) -> p a n", a=2)
        AT0 = top[0]
        lg = cut(2 * 512).rearrange("p (b n) -> p b n", b=2)
        ex = cut(2 * 512).rearrange("p (b n) -> p b n", b=2)
        pt = cut(2 * 512).rearrange("p (b n) -> p b n", b=2)
        cw_raw = cut(CW, AT0)
        relu = lg
        score = ex[:, 0, 0:T]
        work = ex[:, 1, 0:T]
        rt = pt[:, 0, :].rearrange("p (b n) -> p b n", b=2)
        sig = pt[:, 1, :].rearrange("p (b n) -> p b n", b=2)
        qpT = cut(16 * T, CV0).rearrange("p (g t) -> p g t", g=16)
        TK0 = CV0 + 16 * T
        v1 = cut(256, TK0).rearrange("p (a g k) -> p a g k", a=2, g=8)
        i1u = cut(256, TK0 + 256).bitcast(U32).rearrange("p (g k) -> p g k", k=16)
        work1 = cut(256, TK0 + 512)
        i1f = cut(512, GM0).rearrange("p (a r h k) -> p a r h k", a=2, r=2, h=HP)
        topv = cut(256, TK0 + 768).rearrange("p (a h k) -> p a h k", a=2, h=HP)
        posu = cut(256, TK0 + 1024).bitcast(U32).rearrange("p (a h k) -> p a h k", a=2, h=HP)
        seln = cut(384, GM0 + 512).rearrange("p (r h k) -> p r h k", r=3, h=HP)
        pab = cut(256, TK0 + 1280)
        assert TK0 + 1536 <= P * T

        ps = ctx.enter_context(nc.psum_tensor("ps", [P, 8, 512], F32))

        full = [sem(f"bank{b}_full") for b in range(RING)]
        free = [sem(f"bank{b}_free") for b in range(RING)]
        w_in_slot = [sem(f"weights_landed{s}") for s in range(WSLOTS)]
        x_landed = sem("x_landed")
        c_landed = sem("c_landed")
        pos_landed = sem("pos_landed")
        small_landed = sem("small_landed")
        consts_made = sem("consts_made")
        pool_step = sem("pool_step")
        dve_step = sem("dve_step")
        act_step = sem("act_step")
        cact_made = sem("cact_made")
        mod_stored = [sem(f"mod_stored{i}") for i in range(2)]
        mod1_landed = sem("mod1_landed")
        out_gains_landed = sem("out_gains_landed")
        gate_landed = sem("gate_landed")
        mod2_landed = sem("mod2_landed")
        rsqrt_asked = sem("rsqrt_asked")
        rsqrt_done = sem("rsqrt_done")
        rope_ready = sem("rope_ready")
        rope_args = sem("rope_args")
        cw_ready = sem("cw_ready")
        h_ready = sem("h_ready")
        hT_ready = sem("hT_ready")
        proj_ready = sem("proj_ready")
        idx_ready = sem("idx_ready")
        idxT_ready = sem("idxT_ready")
        sig_ready = sem("sig_ready")
        glu_done = sem("glu_done")
        exp_part = sem("exp_part")
        act_hi = sem("act_hi")
        h2lo_done = sem("h2lo_done")
        relu_ready = sem("relu_ready")
        relu_used = sem("relu_used")
        conv_ready = sem("conv_ready")
        qk_ready = sem("qk_ready")
        qkT_ready = sem("qkT_ready")
        logits_ready = sem("logits_ready")
        exp_ready = sem("exp_ready")
        ptT_ready = sem("ptT_ready")
        pv_full = sem("pv_full")
        pv_free = sem("pv_free")
        silu_in = sem("silu_in")
        silu_done = sem("silu_done")
        mixed_ready = sem("mixed_ready")
        mixedT_ready = sem("mixedT_ready")
        xmid_ready = sem("xmid_ready")
        skT_ready = sem("skT_ready")
        h2_ready = sem("h2_ready")
        h2T_ready = sem("h2T_ready")
        qpT_ready = sem("qpT_ready")
        s_ready = sem("s_ready")
        gexp_in = sem("gexp_in")
        gexp_done = sem("gexp_done")
        sel_ready = sem("sel_ready")
        selT_ready = sem("selT_ready")
        b_onehot = sem("b_onehot")
        a_onehot = sem("a_onehot")
        a_gated = sem("a_gated")
        gate_mm = sem("gate_mm")
        gate_stored = sem("gate_stored")
        u_landed = [sem(f"u_landed{s}") for s in range(2)]
        v_landed = [sem(f"v_landed{s}") for s in range(2)]
        uT_turned = sem("uT_turned")
        uThi_done = sem("uThi_done")
        uTlo_done = sem("uTlo_done")
        vhi_done = sem("vhi_done")
        vlo_done = sem("vlo_done")
        act_mm = sem("act_mm")
        gelu_done = sem("gelu_done")
        c_done = sem("c_done")
        y_mm = sem("y_mm")
        x_done = sem("x_done")
        out_stored = sem("out_stored")

        def bank(name):
            n = job_at[name]
            return n % RING, n // RING + 1

        def wait_full(eng, name):
            b, n = bank(name)
            eng.wait_ge(full[b], n)
            return ps[:, b, :]

        mod_order = [(n[1], n[2]) for n in blocks if n[0] == "ada"]
        NSTEP = NK

        def expert_steps(eng, chain, per, step):
            step(0, 0)
            step(1, 1)
            with eng.Fori(0, (NSTEP - 4) // 4) as i:
                if chain is not None:
                    chain.enter(i, per)
                for u in range(4):
                    step(i * 4 + (2 + u), 2 + u)
                if chain is not None:
                    chain.leave((NSTEP - 4) // 4)
            step(NSTEP - 2, NSTEP - 2)
            step(NSTEP - 1, NSTEP - 1)

        def brow(n):
            s = n % WSLOTS
            return v_raw[0:1, s // 2, (s % 2) * 512:(s % 2) * 512 + 512]

        def stage(m):
            return v_raw[0:1, 1, 512:1024] if m % 2 else gel[0:1, :, :].rearrange("p a n -> p (a n)")

        def loads(l, j, k):
            if isinstance(j, int):
                return 16 * ((l * NSTEP + j) // 2 + 1)
            return (j - k % 2) * 8 + 16 * (l * NSTEP // 2 + 1)

        block_ctx = ctx.enter_context(nc.Block())

        @block_ctx.sync
        def _(sp):
            sp.dma_start(ccol[:, :], c[0, :].rearrange("(p k) -> p k", k=KT)).then_inc(c_landed, 16)
            sp.dma_start(xs[:, :, :], x[0].rearrange("(a p) d -> p a d", p=P)).then_inc(x_landed, 16)

            def load_block(n):
                name = blocks[n]
                slot = n % WSLOTS
                if n >= WSLOTS:
                    b, k = bank(last_job[blocks[n - WSLOTS]])
                    sp.wait_ge(full[b], k)
                w = wring[:, slot, :].rearrange("p (k n) -> p k n", k=KT)
                l = name[1]
                got = w_in_slot[slot]
                win = w_in[l].rearrange("(k p) n -> p k n", p=P)
                if name[0] == "ada":
                    src = w_ada[l].rearrange("(p k) n -> p k n", k=KT)[:, :, name[2] * 512:name[2] * 512 + 512]
                    sp.dma_start(w, src).then_inc(got, 16)
                    sp.dma_start(brow(n), b_ada[l:l + 1, name[2] * 512:name[2] * 512 + 512]).then_inc(got, 16)
                    return
                if name[0] in ("q", "k", "v", "qi"):
                    a = {"q": 0, "k": 1, "v": 2, "qi": 3}[name[0]] * AW
                    pieces = [(w, win[:, :, a:a + 512])]
                elif name[0] == "ki":
                    pieces = [(w[:, :, 0:DH + NI], win[:, :, 4 * AW:CU0])]
                elif name[0] in ("cu0", "cu1"):
                    a = CU0 + 256 * int(name[0][2])
                    pieces = [(w[:, :, 0:256], win[:, :, a:a + 256]),
                              (w[:, :, 256:512], win[:, :, a + CW:a + CW + 256])]
                elif name[0] == "out":
                    pieces = [(w, w_out[l].rearrange("(k p) n -> p k n", p=P)[:, :, name[2] * 512:name[2] * 512 + 512])]
                elif name[0] == "wq":
                    pieces = [(w, peer_wq[l].rearrange("(k p) n -> p k n", p=P)[:, :, name[2] * 512:name[2] * 512 + 512])]
                else:
                    pieces = [(wring[:, slot, 0:16 * NK].rearrange("p (g n) -> p g n", g=16),
                               peer_sub_keys[l].rearrange("h s n k -> n (h s) k"))]
                for dst, src in pieces:
                    sp.dma_start(dst, src).then_inc(got, 16)

            n = 0
            for l in range(L):
                while n < len(blocks) and (blocks[n][1] == l or blocks[n][0] == "ada"):
                    if l and n == block_at[("qi", l)]:
                        sp.wait_ge(c_done, l * NSTEP)
                    load_block(n)
                    n += 1
                sp.wait_ge(gate_mm, (l + 1) * 32)

                def load_experts(j, k):
                    jj = j + l * NSTEP
                    if k >= 2:
                        sp.wait_ge(uT_turned, jj * 2 - 2)
                    sp.dma_start(u_raw[:, k % 2, :],
                                 peer_u[l, bass.ds(j * P, P), :]).then_inc(u_landed[k % 2], 16)
                    if k >= 2:
                        sp.wait_ge(vlo_done, jj - 1)
                    sp.dma_start(v_raw[:, k % 2, :],
                                 peer_v[l, bass.ds(j * P, P), :]).then_inc(v_landed[k % 2], 16)

                expert_steps(sp, None, None, load_experts)
            sp.wait_ge(x_done, 2 * L)
            sp.dma_start(out[0].rearrange("(a p) d -> p a d", p=P), xs[:, :, :]).then_inc(out_stored, 16)
            sp.wait_ge(out_stored, 16)

        @block_ctx.gpsimd
        def _(pool):
            seq_ = Chain(pool, pool_step)
            seq_(pool.memset(ident[:, :], 0.0))
            seq_(pool.affine_select(out=ident[:, :], in_=ident[:, :], compare_op=ALU.not_equal, fill=1.0,
                                    base=0, pattern=[[-1, P]], channel_multiplier=1))
            seq_(pool.iota(iota[:, :], [[1, P]], base=0, channel_multiplier=0,
                           allow_small_or_imprecise_dtypes=True))
            seq_(pool.memset(tri[:, :], 0.0))
            seq_(pool.affine_select(out=tri[:, :], in_=tri[:, :], compare_op=ALU.is_ge, fill=NEG,
                                    base=0, pattern=[[-1, P]], channel_multiplier=1))
            seq_(pool.memset(neghalf[:, :], -0.5))
            inv_freq = np.power(np.float32(ROPE_THETA), -np.arange(0, ROT, 2, dtype=np.float32) / ROT)
            for i, f in enumerate(inv_freq):
                seq_(pool.memset(invf[:, i:i + 1], float(f)))
            seq_(pool.memset(hc[:, :, 0:TAPS - 1], 0.0))
            pool.nop().then_inc(consts_made, 1) if False else seq_(pool.memset(rs[:, :], 1.0), consts_made)
            pool.dma_start(posi[:, :], positions[0, :].rearrange("(a p) -> p a", p=P),
                           allow_slow_non_contiguous=True).then_inc(pos_landed, 16)

            asked = 0

            def rsqrt(width):
                nonlocal asked
                asked += 1
                pool.wait_ge(rsqrt_asked, asked)
                pool.tensor_tensor(rs[:, 0:width], rs[:, 0:width], neghalf[:, 0:width],
                                   ALU.pow).then_inc(rsqrt_done, 1)

            def mod_rows(l, first, last):
                m = mod_order.index((l, last))
                for i in range(2):
                    pool.wait_ge(mod_stored[i], 16 * ((m - i) // 2 + 1))

            def spread(dst, src, landed):
                pool.dma_start(dst, src).then_inc(landed, 16)

            for l in range(L):
                if l:
                    pool.wait_ge(c_done, l * NSTEP)
                    seq_(pool.memset(hc[:, :, 0:TAPS - 1], 0.0), consts_made)
                for i, g in enumerate((q_norm_g, k_norm_g, idx_k_ln_g, idx_k_ln_b)):
                    spread(gain_small[:, i, :], g[l, :].partition_broadcast(P), small_landed)
                spread(cw_raw[0:TAPS, :], conv_dw[l], small_landed)
                spread(cw_raw[TAPS:TAPS + 1, :], conv_b[l:l + 1, :], small_landed)
                mod_rows(l, 0, 3)
                if l:
                    pool.wait_ge(x_done, 2 * l)
                for i in range(2):
                    spread(moda[:, i, :], scratch[l, i * D:(i + 1) * D].partition_broadcast(P), mod1_landed)
                rsqrt(2)
                pool.wait_ge(h_ready, 2 * (l + 1))
                spread(ln_gb[:, 0, :], conv_ln_g[l, :].partition_broadcast(P), out_gains_landed)
                spread(ln_gb[:, 1, :], conv_ln_b[l, :].partition_broadcast(P), out_gains_landed)
                spread(out_g[:, 0:AW], out_g_attn[l, :].partition_broadcast(P), out_gains_landed)
                spread(out_g[:, AW:D], out_g_conv[l, :].partition_broadcast(P), out_gains_landed)
                rsqrt(2)
                rsqrt(32)
                rsqrt(2)
                rsqrt(2)
                mod_rows(l, 4, 5)
                spread(gmod, scratch[l, 2 * D:3 * D].partition_broadcast(P), gate_landed)
                for t in range(2):
                    wait_full(pool, ("cT", l, t))
                mod_rows(l, 6, 9)
                for i in range(2):
                    spread(modb[:, i, :], scratch[l, (3 + i) * D:(4 + i) * D].partition_broadcast(P), mod2_landed)
                rsqrt(2)
                rsqrt(2)

                def gate_batch(n, k):
                    nn = n + l * 32
                    pool.wait_ge(a_onehot, nn + 1)
                    hot = v_raw[:, k % 2, :].rearrange("p (t i) -> p t i", t=8)
                    g = selT[:, 2, bass.ds(n * 8, 8)].unsqueeze(2).to_broadcast([P, 8, P])
                    pool.tensor_tensor(hot, hot, g, ALU.mult).then_inc(a_gated, 1)

                with pool.Fori(0, 8) as i:
                    for u in range(4):
                        gate_batch(i * 4 + u, u)
                mod_rows(l, 10, 11)
                pool.wait_ge(c_done, (l + 1) * NSTEP)
                spread(gmod, scratch[l, 5 * D:6 * D].partition_broadcast(P), gate_landed)

        @block_ctx.tensor
        def _(pe):
            done = [0]
            state = {"block": -1}

            def next_is(kind, name):
                assert seq[done[0]] == (kind, name), (seq[done[0]], name)
                done[0] += 1

            landed_count = [0] * WSLOTS

            def use_block(*name):
                next_is("block", name)
                n = block_at[name]
                slot = n % WSLOTS
                landed_count[slot] += 2 if name[0] in ("ada", "cu0", "cu1") else 1
                pe.wait_ge(w_in_slot[slot], 16 * landed_count[slot])
                state["block"] = n
                return wring[:, slot, :].rearrange("p (k n) -> p k n", k=KT)

            def open_job(*name):
                next_is("job", name)
                b, n = bank(name)
                if n > 1:
                    pe.wait_ge(free[b], n - 1)
                return b, ps[:, b, :]

            def mm_all(o, pairs):
                for i, (a, b) in enumerate(pairs):
                    ins = pe.matmul(o, a, b, start=i == 0, stop=i == len(pairs) - 1)
                return ins

            def ada(layer, blk):
                w = use_block("ada", layer, blk)
                b, o = open_job("ada", layer, blk)
                pairs = [(cact[:, k:k + 1], w[:, k, :]) for k in range(KT)]
                pairs.append((ident[0:1, 0:1], brow(state["block"])))
                mm_all(o[0:1, :], pairs).then_inc(full[b], 1)

            def turn4(name, srcs, width=P):
                b, o = open_job(*name)
                for i, s in enumerate(srcs):
                    n = s.shape[0]
                    ins = pe.transpose(o[:, i * n:(i + 1) * n], s, ident[0:n, 0:n])
                ins.then_inc(full[b], 1)

            def proj(w, name, lhs, width):
                b, o = open_job(*name)
                mm_all(o[:, 0:width], [(lhs[:, k, :], w[:, k, 0:width]) for k in range(KT)]).then_inc(full[b], 1)

            pe.wait_ge(consts_made, 1)
            pe.wait_ge(cact_made, 1)
            for blk in range(4):
                ada(0, blk)
            for l in range(L):
                if l:
                    pe.wait_ge(x_done, 2 * l)
                pe.wait_ge(small_landed, 16 * 6 * (l + 1))
                turn4(("wT", l), [cw_raw[0:TAPS + 1, j * P:(j + 1) * P] for j in range(CT)])
                for t in range(2):
                    pe.wait_ge(h_ready, 2 * l + t + 1)
                    for q in range(2):
                        turn4(("hT", l, t, q), [hb[:, t, (4 * q + i) * P:(4 * q + i + 1) * P] for i in range(4)])
                for t in range(4):
                    pass
                pe.wait_ge(hT_ready, 4 * (l + 1))
                for name, width in (("qi", 512), ("ki", DH + NI)):
                    w = use_block(name, l)
                    for t in range(2):
                        proj(w, (name, l, t), hT[:, :, t * P:(t + 1) * P], width)

                def conv_proj(w, ct):
                    b, o = open_job("cv", l, ct)
                    for s in range(2):
                        col = s * 256 + (ct % 2) * P
                        ins = mm_all(o[:, s * T:(s + 1) * T],
                                     [(w[:, k, col:col + P], hT[:, k, :]) for k in range(KT)])
                    ins.then_inc(full[b], 1)

                w = use_block("cu0", l)
                conv_proj(w, 0)
                conv_proj(w, 1)
                for t in range(2):
                    pe.wait_ge(idx_ready, 2 * l + t + 1)
                    turn4(("iT", l, t), [pj[:, t, (12 + i) * P:(13 + i) * P] for i in range(4)])
                turn4(("kiT", l), [pj[:, t, 16 * P:17 * P] for t in range(2)])
                w = use_block("cu1", l)
                conv_proj(w, 2)
                conv_proj(w, 3)
                pe.wait_ge(idxT_ready, 3 * (l + 1))
                for n in range(6):
                    t, heads, nk = DOTS[n]
                    b, o = open_job("dot", l, n)
                    for i, h in enumerate(heads):
                        r = (h % 2) * DH
                        ins = pe.matmul(o[:, i * nk:(i + 1) * nk], qiT[r:r + DH, h // 2, t * P:(t + 1) * P],
                                        kiT[r:r + DH, 0:nk], start=True, stop=True)
                    ins.then_inc(full[b], 1)
                for name in ("q", "k", "v"):
                    w = use_block(name, l)
                    for t in range(2):
                        proj(w, (name, l, t), hT[:, :, t * P:(t + 1) * P], 512)
                for t in range(2):
                    pe.wait_ge(qk_ready, 2 * l + t + 1)
                    turn4(("qT", l, t), [pj[:, t, i * P:(i + 1) * P] for i in range(4)])
                    turn4(("kT", l, t), [pj[:, t, (4 + i) * P:(5 + i) * P] for i in range(4)])
                pe.wait_ge(conv_ready, CT * (l + 1))
                for t in range(2):
                    turn4(("cT", l, t), [acc[:, j, t * P:(t + 1) * P] for j in range(CT)])

                pe.wait_ge(qkT_ready, 4 * (l + 1))

                def logits(n):
                    t, heads, nk = DOTS[n]
                    b, o = open_job("S", l, n)
                    for i, h in enumerate(heads):
                        r = (h % 2) * DH
                        ins = pe.matmul(o[:, i * nk:(i + 1) * nk], qT[r:r + DH, h // 2, t * P:(t + 1) * P],
                                        kT[r:r + DH, h // 2, 0:nk], start=True, stop=True)
                    ins.then_inc(full[b], 1)

                def values(n):
                    t, heads, nk = DOTS[n]
                    pe.wait_ge(ptT_ready, 6 * l + n + 1)
                    if heads[0] == 0 and (l or t):
                        pe.wait_ge(pv_free, 2 * l + t)
                    for i, h in enumerate(heads):
                        for kb in range(nk // P):
                            ins = pe.matmul(ps[:, 7, h * DH:(h + 1) * DH],
                                            pt[:, n % 2, (i * (nk // P) + kb) * P:(i * (nk // P) + kb + 1) * P],
                                            pjh[:, kb, 16 + h, :], start=kb == 0, stop=kb == nk // P - 1)
                    ins.then_inc(pv_full, 1)

                logits(0)
                for n in range(6):
                    if n < 5:
                        logits(n + 1)
                    if n:
                        values(n - 1)
                    if l == 0:
                        ada(0, 4 + n)
                    pe.wait_ge(exp_ready, 6 * l + n + 1)
                    turn4(("PT", l, n), [ex[:, n % 2, i * P:(i + 1) * P] for i in range(4)])
                values(5)

                for t in range(2):
                    pe.wait_ge(mixed_ready, 2 * l + t + 1)
                    for q in range(2):
                        turn4(("mT", l, t, q), [hb[:, t, (4 * q + i) * P:(4 * q + i + 1) * P] for i in range(4)])
                pe.wait_ge(mixedT_ready, 4 * (l + 1))
                for blk in range(2):
                    w = use_block("out", l, blk)
                    for t in range(2):
                        proj(w, ("out", l, blk, t), hT[:, :, t * P:(t + 1) * P], 512)
                use_block("sk", l)
                raw = wring[:, block_at[("sk", l)] % WSLOTS, 0:16 * NK].rearrange("p (g n) -> p g n", g=16)
                for n in range(4):
                    turn4(("skT", l, n), [raw[:, 4 * n + i, :] for i in range(4)])
                for t in range(2):
                    pe.wait_ge(h2_ready, 2 * l + t + 1)
                    for q in range(2):
                        turn4(("h2T", l, t, q), [hb[:, t, (4 * q + i) * P:(4 * q + i + 1) * P] for i in range(4)])
                pe.wait_ge(h2T_ready, 4 * (l + 1))
                pe.wait_ge(skT_ready, 4 * (l + 1))

                def subkeys(blk):
                    pe.wait_ge(qpT_ready, 2 * (4 * l + blk + 1))
                    for t in range(2):
                        b, o = open_job("s", l, blk, t)
                        for i in range(4):
                            g = 4 * blk + i
                            ins = pe.matmul(o[:, i * NK:(i + 1) * NK], qpT[:, g, t * P:(t + 1) * P], skT[:, g, :],
                                            start=True, stop=True)
                        ins.then_inc(full[b], 1)

                for blk in range(4):
                    w = use_block("wq", l, blk)
                    for s in range(2):
                        b, o = open_job("qp", l, blk, s)
                        for i in range(2):
                            col = (2 * s + i) * P
                            ins = mm_all(o[:, i * T:(i + 1) * T],
                                         [(w[:, k, col:col + P], hT[:, k, :]) for k in range(KT)])
                        ins.then_inc(full[b], 1)
                    if l == 0:
                        for a in ADA_MID[blk]:
                            ada(*a)
                    if blk:
                        subkeys(blk - 1)
                subkeys(3)
                if l == 0:
                    for a in ADA_TAIL:
                        ada(*a)
                for t in range(2):
                    pe.wait_ge(sel_ready, 2 * l + t + 1)
                    b, o = open_job("eT", l, t)
                    for i in range(3):
                        ins = pe.transpose(o[:, i * P:(i + 1) * P], seln[:, i, :, :].rearrange("p h k -> p (h k)"),
                                           ident[:, :])
                    ins.then_inc(full[b], 1)

                last_jobs = jobs[:job_at[("eT", l, 1)] + 1][-RING:]
                for name in last_jobs:
                    b, n = bank(name)
                    pe.wait_ge(free[b], n)

                def gate_batch(n, k):
                    nn = n + l * 32
                    pe.wait_ge(b_onehot, nn + 1)
                    pe.wait_ge(a_gated, nn + 1)
                    if l or k >= 2 or not isinstance(n, int):
                        pass
                    pe.wait_ge(gate_stored, nn + 1)
                    hotb = u_raw[:, k % 2, :].rearrange("p (t i) -> p t i", t=8)
                    hota = v_raw[:, k % 2, :].rearrange("p (t i) -> p t i", t=8)
                    for t in range(8):
                        ins = pe.matmul(ps[:, 2 * (k % 2) + t // 4, (t % 4) * P:(t % 4 + 1) * P],
                                        hotb[:, t, :], hota[:, t, :], start=True, stop=True)
                    ins.then_inc(gate_mm, 1)

                with pe.Fori(0, 8) as i:
                    for u in range(4):
                        gate_batch(i * 4 + u, u)

                def turn(j, k):
                    pe.wait_ge(u_landed[k % 2], loads(l, j, k))
                    for q in range(2):
                        for i in range(4):
                            d = 4 * q + i
                            ins = pe.transpose(ps[:, q, i * P:(i + 1) * P], u_raw[:, k % 2, d * P:(d + 1) * P],
                                               ident[:, :])
                        ins.then_inc(uT_turned, 1)

                def activations(j, k):
                    jj = j + l * NSTEP
                    pe.wait_ge(uThi_done, jj * 2 + 2)
                    pe.wait_ge(uTlo_done, jj * 2 + 2)
                    o = ps[:, 2 + k % 2, 0:T]
                    for d in range(KT):
                        pe.matmul(o, uT_hi[:, d, :], h2hi[:, d, :], start=d == 0, stop=False)
                        pe.matmul(o, uT_hi[:, d, :], h2lo[:, d, :], start=False, stop=False)
                        ins = pe.matmul(o, uT_lo[:, d, :], h2hi[:, d, :], start=False, stop=d == KT - 1)
                    ins.then_inc(act_mm, 1)

                def outputs(j, k):
                    jj = j + l * NSTEP
                    pe.wait_ge(c_done, jj + 1)
                    pe.wait_ge(vlo_done, jj + 1)
                    s = k % 2
                    for t in range(2):
                        for q in range(2):
                            o = ps[:, 4 + 2 * t + q, :]
                            ts, qs = slice(t * P, (t + 1) * P), slice(q * 512, (q + 1) * 512)
                            pe.matmul(o, c_hi[:, s, ts], v_hi[:, s, qs], start=k == 0, stop=False)
                            pe.matmul(o, c_hi[:, s, ts], v_lo[:, s, qs], start=False, stop=False)
                            ins = pe.matmul(o, c_lo[:, s, ts], v_hi[:, s, qs], start=False, stop=k == NSTEP - 1)
                    ins.then_inc(y_mm, 1)

                pe.wait_ge(h2lo_done, 4 * (l + 1))
                pe.wait_ge(gate_stored, 32 * (l + 1) + 2)
                turn(0, 0)

                def step(j, k):
                    activations(j, k)
                    if k < NSTEP - 1:
                        turn(j + 1, k + 1)
                    if k > 0:
                        outputs(j - 1, k - 1)

                expert_steps(pe, None, None, step)
                outputs(NSTEP - 1, NSTEP - 1)
            assert done[0] == len(seq)

        @block_ctx.scalar
        def _(act):
            seq_ = Chain(act, act_step)

            def take(name, fn, signal=None, wait=False):
                o = wait_full(act, name)
                b, _ = bank(name)
                ins = fn(o)
                ins.then_inc(free[b], 1)

            n_mod = [0]

            def ada(layer, blk):
                m = n_mod[0]
                n_mod[0] += 1
                name = ("ada", layer, blk)
                o = wait_full(act, name)
                b, n = bank(name)
                if m >= 2:
                    act.wait_ge(mod_stored[m % 2], 16 * (m // 2))
                act.copy(stage(m), o[0:1, :]).then_inc(free[b], 1)
                act.wait_ge(free[b], n)
                act.dma_start(scratch[layer:layer + 1, blk * 512:blk * 512 + 512], stage(m)).then_inc(mod_stored[m % 2], 16)

            act.wait_ge(c_landed, 16)
            act.activation(cact[:, :], ccol[:, :], ACT.Silu).then_inc(cact_made, 1)
            act.wait_ge(rope_args, 1)
            flat = rope[:, :, :, :].rearrange("p s a f -> p (s a f)")
            act.activation(flat, flat, ACT.Sin).then_inc(rope_ready, 1)
            for blk in range(4):
                ada(0, blk)

            for l in range(L):
                def evac(name, dst, sem_done, scale=None, src=None):
                    o = wait_full(act, name)
                    b, n = bank(name)
                    s = o if src is None else src(o)
                    ins = act.copy(dst, s) if scale is None else act.mul(dst, s, scale)
                    ins.then_inc(free[b], 1)
                    act.wait_ge(free[b], n)
                    act.sem_inc(sem_done, 1)

                def four(o):
                    return o.rearrange("p (k t) -> p k t", k=4)

                evac(("wT", l), cwT[:, :, :].rearrange("p j t -> p (j t)"), cw_ready,
                     src=lambda o: o[:, 0:CT * (TAPS + 1)])
                for t in range(2):
                    for q in range(2):
                        evac(("hT", l, t, q), hT[:, 4 * q:4 * q + 4, t * P:(t + 1) * P], hT_ready, src=four)
                for t in range(2):
                    evac(("qi", l, t), pj[:, t, 3 * AW:4 * AW], proj_ready)
                for t in range(2):
                    o = wait_full(act, ("ki", l, t))
                    b, n = bank(("ki", l, t))
                    seq_(act.mul(wis[:, t, :], o[:, DH:DH + NI], float(NI) ** -0.5), wait=False)
                    evac(("ki", l, t), pjh[:, t, 32, :], proj_ready, src=lambda o: o[:, 0:DH])

                def sigmoid(ct):
                    o = wait_full(act, ("cv", l, ct))
                    if CT * l + ct >= 2:
                        act.wait_ge(glu_done, CT * l + ct - 1)
                    act.activation(sig[:, ct % 2, :], o[:, T:2 * T], ACT.Sigmoid).then_inc(sig_ready, 1)

                sigmoid(0)
                sigmoid(1)
                for t in range(2):
                    evac(("iT", l, t), qiT[:, :, t * P:(t + 1) * P], idxT_ready, src=four)
                evac(("kiT", l), kiT, idxT_ready, src=lambda o: o[:, 0:T])
                sigmoid(2)
                sigmoid(3)
                for n in range(6):
                    name = ("dot", l, n)
                    o = wait_full(act, name)
                    b, k = bank(name)
                    if n >= 2:
                        act.wait_ge(relu_used, 6 * l + n - 1)
                    act.activation(relu[:, n % 2, :], o, ACT.Relu, scale=float(DH) ** -0.5).then_inc(free[b], 1)
                    act.wait_ge(free[b], k)
                    act.sem_inc(relu_ready, 1)
                for i, name in enumerate(("q", "k", "v")):
                    for t in range(2):
                        evac((name, l, t), pj[:, t, i * AW:(i + 1) * AW], proj_ready)
                for t in range(2):
                    evac(("qT", l, t), qT[:, :, t * P:(t + 1) * P], qkT_ready, src=four)
                    evac(("kT", l, t), kT[:, :, t * P:(t + 1) * P], qkT_ready, src=four)
                for t in range(2):
                    act.wait_ge(silu_in, 2 * l + t + 1)
                    act.activation(hb[:, t, AW:D], hb[:, t, AW:D], ACT.Silu).then_inc(silu_done, 1)
                for n in range(6):
                    t, heads, nk = DOTS[n]
                    act.wait_ge(logits_ready, 6 * l + n + 1)
                    if n >= 2:
                        wait_full(act, ("PT", l, n - 2))
                    for i, h in enumerate(heads):
                        ins = act.activation(ex[:, n % 2, i * nk:(i + 1) * nk], lg[:, n % 2, i * nk:(i + 1) * nk],
                                             ACT.Exp, bias=negm[:, n % 2, i:i + 1], scale=float(DH) ** -0.5,
                                             accum_out=rsum[:, t, h:h + 1])
                        seq_(ins, sem=exp_part, wait=h == heads[-1])
                    act.sem_inc(exp_ready, 1)
                    if l == 0:
                        ada(0, 4 + n)
                    if n >= 2:
                        act.wait_ge(pv_full, 6 * l + n - 1)
                    evac(("PT", l, n), pt[:, n % 2, :], ptT_ready)
                for t in range(2):
                    for q in range(2):
                        evac(("mT", l, t, q), hT[:, 4 * q:4 * q + 4, t * P:(t + 1) * P], mixedT_ready, src=four)
                for n in range(4):
                    evac(("skT", l, n), skT[:, 4 * n:4 * n + 4, :].rearrange("p g n -> p (g n)"), skT_ready)
                for t in range(2):
                    for q in range(2):
                        o = wait_full(act, ("h2T", l, t, q))
                        act.copy(h2hi[:, 4 * q:4 * q + 4, t * P:(t + 1) * P], four(o)).then_inc(act_hi, 1)
                        act.wait_ge(act_hi, 4 * l + 2 * t + q + 1)
                        evac(("h2T", l, t, q), hT[:, 4 * q:4 * q + 4, t * P:(t + 1) * P], h2T_ready, src=four)

                def scores(blk):
                    for t in range(2):
                        evac(("s", l, blk, t), sc[:, t, 4 * blk:4 * blk + 4, :].rearrange("p g n -> p (g n)"), s_ready)

                for blk in range(4):
                    for s in range(2):
                        g = 4 * blk + 2 * s
                        evac(("qp", l, blk, s), qpT[:, g:g + 2, :].rearrange("p g t -> p (g t)"), qpT_ready)
                    if l == 0:
                        for a in ADA_MID[blk]:
                            ada(*a)
                    if blk:
                        scores(blk - 1)
                scores(3)
                if l == 0:
                    for a in ADA_TAIL:
                        ada(*a)
                for t in range(2):
                    act.wait_ge(gexp_in, 2 * l + t + 1)
                    g = seln[:, 2, :, :].rearrange("p h k -> p (h k)")
                    act.activation(g, g, ACT.Exp).then_inc(gexp_done, 1)
                    evac(("eT", l, t), selT[:, :, t * P:(t + 1) * P], selT_ready,
                         src=lambda o: o[:, 0:3 * P].rearrange("p (a t) -> p a t", a=3))

                if l == 0:
                    act.sem_inc(gate_stored, 2)

                def gate_batch(n, k):
                    nn = n + l * 32
                    act.wait_ge(gate_mm, nn + 1)
                    src = ps[:, 2 * (k % 2):2 * (k % 2) + 2, :].rearrange("p b (t i) -> p (b t) i", i=P)
                    act.copy(gates[:, :, bass.ds(n * 8, 8)].rearrange("p i t -> p t i"), src).then_inc(gate_stored, 1)

                with act.Fori(0, 8) as i:
                    for u in range(4):
                        gate_batch(i * 4 + u, u)

                def split_uT(j, k):
                    jj = j + l * NSTEP
                    for q in range(2):
                        act.wait_ge(uT_turned, jj * 2 + (q + 1))
                        act.copy(uT_hi[:, 4 * q:4 * q + 4, :].rearrange("p k e -> p (k e)"),
                                 ps[:, q, :]).then_inc(uThi_done, 1)

                split_uT(0, 0)

                def step(j, k):
                    jj = j + l * NSTEP
                    act.wait_ge(v_landed[k % 2], loads(l, j, k))
                    if l or k >= 2:
                        act.wait_ge(y_mm, jj - 1)
                    act.copy(v_hi[:, k % 2, :], v_raw[:, k % 2, :]).then_inc(vhi_done, 1)
                    act.wait_ge(act_mm, jj + 1)
                    if k < NSTEP - 1:
                        split_uT(j + 1, k + 1)
                    if l or k >= 2:
                        act.wait_ge(c_done, jj - 1)
                    act.activation(gel[:, k % 2, :], ps[:, 2 + k % 2, 0:T], ACT.Gelu).then_inc(gelu_done, 1)

                expert_steps(act, None, None, step)

        @block_ctx.vector
        def _(dve):
            seq_ = Chain(dve, dve_step)
            asked = [0]

            def rsqrt(last):
                seq_(last, rsqrt_asked, wait=False)
                asked[0] += 1
                dve.wait_ge(rsqrt_done, asked[0])

            def take(name):
                return wait_full(dve, name)

            def give(ins, name):
                b, n = bank(name)
                ins.then_inc(free[b], 1)
                dve.wait_ge(free[b], n)

            tt, ts, stt = dve.tensor_tensor, dve.tensor_scalar, dve.scalar_tensor_tensor

            dve.wait_ge(consts_made, 1)
            dve.wait_ge(pos_landed, 16)
            seq_(dve.tensor_copy(posf[:, :], posi[:, :]))
            for s in range(2):
                for t in range(2):
                    seq_(ts(rope[:, s, t, :], invf[:, :], posf[:, t:t + 1], None, ALU.mult))
            MAGIC = 1.5 * 2.0 ** 23
            C1, C2 = 6.28125, float(np.float32(2 * np.pi - 6.28125).view(np.uint32) and 0.0019350051879882812)
            C3 = 2 * np.pi - C1 - C2
            for s in range(2):
                seq_(ts(ropek[:, s], rope[:, s], 1.0 / (2 * np.pi), 0.25 * s, ALU.mult, ALU.add))
            kf = ropek[:, :, :, :].rearrange("p s a f -> p (s a f)")
            af = rope[:, :, :, :].rearrange("p s a f -> p (s a f)")
            seq_(ts(kf, kf, MAGIC, None, ALU.add))
            seq_(ts(kf, kf, -MAGIC, None, ALU.add))
            for cst in (C1, C2, C3):
                seq_(stt(af, kf, -cst, af, ALU.mult, ALU.add))
            seq_(ts(rope[:, 1], rope[:, 1], float(np.pi / 2), None, ALU.add))
            seq_(ts(af, af, 3.1415925, -3.1415925, ALU.min, ALU.max), rope_args)
            dve.wait_ge(x_landed, 16)

            def rms_stats(src, t, width):
                return dve.tensor_tensor_reduce(out=hb_junk(t, width), in0=src, in1=src, scale=1.0 / width,
                                                scalar=NORM_EPS, op0=ALU.mult, op1=ALU.add,
                                                accum_out=rs[:, t:t + 1])

            def hb_junk(t, width):
                return hb[:, t, 0:width]

            def modulated(l, mod, ready, landed):
                seq_(rms_stats(xs[:, 0, :], 0, D))
                rsqrt(rms_stats(xs[:, 1, :], 1, D))
                dve.wait_ge(landed, 32 * (l + 1))
                seq_(ts(mod[:, 1, :], mod[:, 1, :], 1.0, None, ALU.add))
                for t in range(2):
                    seq_(stt(hb[:, t, :], xs[:, t, :], rs[:, t:t + 1], mod[:, 1, :], ALU.mult, ALU.mult))
                    seq_(tt(hb[:, t, :], hb[:, t, :], mod[:, 0, :], ALU.add), ready)

            def rotate(t, h0, nh):
                v = pjh[:, t, h0:h0 + nh, 0:ROT].rearrange("p h (s f) -> p h s f", s=2)
                pc = rt[:, 0, 0:nh * ROT].rearrange("p (h s f) -> p h s f", s=2, f=HALF)
                pn = rt[:, 1, 0:nh * ROT].rearrange("p (h s f) -> p h s f", s=2, f=HALF)

                def spread(k):
                    return rope[:, k, t, :].unsqueeze(1).unsqueeze(1).to_broadcast([P, nh, 2, HALF])
                seq_(tt(pc, v, spread(1), ALU.mult))
                seq_(tt(pn, v, spread(0), ALU.mult))
                seq_(tt(v[:, :, 0, :], pc[:, :, 0, :], pn[:, :, 1, :], ALU.subtract))
                return tt(v[:, :, 1, :], pc[:, :, 1, :], pn[:, :, 0, :], ALU.add)

            def conv(l, ct):
                o = acc[:, ct, :]
                seq_(ts(o, hc[:, ct, 0:T], cwT[:, ct, 0:1], cwT[:, ct, TAPS:TAPS + 1], ALU.mult, ALU.add))
                for i in range(1, TAPS):
                    seq_(stt(o, hc[:, ct, i:i + T], cwT[:, ct, i:i + 1], o, ALU.mult, ALU.add),
                         conv_ready if i == TAPS - 1 else None)

            def select(l, t):
                nk = P * (t + 1)
                first = True
                for n, (tile, heads, _) in enumerate(DOTS):
                    if tile != t:
                        continue
                    dve.wait_ge(relu_ready, 6 * l + n + 1)
                    for i, h in enumerate(heads):
                        r = relu[:, n % 2, i * nk:(i + 1) * nk]
                        last = relu_used if h == heads[-1] else None
                        if first:
                            seq_(ts(score[:, 0:nk], r, wis[:, t, h:h + 1], 0.0, ALU.mult, ALU.add), last)
                            first = False
                        else:
                            seq_(stt(score[:, 0:nk], r, wis[:, t, h:h + 1], score[:, 0:nk], ALU.mult, ALU.add), last)
                seq_(tt(score[:, nk - P:nk], score[:, nk - P:nk], tri[:, :], ALU.add))
                a, b = score[:, 0:nk], work[:, 0:nk]
                for i in range(SEL // 8):
                    seq_(dve.max(m8[:, :], a))
                    seq_(dve.match_replace(b, m8[:, :], a, TAKEN))
                    a, b = b, a
                seq_(ts(bias[:, t, 0:nk], a, 0.5 * TAKEN, NEG, ALU.is_gt, ALU.mult))
                seq_(tt(bias[:, t, nk - P:nk], bias[:, t, nk - P:nk], tri[:, :], ALU.add))

            for l in range(L):
                modulated(l, moda, h_ready, mod1_landed)
                dve.wait_ge(small_landed, 16 * 6 * (l + 1))
                dve.wait_ge(proj_ready, 10 * l + 4)
                for t in range(2):
                    seq_(dve.bn_stats(bn6[:, t, :], pjh[:, t, 32, :]))
                    seq_(dve.bn_aggr(mv[:, t, :], bn6[:, t, :]))
                rsqrt(ts(rs[:, 0:2], mv[:, :, 1], NORM_EPS, None, ALU.add))
                for t in range(2):
                    seq_(ts(pjh[:, t, 32, :], pjh[:, t, 32, :], mv[:, t, 0:1], rs[:, t:t + 1], ALU.subtract, ALU.mult))
                ki = pjh[:, :, 32, :]
                seq_(tt(ki, ki, gain_small[:, 2, :].unsqueeze(1).to_broadcast([P, 2, DH]), ALU.mult))
                seq_(tt(ki, ki, gain_small[:, 3, :].unsqueeze(1).to_broadcast([P, 2, DH]), ALU.add))
                if l == 0:
                    dve.wait_ge(rope_ready, 1)
                for t in range(2):
                    seq_(rotate(t, 24, NI + 1))
                    seq_(dve.tensor_copy(pjh[:, t, 33, :], pjh[:, t, 32, :]), idx_ready)

                def glu(ct):
                    name = ("cv", l, ct)
                    dve.wait_ge(sig_ready, CT * l + ct + 1)
                    o = take(name)
                    give(tt(hc[:, ct, TAPS - 1:HCW], o[:, 0:T], sig[:, ct % 2, :], ALU.mult), name)
                    dve.sem_inc(glu_done, 1)

                dve.wait_ge(cw_ready, l + 1)
                glu(0)
                glu(1)
                conv(l, 0)
                glu(2)
                glu(3)
                conv(l, 1)
                select(l, 0)
                select(l, 1)
                conv(l, 2)
                conv(l, 3)

                dve.wait_ge(proj_ready, 10 * (l + 1))
                for t in range(2):
                    sq = hb[:, t, :].rearrange("p (h d) -> p h d", d=DH)
                    seq_(tt(sq, pjh[:, t, 0:16, :], pjh[:, t, 0:16, :], ALU.mult))
                    seq_(dve.tensor_reduce(rs[:, 16 * t:16 * t + 16], sq, AX.X, ALU.add))
                rsqrt(ts(rs[:, 0:32], rs[:, 0:32], 1.0 / DH, NORM_EPS, ALU.mult, ALU.add))
                for t in range(2):
                    v = pjh[:, t, 0:16, :]
                    r = rs[:, 16 * t:16 * t + 16].unsqueeze(2).to_broadcast([P, 16, DH])
                    seq_(tt(v, v, r, ALU.mult))
                    v4 = pj[:, t, 0:2 * AW].rearrange("p (s h d) -> p s h d", s=2, d=DH)
                    g = gain_small[:, 0:2, :].unsqueeze(2).to_broadcast([P, 2, NH, DH])
                    seq_(tt(v4, v4, g, ALU.mult))
                    seq_(rotate(t, 0, 16), qk_ready)

                for t in range(2):
                    o = take(("cT", l, t))
                    seq_(dve.bn_stats(bn6[:, t, :], o))
                    seq_(dve.bn_aggr(mv[:, t, :], bn6[:, t, :]))
                rsqrt(ts(rs[:, 0:2], mv[:, :, 1], NORM_EPS, None, ALU.add))
                dve.wait_ge(out_gains_landed, 64 * (l + 1))
                for t in range(2):
                    name = ("cT", l, t)
                    o = take(name)
                    hv = hb[:, t, AW:D]
                    give(ts(hv, o, mv[:, t, 0:1], rs[:, t:t + 1], ALU.subtract, ALU.mult), name)
                    seq_(tt(hv, hv, ln_gb[:, 0, :], ALU.mult))
                    seq_(tt(hv, hv, ln_gb[:, 1, :], ALU.add), silu_in)
                for t in range(2):
                    dve.wait_ge(silu_done, 2 * l + t + 1)
                    ins = rms_stats(hb[:, t, AW:D], t, CW)
                    if t:
                        rsqrt(ins)
                    else:
                        seq_(ins)
                for t in range(2):
                    seq_(stt(hb[:, t, AW:D], hb[:, t, AW:D], rs[:, t:t + 1], out_g[:, AW:D], ALU.mult, ALU.mult))

                def logits(n):
                    t, heads, nk = DOTS[n]
                    nh = len(heads)
                    name = ("S", l, n)
                    o = take(name).rearrange("p (h k) -> p h k", h=nh)
                    if n >= 2:
                        dve.wait_ge(exp_ready, 6 * l + n - 1)
                    v = lg[:, n % 2, :].rearrange("p (h k) -> p h k", h=nh)
                    give(tt(v, o, bias[:, t, 0:nk].unsqueeze(1).to_broadcast([P, nh, nk]), ALU.add), name)
                    seq_(dve.tensor_reduce(gmx[:, n % 2, 0:nh], v, AX.X, ALU.max))
                    seq_(ts(negm[:, n % 2, 0:nh], gmx[:, n % 2, 0:nh], -float(DH) ** -0.5, None, ALU.mult), logits_ready)

                def attended(t):
                    dve.wait_ge(pv_full, 6 * l + (2 if t == 0 else 6))
                    seq_(dve.reciprocal(rinv[:, t, :], rsum[:, t, :]))
                    o = ps[:, 7, :].rearrange("p (h d) -> p h d", d=DH)
                    seq_(tt(hb[:, t, 0:AW].rearrange("p (h d) -> p h d", d=DH), o,
                            rinv[:, t, :].unsqueeze(2).to_broadcast([P, NH, DH]), ALU.mult), pv_free)

                for n in range(6):
                    logits(n)
                    if n == 3:
                        attended(0)
                attended(1)
                for t in range(2):
                    ins = dve.tensor_tensor_reduce(out=lg[:, t, :], in0=hb[:, t, 0:AW], in1=hb[:, t, 0:AW],
                                                   scale=1.0 / AW, scalar=NORM_EPS, op0=ALU.mult, op1=ALU.add,
                                                   accum_out=rs[:, t:t + 1])
                    if t:
                        rsqrt(ins)
                    else:
                        seq_(ins)
                for t in range(2):
                    seq_(stt(hb[:, t, 0:AW], hb[:, t, 0:AW], rs[:, t:t + 1], out_g[:, 0:AW], ALU.mult, ALU.mult),
                         mixed_ready)

                dve.wait_ge(gate_landed, 16 * (2 * l + 1))
                for blk in range(2):
                    cols = slice(blk * 512, blk * 512 + 512)
                    for t in range(2):
                        name = ("out", l, blk, t)
                        o = take(name)
                        give(tt(lg[:, t, :], o, gmod[:, cols], ALU.mult), name)
                        seq_(tt(xs[:, t, cols], xs[:, t, cols], lg[:, t, :], ALU.add))
                for _ in range(2):
                    pass
                modulated(l, modb, h2_ready, mod2_landed)
                for t in range(2):
                    for q in range(2):
                        dve.wait_ge(h2T_ready, 4 * l + 2 * t + q + 1)
                        a = (slice(None), slice(4 * q, 4 * q + 4), slice(t * P, (t + 1) * P))
                        seq_(tt(h2lo[a], hT[a], h2hi[a].bitcast(F32), ALU.subtract), h2lo_done)

                for blk in range(4):
                    for t in range(2):
                        dve.wait_ge(s_ready, 8 * l + 2 * blk + t + 1)
                        for i in range(4):
                            g = 4 * blk + i
                            s = sc[:, t, g, :]
                            w = work1[:, 0:NK]
                            seq_(dve.max(v1[:, t, i, 0:8], s))
                            seq_(dve.max_index(i1u[:, i, 0:8], v1[:, t, i, 0:8], s))
                            seq_(dve.match_replace(w, v1[:, t, i, 0:8], s, TAKEN))
                            seq_(dve.max(v1[:, t, i, 8:16], w))
                            seq_(dve.max_index(i1u[:, i, 8:16], v1[:, t, i, 8:16], w))
                        for r in range(2):
                            seq_(dve.tensor_copy(i1f[:, t, r, 2 * blk:2 * blk + 2, :],
                                                 i1u[:, 0:4, :].rearrange("p (h s) k -> p h s k", s=2)[:, :, r, :]))
                        cd = cand[:, t * 1024:t * 1024 + 512].rearrange("p (h a b) -> p h a b", a=16, b=16)
                        v = v1[:, t, 0:4, :].rearrange("p (h s) k -> p h s k", s=2)
                        for h in range(2):
                            seq_(tt(cd[:, h], v[:, h, 0, :].unsqueeze(2).to_broadcast([P, 16, 16]),
                                    v[:, h, 1, :].unsqueeze(1).to_broadcast([P, 16, 16]), ALU.add))
                        for h in range(2):
                            hh = 2 * blk + h
                            s = cand[:, t * 1024 + h * 256:t * 1024 + h * 256 + 256]
                            seq_(dve.max(topv[:, t, hh, 0:8], s))
                            seq_(dve.max_index(posu[:, t, hh, 0:8], topv[:, t, hh, 0:8], s))
                            seq_(dve.match_replace(work1[:, :], topv[:, t, hh, 0:8], s, TAKEN))
                            seq_(dve.max(topv[:, t, hh, 8:16], work1[:, :]))
                            seq_(dve.max_index(posu[:, t, hh, 8:16], topv[:, t, hh, 8:16], work1[:, :]))

                for t in range(2):
                    if l or t:
                        wait_full(dve, ("eT", l, t - 1) if t else ("eT", l - 1, 1))
                    g = seln[:, 2, :, :]
                    seq_(tt(g, topv[:, t], topv[:, t, :, 0:1].to_broadcast([P, HP, 16]), ALU.subtract), gexp_in)
                    pu = pab.bitcast(U32)[:, 0:128]
                    pf = pab[:, 128:256]
                    flatpos = posu[:, t].rearrange("p h k -> p (h k)")
                    for r in range(2):
                        if r == 0:
                            seq_(ts(pu, flatpos, 4, None, ALU.logical_shift_right))
                        else:
                            seq_(ts(pu, flatpos, 15, None, ALU.bitwise_and))
                        seq_(dve.tensor_copy(pf, pu))
                        e = eq.rearrange("p (m a) -> p m a", a=16)
                        seq_(tt(e, pf.unsqueeze(2).to_broadcast([P, 128, 16]),
                                iota[:, 0:16].unsqueeze(1).to_broadcast([P, 128, 16]), ALU.is_equal))
                        e4 = eq.rearrange("p (h k a) -> p h k a", h=HP, a=16)
                        seq_(tt(e4, e4, i1f[:, t, r].unsqueeze(2).to_broadcast([P, HP, 16, 16]), ALU.mult))
                        seq_(dve.tensor_reduce(seln[:, r, :, :].rearrange("p h k -> p (h k)"), e, AX.X, ALU.add))
                    dve.wait_ge(gexp_done, 2 * l + t + 1)
                    seq_(dve.tensor_reduce(rs[:, 0:HP], g, AX.X, ALU.add))
                    seq_(dve.reciprocal(rs[:, 8:16], rs[:, 0:HP]))
                    seq_(tt(g, g, rs[:, 8:16].unsqueeze(2).to_broadcast([P, HP, 16]), ALU.mult), sel_ready)

                dve.wait_ge(selT_ready, 2 * (l + 1))
                if l == 0:
                    for i in range(2):
                        dve.wait_ge(mod_stored[i], 16 * (len(mod_order) // 2))
                ramp = iota[:, :].unsqueeze(1).to_broadcast([P, 8, P])

                def gate_batch(n, k):
                    nn = n + l * 32
                    if l or k >= 2 or not isinstance(n, int):
                        pass
                    dve.wait_ge(gate_stored, nn + 1)
                    for r, dst, ready in ((1, u_raw, b_onehot), (0, v_raw, a_onehot)):
                        hot = dst[:, k % 2, :].rearrange("p (t i) -> p t i", t=8)
                        e = selT[:, r, bass.ds(n * 8, 8)].unsqueeze(2).to_broadcast([P, 8, P])
                        tt(hot, ramp, e, ALU.is_equal).then_inc(ready, 1)

                with dve.Fori(0, 8) as i:
                    for u in range(4):
                        gate_batch(i * 4 + u, u)

                def split_uT(j, k):
                    jj = j + l * NSTEP
                    for q in range(2):
                        dve.wait_ge(uThi_done, jj * 2 + (q + 1))
                        hi = uT_hi[:, 4 * q:4 * q + 4, :].rearrange("p k e -> p (k e)")
                        lo = uT_lo[:, 4 * q:4 * q + 4, :].rearrange("p k e -> p (k e)")
                        tt(lo, ps[:, q, :], hi.bitcast(F32), ALU.subtract).then_inc(uTlo_done, 1)

                split_uT(0, 0)

                def step(j, k):
                    jj = j + l * NSTEP
                    s = k % 2
                    dve.wait_ge(vhi_done, jj + 1)
                    tt(v_lo[:, s, :], v_raw[:, s, :], v_hi[:, s, :].bitcast(F32), ALU.subtract).then_inc(vlo_done, 1)
                    if k < NSTEP - 1:
                        split_uT(j + 1, k + 1)
                    dve.wait_ge(gelu_done, jj + 1)
                    seq_(tt(gel[:, s, :], gel[:, s, :], gates[:, j, :] if isinstance(j, int)
                            else gates[:, bass.ds(j, 1), :].rearrange("p a t -> p (a t)"), ALU.mult))
                    seq_(dve.tensor_copy(c_hi[:, s, :], gel[:, s, :]))
                    tt(c_lo[:, s, :], gel[:, s, :], c_hi[:, s, :].bitcast(F32), ALU.subtract).then_inc(c_done, 1)

                expert_steps(dve, seq_, {dve_step: 8}, step)

                dve.wait_ge(y_mm, NSTEP * (l + 1))
                dve.wait_ge(gate_landed, 32 * (l + 1))
                for t in range(2):
                    for q in range(2):
                        cols = slice(q * 512, q * 512 + 512)
                        gy = gel[:, :, :].rearrange("p a n -> p (a n)")
                        seq_(tt(gy, ps[:, 4 + 2 * t + q, :], gmod[:, cols], ALU.mult))
                        seq_(tt(xs[:, t, cols], xs[:, t, cols], gy, ALU.add), x_done if q else None)


DOTS = [(0, (0, 2, 4, 6), 128), (0, (1, 3, 5, 7), 128),
        (1, (0, 2), 256), (1, (4, 6), 256), (1, (1, 3), 256), (1, (5, 7), 256)]

_INS = ["x", "c", "positions", "w_ada", "b_ada", "w_in", "q_norm_g", "k_norm_g", "idx_k_ln_g",
        "idx_k_ln_b", "conv_dw", "conv_b", "conv_ln_g", "conv_ln_b", "out_g_attn", "out_g_conv",
        "w_out", "peer_wq", "peer_sub_keys", "peer_u", "peer_v"]


def kernel(**inputs):
    import concourse.bacc as bacc
    from concourse.bass_utils import run_bass_kernel_spmd

    nc = bacc.Bacc("TRN2", target_bir_lowering=False, num_devices=1)
    arrays, args = {}, {}
    for name in _INS:
        a = np.ascontiguousarray(inputs[name])
        arrays[f"in_{name}"] = a
        args[name] = nc.dram_tensor(f"in_{name}", a.shape, mybir.dt.from_np(a.dtype), kind="ExternalInput").ap()
    o = nc.dram_tensor("out_x", inputs["x"].shape, F32, kind="ExternalOutput").ap()
    trunk(nc, out=o, **args)
    r = run_bass_kernel_spmd(nc, [arrays], core_ids=[0])
    return r.results[0]["out_x"]
```

```python
from contextlib import ExitStack

import numpy as np

import concourse.bass as bass
from concourse import mybir

F32 = mybir.dt.float32
F32R = mybir.dt.float32r
I32 = mybir.dt.int32
U32 = mybir.dt.uint32
ALU = mybir.AluOpType
ACT = mybir.ActivationFunctionType
AX = mybir.AxisListType

P = 128
NORM_EPS = 1e-6
ROPE_THETA = 500000.0
PEER_TOPK = 16
NEG = -1.0e30
TAKEN = -3.0e38
RING = 7
WSLOTS = 3


class Chain:

    def __init__(self, eng, step_sem):
        self.eng, self.step_sem, self.count = eng, step_sem, {}
        self.i, self.per, self.start = None, {}, {}

    def lag(self, ins):
        self(ins, wait=False)
        if self.count[self.step_sem] > 1:
            self.eng.wait_ge(self.step_sem, self.count[self.step_sem] - 1)

    def settle(self):
        self.eng.wait_ge(self.step_sem, self.count[self.step_sem])

    def __call__(self, ins, sem=None, wait=True):
        s = self.step_sem if sem is None else sem
        n = self.count.get(s, 0) + 1
        self.count[s] = n
        ins.then_inc(s, 1)
        if wait:
            self.eng.wait_ge(s, n if self.i is None else n + self.i * self.per[s])

    def enter(self, i, per):
        self.i, self.per, self.start = i, per, dict(self.count)

    def leave(self, iterations):
        for s, n in self.per.items():
            assert self.count.get(s, 0) - self.start.get(s, 0) == n
            self.count[s] = self.start.get(s, 0) + n * iterations
        self.i = None


def plan(depth):
    seq = []

    def block(*name):
        seq.append(("block", name))

    def job(*name):
        seq.append(("job", name))

    def ada(items):
        for layer, blk in items:
            block("ada", layer, blk)
            job("ada", layer, blk)

    def out_tile(l, t):
        for q in range(2):
            job("mT", l, t, q)
        for b in range(2):
            job("out", l, b, t)

    for l in range(depth):
        more = l == 0 and depth > 1
        if l == 0:
            ada([(0, b) for b in range(4)])
        job("wT", l)
        for t in range(2):
            for q in range(2):
                job("hT", l, t, q)
        block("cu1", l)
        job("cv", l, 2)
        job("cv", l, 3)
        block("cu0", l)
        job("cv", l, 0)
        job("cv", l, 1)
        for name in ("qi", "ki", "q", "k", "v"):
            block(name, l)
            for t in range(2):
                job(name, l, t)
        job("iT", l, 0)
        job("iT", l, 1)
        job("kiT", l)
        for n in range(6):
            job("dot", l, n)
        for t in range(2):
            for name in ("qT", "kT"):
                job(name, l, t)
        for t in range(2):
            job("cT", l, t)
        job("S", l, 0)
        for n in range(6):
            for m in LOGITS_AHEAD[n]:
                job("S", l, m)
            if l == 0:
                ada(ADA_ATTENTION[n])
            job("PT", l, n)
            if n == 3:
                block("out", l, 0)
                block("out", l, 1)
                out_tile(l, 0)
        out_tile(l, 1)
        for q in range(2):
            job("h2T", l, 0, q)
        block("sk", l)
        for n in range(4):
            job("skT", l, n)
        for q in range(2):
            job("h2T", l, 1, q)
        mid = ADA_MID if l == 0 else [[], [], [], []]
        for b in range(4):
            block("wq", l, b)
            job("qp", l, b, 0)
            job("qp", l, b, 1)
            ada(mid[b] if more or l else [])
            if b:
                job("s", l, b - 1, 0)
                job("s", l, b - 1, 1)
        job("s", l, 3, 0)
        job("s", l, 3, 1)
        if more:
            ada(ADA_TAIL)
        job("eT", l, 0)
        job("eT", l, 1)
    return seq


LOGITS_AHEAD = [[1], [2], [3], [4, 5], [], []]
ADA_ATTENTION = [[(0, 4), (0, 5)], [(0, 6), (0, 7)], [(0, 8)], [(0, 9)], [], []]
ADA_MID = [[(0, 10)], [(0, 11), (1, 0)], [(1, 1), (1, 2)], [(1, 3)]]
ADA_TAIL = [(1, b) for b in range(4, 12)]


def trunk(nc, x, c, positions, w_ada, b_ada, w_in, q_norm_g, k_norm_g, idx_k_ln_g, idx_k_ln_b,
          conv_dw, conv_b, conv_ln_g, conv_ln_b, out_g_attn, out_g_conv, w_out, peer_wq,
          peer_sub_keys, peer_u, peer_v, out):
    _, T, D = x.shape
    L = w_ada.shape[0]
    DH = q_norm_g.shape[1]
    TAPS, CW = conv_dw.shape[1:]
    AW = out_g_attn.shape[1]
    NH = AW // DH
    NI = NH
    ROT = DH // 4
    HALF = ROT // 2
    KT = D // P
    CT = CW // P
    HP = peer_sub_keys.shape[1]
    NK = peer_sub_keys.shape[3]
    SEL = min(256, T // 4)
    CU0 = 3 * AW + NI * DH + DH + NI
    assert (T, D, NH, DH, CW, NK, HP) == (256, 1024, 8, 64, 512, 128, 8) and L == 2

    seq = plan(L)
    blocks = [n for kind, n in seq if kind == "block"]
    jobs = [n for kind, n in seq if kind == "job"]
    job_at = {n: i for i, n in enumerate(jobs)}
    block_at = {n: i for i, n in enumerate(blocks)}
    last_job, cur = {}, None
    for kind, n in seq:
        if kind == "block":
            cur = n
        elif n[0] == "out":
            last_job[("out", n[1], n[2])] = n
        elif cur is not None and (n[0] == cur[0] or (cur[0][:2] == "cu" and n[0] == "cv")
                                  or (cur[0], n[0]) in (("sk", "skT"), ("wq", "qp"))):
            last_job[cur] = n

    scratch = nc.dram_tensor("mod_rows", [L, 6 * D], F32, kind="Internal").ap()

    with ExitStack() as ctx:
        def sb(name, shape, dt=F32):
            return ctx.enter_context(nc.sbuf_tensor(name, shape, dt))

        def sem(name):
            return ctx.enter_context(nc.semaphore(name))

        xs = sb("xs", [P, 2, D])
        h2hi = sb("h2hi", [P, KT, T], F32R)
        h2lo = sb("h2lo", [P, KT, T], F32R)
        u_raw = sb("u_raw", [P, 2, D])
        v_raw = sb("v_raw", [P, 2, D])
        uT_hi = sb("uT_hi", [P, KT, P], F32R)
        uT_lo = sb("uT_lo", [P, KT, P], F32R)
        v_hi = sb("v_hi", [P, 2, D], F32R)
        v_lo = sb("v_lo", [P, 2, D], F32R)
        c_hi = sb("c_hi", [P, 2, T], F32R)
        c_lo = sb("c_lo", [P, 2, T], F32R)
        gel = sb("gel", [P, 2, T])
        ident = sb("ident", [P, P])
        iota = sb("iota", [P, P])
        tri = sb("tri", [P, P])
        selT = sb("selT", [P, 3, T])
        bias = sb("bias", [P, 2, T])
        cwT = sb("cwT", [P, CT, TAPS + 1])
        gain_small = sb("gain_small", [P, 4, DH])
        rope = sb("rope", [P, 2, 2, HALF])
        ropek = sb("ropek", [P, 2, 2, HALF])
        invf = sb("invf", [P, HALF])
        posi = sb("posi", [P, 2], I32)
        posf = sb("posf", [P, 2])
        ccol = sb("ccol", [P, KT])
        cact = sb("cact", [P, KT])
        wis = sb("wis", [P, 2, NI])
        rs = sb("rs", [P, 32])
        neghalf = sb("neghalf", [P, 32])
        bn6 = sb("bn6", [P, 2, 6])
        mv = sb("mv", [P, 2, 2])
        m8 = sb("m8", [P, 2, 8])
        negm = sb("negm", [P, 2, 4])
        rsum = sb("rsum", [P, 2, NH])
        rinv = sb("rinv", [P, 2, NH])
        gmx = sb("gmx", [P, 2, 4])

        arena = sb("arena", [P, P * T])
        gates = arena[:, :].rearrange("p (i t) -> p i t", t=T)
        top = [0]

        def cut(n, at=None):
            a = top[0] if at is None else at
            if at is None:
                top[0] = a + n
            assert a + n <= P * T
            return arena[:, a:a + n]

        wring = cut(WSLOTS * 8 * 512).rearrange("p (s n) -> p s n", s=WSLOTS)
        MODA = top[0]
        moda = cut(2 * D).rearrange("p (a n) -> p a n", a=2)
        ln_gb = moda[:, 0, :].rearrange("p (a n) -> p a n", a=2)
        out_g = moda[:, 1, :]
        eq = cut(2 * D, MODA)
        GM0 = top[0]
        gmod = cut(D)
        HT0 = top[0]
        hT = cut(KT * T).rearrange("p (k t) -> p k t", k=KT)
        HB0 = top[0]
        hb = cut(2 * D).rearrange("p (a n) -> p a n", a=2)
        cand = cut(2 * D, HB0)
        P0 = top[0]
        PW = 34 * DH
        pj = cut(2 * PW).rearrange("p (a n) -> p a n", a=2)
        pjh = pj.rearrange("p a (h d) -> p a h d", d=DH)
        sc = cut(2 * 16 * NK, P0).rearrange("p (a g n) -> p a g n", a=2, g=16)
        QK0 = top[0]
        qT = cut(4 * T).rearrange("p (j t) -> p j t", j=4)
        kT = cut(4 * T).rearrange("p (j t) -> p j t", j=4)
        qiT = cut(4 * T).rearrange("p (j t) -> p j t", j=4)
        kiT = cut(T)
        xtmp = qiT.rearrange("p j t -> p (j t)").rearrange("p (b n) -> p b n", b=2)
        skT = cut(16 * NK, QK0).rearrange("p (g n) -> p g n", g=16)
        CV0 = top[0]
        HCW = TAPS - 1 + T
        hc = cut(CT * HCW).rearrange("p (j t) -> p j t", j=CT)
        acc = cut(CT * T).rearrange("p (j t) -> p j t", j=CT)
        modb = cut(2 * D, CV0).rearrange("p (a n) -> p a n", a=2)
        AT0 = top[0]
        lg = cut(2 * 512).rearrange("p (b n) -> p b n", b=2)
        ex = cut(2 * 512).rearrange("p (b n) -> p b n", b=2)
        pt = cut(2 * 512).rearrange("p (b n) -> p b n", b=2)
        cw_raw = cut(CW, AT0)
        relu = lg
        score = ex[:, 0, :].rearrange("p (t n) -> p t n", t=2)
        work = ex[:, 1, :].rearrange("p (t n) -> p t n", t=2)
        tap_tmp = gmod.rearrange("p (b n) -> p b n", b=2)
        rt = pt[:, 0, :].rearrange("p (b n) -> p b n", b=2)
        sig = pt[:, 1, :].rearrange("p (b n) -> p b n", b=2)
        qpT = cut(16 * T, CV0).rearrange("p (g t) -> p g t", g=16)
        TK0 = CV0 + 16 * T
        v1 = cut(256, TK0).rearrange("p (a g k) -> p a g k", a=2, g=8)
        i1u = cut(256, TK0 + 256).bitcast(U32).rearrange("p (g k) -> p g k", k=16)
        work1 = cut(256, TK0 + 512)
        i1f = cut(512, GM0).rearrange("p (a r h k) -> p a r h k", a=2, r=2, h=HP)
        topv = cut(256, TK0 + 768).rearrange("p (a h k) -> p a h k", a=2, h=HP)
        posu = cut(256, TK0 + 1024).bitcast(U32).rearrange("p (a h k) -> p a h k", a=2, h=HP)
        seln = cut(384, GM0 + 512).rearrange("p (r h k) -> p r h k", r=3, h=HP)
        pab = cut(256, TK0 + 1280)
        assert TK0 + 1536 <= P * T

        ps = ctx.enter_context(nc.psum_tensor("ps", [P, 8, 512], F32))

        full = [sem(f"bank{b}_full") for b in range(RING)]
        free = [sem(f"bank{b}_free") for b in range(RING)]
        w_in_slot = [sem(f"weights_landed{s}") for s in range(WSLOTS)]
        x_landed = sem("x_landed")
        c_landed = sem("c_landed")
        pos_landed = sem("pos_landed")
        small_landed = sem("small_landed")
        consts_made = sem("consts_made")
        pool_step = sem("pool_step")
        dve_step = sem("dve_step")
        act_step = sem("act_step")
        cact_made = sem("cact_made")
        mod_stored = [sem(f"mod_stored{i}") for i in range(2)]
        mod1_landed = sem("mod1_landed")
        out_gains_landed = sem("out_gains_landed")
        gate_landed = sem("gate_landed")
        mod2_landed = sem("mod2_landed")
        rsqrt_asked = sem("rsqrt_asked")
        rsqrt_done = sem("rsqrt_done")
        rope_ready = sem("rope_ready")
        rope_args = sem("rope_args")
        cw_ready = sem("cw_ready")
        h_ready = sem("h_ready")
        hT_ready = sem("hT_ready")
        proj_ready = sem("proj_ready")
        idx_ready = sem("idx_ready")
        idxT_ready = sem("idxT_ready")
        sig_ready = sem("sig_ready")
        glu_done = sem("glu_done")
        exp_part = sem("exp_part")
        act_hi = sem("act_hi")
        h2lo_done = sem("h2lo_done")
        relu_ready = sem("relu_ready")
        relu_used = sem("relu_used")
        conv_ready = sem("conv_ready")
        conv_pool = sem("conv_pool")
        qk_ready = sem("qk_ready")
        qkT_ready = sem("qkT_ready")
        logits_ready = sem("logits_ready")
        exp_ready = sem("exp_ready")
        ptT_ready = sem("ptT_ready")
        pv_full = sem("pv_full")
        pv_free = sem("pv_free")
        silu_in = sem("silu_in")
        silu_done = sem("silu_done")
        mixed_ready = sem("mixed_ready")
        mixedT_ready = sem("mixedT_ready")
        xmid_ready = sem("xmid_ready")
        skT_ready = sem("skT_ready")
        h2_ready = sem("h2_ready")
        h2T_ready = sem("h2T_ready")
        qpT_ready = sem("qpT_ready")
        s_ready = sem("s_ready")
        gexp_in = sem("gexp_in")
        gexp_done = sem("gexp_done")
        sel_ready = sem("sel_ready")
        selT_ready = sem("selT_ready")
        hot_ready = sem("hot_ready")
        hot2_ready = sem("hot2_ready")
        gated = sem("gated")
        gate_mm = sem("gate_mm")
        gate_stored = sem("gate_stored")
        u_landed = [sem(f"u_landed{s}") for s in range(2)]
        v_landed = [sem(f"v_landed{s}") for s in range(2)]
        uT_turned = sem("uT_turned")
        uThi_done = sem("uThi_done")
        uTlo_done = sem("uTlo_done")
        vhi_done = sem("vhi_done")
        vlo_done = sem("vlo_done")
        act_mm = sem("act_mm")
        gelu_done = sem("gelu_done")
        c_done = sem("c_done")
        y_mm = sem("y_mm")
        x_done = sem("x_done")
        out_stored = sem("out_stored")

        def bank(name):
            n = job_at[name]
            return n % RING, n // RING + 1

        def wait_full(eng, name):
            b, n = bank(name)
            eng.wait_ge(full[b], n)
            return ps[:, b, :]

        mod_order = [(n[1], n[2]) for n in blocks if n[0] == "ada"]
        BT = 4
        NBATCH = T // BT
        NSTEP = NK

        def expert_steps(eng, chain, per, step):
            step(0, 0)
            step(1, 1)
            with eng.Fori(0, (NSTEP - 4) // 4) as i:
                if chain is not None:
                    chain.enter(i, per)
                for u in range(4):
                    step(i * 4 + (2 + u), 2 + u)
                if chain is not None:
                    chain.leave((NSTEP - 4) // 4)
            step(NSTEP - 2, NSTEP - 2)
            step(NSTEP - 1, NSTEP - 1)

        def brow(n):
            s = n % WSLOTS
            return v_raw[0:1, s // 2, (s % 2) * 512:(s % 2) * 512 + 512]

        def stage(m):
            return gel[:, m % 2, 0:P]

        def loads(l, j, k):
            if isinstance(j, int):
                return 16 * ((l * NSTEP + j) // 2 + 1)
            return (j - k % 2) * 8 + 16 * (l * NSTEP // 2 + 1)

        def hot_rows(k):
            raw = (u_raw, v_raw)[k % 4 // 2]
            return raw[:, k % 2, :].rearrange("p (r t i) -> p r t i", r=2, t=BT)

        def gate_batches(eng, batch):
            with eng.Fori(0, NBATCH // 8) as i:
                for k in range(8):
                    batch(i * 8 + k, i * (8 * BT) + k * BT, k)

        block_ctx = ctx.enter_context(nc.Block())

        @block_ctx.sync
        def _(sp):
            sp.dma_start(ccol[:, :], c[0, :].rearrange("(p k) -> p k", k=KT)).then_inc(c_landed, 16)
            sp.dma_start(xs[:, :, :], x[0].rearrange("(a p) d -> p a d", p=P)).then_inc(x_landed, 16)

            def load_block(n):
                name = blocks[n]
                slot = n % WSLOTS
                if n >= WSLOTS:
                    b, k = bank(last_job[blocks[n - WSLOTS]])
                    sp.wait_ge(full[b], k)
                w = wring[:, slot, :].rearrange("p (k n) -> p k n", k=KT)
                l = name[1]
                got = w_in_slot[slot]
                win = w_in[l].rearrange("(k p) n -> p k n", p=P)
                if name[0] == "ada":
                    src = w_ada[l].rearrange("(p k) n -> p k n", k=KT)[:, :, name[2] * 512:name[2] * 512 + 512]
                    sp.dma_start(w, src).then_inc(got, 16)
                    sp.dma_start(brow(n), b_ada[l:l + 1, name[2] * 512:name[2] * 512 + 512]).then_inc(got, 16)
                    return
                if name[0] in ("q", "k", "v", "qi"):
                    a = {"q": 0, "k": 1, "v": 2, "qi": 3}[name[0]] * AW
                    pieces = [(w, win[:, :, a:a + 512])]
                elif name[0] == "ki":
                    pieces = [(w[:, :, 0:DH + NI], win[:, :, 4 * AW:CU0])]
                elif name[0] in ("cu0", "cu1"):
                    a = CU0 + 256 * int(name[0][2])
                    pieces = [(w[:, :, 0:256], win[:, :, a:a + 256]),
                              (w[:, :, 256:512], win[:, :, a + CW:a + CW + 256])]
                elif name[0] == "out":
                    pieces = [(w, w_out[l].rearrange("(k p) n -> p k n", p=P)[:, :, name[2] * 512:name[2] * 512 + 512])]
                elif name[0] == "wq":
                    pieces = [(w, peer_wq[l].rearrange("(k p) n -> p k n", p=P)[:, :, name[2] * 512:name[2] * 512 + 512])]
                else:
                    pieces = [(wring[:, slot, 0:16 * NK].rearrange("p (g n) -> p g n", g=16),
                               peer_sub_keys[l].rearrange("h s n k -> n (h s) k"))]
                for dst, src in pieces:
                    sp.dma_start(dst, src).then_inc(got, 16)

            n = 0
            for l in range(L):
                while n < len(blocks) and (blocks[n][1] == l or blocks[n][0] == "ada"):
                    if l and n == block_at[("cu1", l)]:
                        sp.wait_ge(c_done, l * NSTEP)
                    load_block(n)
                    n += 1
                sp.wait_ge(gate_mm, (l + 1) * NBATCH + 4)

                def load_experts(j, k):
                    jj = j + l * NSTEP
                    if k >= 2:
                        sp.wait_ge(uT_turned, jj * 2 - 2)
                    sp.dma_start(u_raw[:, k % 2, :],
                                 peer_u[l, bass.ds(j * P, P), :]).then_inc(u_landed[k % 2], 16)
                    if k >= 2:
                        sp.wait_ge(vlo_done, jj - 1)
                    sp.dma_start(v_raw[:, k % 2, :],
                                 peer_v[l, bass.ds(j * P, P), :]).then_inc(v_landed[k % 2], 16)

                expert_steps(sp, None, None, load_experts)
            sp.wait_ge(x_done, 2 * L)
            sp.dma_start(out[0].rearrange("(a p) d -> p a d", p=P), xs[:, :, :]).then_inc(out_stored, 16)
            sp.wait_ge(out_stored, 16)

        @block_ctx.gpsimd
        def _(pool):
            seq_ = Chain(pool, pool_step)
            seq_(pool.memset(ident[:, :], 0.0))
            seq_(pool.affine_select(out=ident[:, :], in_=ident[:, :], compare_op=ALU.not_equal, fill=1.0,
                                    base=0, pattern=[[-1, P]], channel_multiplier=1))
            seq_(pool.iota(iota[:, :], [[1, P]], base=0, channel_multiplier=0,
                           allow_small_or_imprecise_dtypes=True))
            seq_(pool.memset(tri[:, :], 0.0))
            seq_(pool.affine_select(out=tri[:, :], in_=tri[:, :], compare_op=ALU.is_ge, fill=NEG,
                                    base=0, pattern=[[-1, P]], channel_multiplier=1))
            seq_(pool.memset(neghalf[:, :], -0.5))
            inv_freq = np.power(np.float32(ROPE_THETA), -np.arange(0, ROT, 2, dtype=np.float32) / ROT)
            for i, f in enumerate(inv_freq):
                seq_(pool.memset(invf[:, i:i + 1], float(f)))
            seq_(pool.memset(hc[:, :, 0:TAPS - 1], 0.0))
            seq_(pool.memset(rs[:, :], 1.0), consts_made)
            pool.dma_start(posi[:, :], positions[0, :].rearrange("(a p) -> p a", p=P),
                           allow_slow_non_contiguous=True).then_inc(pos_landed, 16)

            asked = 0

            def rsqrt(width):
                nonlocal asked
                asked += 1
                pool.wait_ge(rsqrt_asked, asked)
                pool.tensor_tensor(rs[:, 0:width], rs[:, 0:width], neghalf[:, 0:width],
                                   ALU.pow).then_inc(rsqrt_done, 1)

            def mod_rows(l, first, last):
                m = mod_order.index((l, last))
                for i in range(2):
                    pool.wait_ge(mod_stored[i], 16 * ((m - i) // 2 + 1))

            def spread(dst, src, landed):
                pool.dma_start(dst, src).then_inc(landed, 16)

            for l in range(L):
                if l:
                    pool.wait_ge(c_done, l * NSTEP)
                    seq_(pool.memset(hc[:, :, 0:TAPS - 1], 0.0), consts_made)
                for i, g in enumerate((q_norm_g, k_norm_g, idx_k_ln_g, idx_k_ln_b)):
                    spread(gain_small[:, i, :], g[l, :].partition_broadcast(P), small_landed)
                spread(cw_raw[0:TAPS, :], conv_dw[l], small_landed)
                spread(cw_raw[TAPS:TAPS + 1, :], conv_b[l:l + 1, :], small_landed)
                mod_rows(l, 0, 3)
                if l:
                    pool.wait_ge(x_done, 2 * l)
                for i in range(2):
                    spread(moda[:, i, :], scratch[l, i * D:(i + 1) * D].partition_broadcast(P), mod1_landed)
                rsqrt(2)
                pool.wait_ge(h_ready, 2 * (l + 1))
                spread(ln_gb[:, 0, :], conv_ln_g[l, :].partition_broadcast(P), out_gains_landed)
                spread(ln_gb[:, 1, :], conv_ln_b[l, :].partition_broadcast(P), out_gains_landed)
                spread(out_g[:, 0:AW], out_g_attn[l, :].partition_broadcast(P), out_gains_landed)
                spread(out_g[:, AW:D], out_g_conv[l, :].partition_broadcast(P), out_gains_landed)
                ct = CONV_ORDER[0]
                pool.wait_ge(cw_ready, l + 1)
                pool.wait_ge(glu_done, CT * l + 1)
                o = acc[:, ct, :]
                seq_(pool.tensor_scalar(o, hc[:, ct, 0:T], cwT[:, ct, 0:1], cwT[:, ct, TAPS:TAPS + 1],
                                        ALU.mult, ALU.add))
                for i in range(1, TAPS):
                    p = tap_tmp[:, i % 2, 0:T]
                    seq_(pool.tensor_scalar(p, hc[:, ct, i:i + T], cwT[:, ct, i:i + 1], None, ALU.mult))
                    seq_(pool.tensor_tensor(o, o, p, ALU.add), conv_pool if i == TAPS - 1 else None)
                    if i == POOL_TAPS[0]:
                        rsqrt(2)
                    if i == POOL_TAPS[1]:
                        rsqrt(32)
                rsqrt(2)
                rsqrt(2)
                mod_rows(l, 4, 5)
                spread(gmod, scratch[l, 2 * D:3 * D].partition_broadcast(P), gate_landed)
                for t in range(2):
                    wait_full(pool, ("cT", l, t))
                mod_rows(l, 6, 9)
                for i in range(2):
                    spread(modb[:, i, :], scratch[l, (3 + i) * D:(4 + i) * D].partition_broadcast(P), mod2_landed)
                for t in range(2):
                    rsqrt(1)
                for t in range(2):
                    rsqrt(1)

                def gate_batch(n, t0, k):
                    pool.wait_ge(hot_ready, n + (l * NBATCH + 1))
                    hot = hot_rows(k)[:, 0]
                    g = selT[:, 2, bass.ds(t0, BT)].unsqueeze(2).to_broadcast([P, BT, P])
                    pool.tensor_tensor(hot, hot, g, ALU.mult).then_inc(gated, 1)

                gate_batches(pool, gate_batch)
                mod_rows(l, 10, 11)
                pool.wait_ge(c_done, (l + 1) * NSTEP)
                spread(gmod, scratch[l, 5 * D:6 * D].partition_broadcast(P), gate_landed)

        @block_ctx.tensor
        def _(pe):
            done = [0]
            state = {"block": -1}

            def next_is(kind, name):
                assert seq[done[0]] == (kind, name), (seq[done[0]], name)
                done[0] += 1

            landed_count = [0] * WSLOTS

            def use_block(*name):
                next_is("block", name)
                n = block_at[name]
                slot = n % WSLOTS
                landed_count[slot] += 2 if name[0] in ("ada", "cu0", "cu1") else 1
                pe.wait_ge(w_in_slot[slot], 16 * landed_count[slot])
                state["block"] = n
                return wring[:, slot, :].rearrange("p (k n) -> p k n", k=KT)

            def open_job(*name):
                next_is("job", name)
                b, n = bank(name)
                if n > 1:
                    pe.wait_ge(free[b], n - 1)
                return b, ps[:, b, :]

            def mm_all(o, pairs):
                for i, (a, b) in enumerate(pairs):
                    ins = pe.matmul(o, a, b, start=i == 0, stop=i == len(pairs) - 1)
                return ins

            def ada(layer, blk):
                w = use_block("ada", layer, blk)
                b, o = open_job("ada", layer, blk)
                for k in range(KT + 1):
                    for q in range(4):
                        cols = slice(q * P, (q + 1) * P)
                        if k < KT:
                            lhs, rhs = cact[:, k:k + 1].to_broadcast([P, 32]), w[:, k, cols]
                        else:
                            lhs, rhs = ident[0:1, 0:1].to_broadcast([1, 32]), brow(state["block"])[:, cols]
                        ins = pe.matmul(o[32 * q:32 * q + 32, 0:P], lhs, rhs, start=k == 0, stop=k == KT)
                ins.then_inc(full[b], 1)

            def turn4(name, srcs, width=P):
                b, o = open_job(*name)
                for i, s in enumerate(srcs):
                    n = s.shape[0]
                    ins = pe.transpose(o[:, i * n:(i + 1) * n], s, ident[0:n, 0:n])
                ins.then_inc(full[b], 1)

            def proj(w, name, lhs, width):
                b, o = open_job(*name)
                mm_all(o[:, 0:width], [(lhs[:, k, :], w[:, k, 0:width]) for k in range(KT)]).then_inc(full[b], 1)

            pe.wait_ge(consts_made, 1)
            pe.wait_ge(cact_made, 1)
            for blk in range(4):
                ada(0, blk)
            for l in range(L):
                if l:
                    pe.wait_ge(x_done, 2 * l)
                pe.wait_ge(small_landed, 16 * 6 * (l + 1))
                turn4(("wT", l), [cw_raw[0:TAPS + 1, j * P:(j + 1) * P] for j in range(CT)])
                for t in range(2):
                    pe.wait_ge(h_ready, 2 * l + t + 1)
                    for q in range(2):
                        turn4(("hT", l, t, q), [hb[:, t, (4 * q + i) * P:(4 * q + i + 1) * P] for i in range(4)])
                pe.wait_ge(hT_ready, 4 * (l + 1))
                def conv_proj(w, ct):
                    b, o = open_job("cv", l, ct)
                    for s in range(2):
                        col = s * 256 + (ct % 2) * P
                        ins = mm_all(o[:, s * T:(s + 1) * T],
                                     [(w[:, k, col:col + P], hT[:, k, :]) for k in range(KT)])
                    ins.then_inc(full[b], 1)

                for name, ct in (("cu1", 2), ("cu0", 0)):
                    w = use_block(name, l)
                    conv_proj(w, ct)
                    conv_proj(w, ct + 1)

                def token_proj(name, width=512):
                    w = use_block(name, l)
                    for t in range(2):
                        proj(w, (name, l, t), hT[:, :, t * P:(t + 1) * P], width)

                token_proj("qi")
                token_proj("ki", DH + NI)
                token_proj("q")
                token_proj("k")
                token_proj("v")
                for t in range(2):
                    pe.wait_ge(idx_ready, 2 * l + t + 1)
                    turn4(("iT", l, t), [pj[:, t, (12 + i) * P:(13 + i) * P] for i in range(4)])
                turn4(("kiT", l), [pj[:, t, 16 * P:17 * P] for t in range(2)])
                pe.wait_ge(idxT_ready, 3 * (l + 1))
                for n in range(6):
                    t, heads, nk = DOTS[n]
                    b, o = open_job("dot", l, n)
                    for i, h in enumerate(heads):
                        r = (h % 2) * DH
                        ins = pe.matmul(o[:, i * nk:(i + 1) * nk], qiT[r:r + DH, h // 2, t * P:(t + 1) * P],
                                        kiT[r:r + DH, 0:nk], start=True, stop=True)
                    ins.then_inc(full[b], 1)
                for t in range(2):
                    pe.wait_ge(qk_ready, 2 * l + t + 1)
                    turn4(("qT", l, t), [pj[:, t, i * P:(i + 1) * P] for i in range(4)])
                    turn4(("kT", l, t), [pj[:, t, (4 + i) * P:(5 + i) * P] for i in range(4)])
                pe.wait_ge(conv_ready, (CT - 1) * (l + 1))
                pe.wait_ge(conv_pool, l + 1)
                for t in range(2):
                    turn4(("cT", l, t), [acc[:, j, t * P:(t + 1) * P] for j in range(CT)])

                pe.wait_ge(qkT_ready, 4 * (l + 1))

                def logits(n):
                    t, heads, nk = DOTS[n]
                    b, o = open_job("S", l, n)
                    for i, h in enumerate(heads):
                        r = (h % 2) * DH
                        ins = pe.matmul(o[:, i * nk:(i + 1) * nk], qT[r:r + DH, h // 2, t * P:(t + 1) * P],
                                        kT[r:r + DH, h // 2, 0:nk], start=True, stop=True)
                    ins.then_inc(full[b], 1)

                def values(n):
                    t, heads, nk = DOTS[n]
                    pe.wait_ge(ptT_ready, 6 * l + n + 1)
                    if heads[0] == 0 and (l or t):
                        pe.wait_ge(pv_free, 2 * l + t)
                    for i, h in enumerate(heads):
                        for kb in range(nk // P):
                            ins = pe.matmul(ps[:, 7, h * DH:(h + 1) * DH],
                                            pt[:, n % 2, (i * (nk // P) + kb) * P:(i * (nk // P) + kb + 1) * P],
                                            pjh[:, kb, 16 + h, :], start=kb == 0, stop=kb == nk // P - 1)
                    ins.then_inc(pv_full, 1)

                pe.wait_ge(proj_ready, 10 * (l + 1))
                logits(0)
                w_out_blocks = []

                def out_tile(t):
                    pe.wait_ge(mixed_ready, 2 * l + t + 1)
                    for q in range(2):
                        turn4(("mT", l, t, q), [hb[:, t, (4 * q + i) * P:(4 * q + i + 1) * P] for i in range(4)])
                    pe.wait_ge(mixedT_ready, 4 * l + 2 * (t + 1))
                    for blk in range(2):
                        proj(w_out_blocks[blk], ("out", l, blk, t), hT[:, :, t * P:(t + 1) * P], 512)

                def turn_h2(t):
                    pe.wait_ge(h2_ready, 2 * l + t + 1)
                    for q in range(2):
                        turn4(("h2T", l, t, q), [hb[:, t, (4 * q + i) * P:(4 * q + i + 1) * P] for i in range(4)])

                for n in range(6):
                    for m in LOGITS_AHEAD[n]:
                        logits(m)
                    if n:
                        values(n - 1)
                    if l == 0:
                        for a in ADA_ATTENTION[n]:
                            ada(*a)
                    pe.wait_ge(exp_ready, 6 * l + n + 1)
                    turn4(("PT", l, n), [ex[:, n % 2, i * P:(i + 1) * P] for i in range(4)])
                    if n == 3:
                        for blk in range(2):
                            w_out_blocks.append(use_block("out", l, blk))
                        out_tile(0)
                values(5)
                out_tile(1)
                turn_h2(0)
                use_block("sk", l)
                raw = wring[:, block_at[("sk", l)] % WSLOTS, 0:16 * NK].rearrange("p (g n) -> p g n", g=16)
                for n in range(4):
                    turn4(("skT", l, n), [raw[:, 4 * n + i, :] for i in range(4)])
                turn_h2(1)
                pe.wait_ge(h2T_ready, 4 * (l + 1))
                pe.wait_ge(skT_ready, 4 * (l + 1))

                def subkeys(blk):
                    pe.wait_ge(qpT_ready, 2 * (4 * l + blk + 1))
                    for t in range(2):
                        b, o = open_job("s", l, blk, t)
                        for i in range(4):
                            g = 4 * blk + i
                            ins = pe.matmul(o[:, i * NK:(i + 1) * NK], qpT[:, g, t * P:(t + 1) * P], skT[:, g, :],
                                            start=True, stop=True)
                        ins.then_inc(full[b], 1)

                for blk in range(4):
                    w = use_block("wq", l, blk)
                    for s in range(2):
                        b, o = open_job("qp", l, blk, s)
                        for i in range(2):
                            col = (2 * s + i) * P
                            ins = mm_all(o[:, i * T:(i + 1) * T],
                                         [(w[:, k, col:col + P], hT[:, k, :]) for k in range(KT)])
                        ins.then_inc(full[b], 1)
                    if l == 0:
                        for a in ADA_MID[blk]:
                            ada(*a)
                    if blk:
                        subkeys(blk - 1)
                subkeys(3)
                if l == 0:
                    for a in ADA_TAIL:
                        ada(*a)
                for t in range(2):
                    pe.wait_ge(sel_ready, 2 * l + t + 1)
                    b, o = open_job("eT", l, t)
                    for i in range(3):
                        ins = pe.transpose(o[:, i * P:(i + 1) * P], seln[:, i, :, :].rearrange("p h k -> p (h k)"),
                                           ident[:, :])
                    ins.then_inc(full[b], 1)

                last_jobs = jobs[:job_at[("eT", l, 1)] + 1][-RING:]
                for name in last_jobs:
                    b, n = bank(name)
                    pe.wait_ge(free[b], n)

                if l == 0:
                    pe.sem_inc(gate_mm, 4)

                def gate_batch(n, t0, k):
                    pe.wait_ge(gated, n + (l * NBATCH + 1))
                    pe.wait_ge(hot2_ready, n + (l * NBATCH + 1))
                    pe.wait_ge(gate_stored, n + (l * NBATCH + 1))
                    hot = hot_rows(k)
                    for t in range(BT):
                        ins = pe.matmul(ps[:, k % 4, t * P:(t + 1) * P], hot[:, 1, t, :], hot[:, 0, t, :],
                                        start=True, stop=True)
                    ins.then_inc(gate_mm, 1)

                gate_batches(pe, gate_batch)

                def turn(j, k):
                    pe.wait_ge(u_landed[k % 2], loads(l, j, k))
                    for q in range(2):
                        for i in range(4):
                            d = 4 * q + i
                            ins = pe.transpose(ps[:, q, i * P:(i + 1) * P], u_raw[:, k % 2, d * P:(d + 1) * P],
                                               ident[:, :])
                        ins.then_inc(uT_turned, 1)

                def activations(j, k):
                    jj = j + l * NSTEP
                    pe.wait_ge(uThi_done, jj * 2 + 2)
                    pe.wait_ge(uTlo_done, jj * 2 + 2)
                    o = ps[:, 2 + k % 2, 0:T]
                    for d in range(KT):
                        pe.matmul(o, uT_hi[:, d, :], h2hi[:, d, :], start=d == 0, stop=False)
                        pe.matmul(o, uT_hi[:, d, :], h2lo[:, d, :], start=False, stop=False)
                        ins = pe.matmul(o, uT_lo[:, d, :], h2hi[:, d, :], start=False, stop=d == KT - 1)
                    ins.then_inc(act_mm, 1)

                def outputs(j, k):
                    jj = j + l * NSTEP
                    pe.wait_ge(c_done, jj + 1)
                    pe.wait_ge(vlo_done, jj + 1)
                    s = k % 2
                    for t in range(2):
                        for q in range(2):
                            o = ps[:, 4 + 2 * t + q, :]
                            ts, qs = slice(t * P, (t + 1) * P), slice(q * 512, (q + 1) * 512)
                            pe.matmul(o, c_hi[:, s, ts], v_hi[:, s, qs], start=k == 0, stop=False)
                            pe.matmul(o, c_hi[:, s, ts], v_lo[:, s, qs], start=False, stop=False)
                            ins = pe.matmul(o, c_lo[:, s, ts], v_hi[:, s, qs], start=False, stop=k == NSTEP - 1)
                    ins.then_inc(y_mm, 1)

                pe.wait_ge(h2lo_done, 4 * (l + 1))
                pe.wait_ge(gate_stored, NBATCH * (l + 1) + 4)
                turn(0, 0)

                def step(j, k):
                    activations(j, k)
                    if k < NSTEP - 1:
                        turn(j + 1, k + 1)
                    if k > 0:
                        outputs(j - 1, k - 1)

                expert_steps(pe, None, None, step)
                outputs(NSTEP - 1, NSTEP - 1)
            assert done[0] == len(seq)

        @block_ctx.scalar
        def _(act):
            seq_ = Chain(act, act_step)

            def take(name, fn, signal=None, wait=False):
                o = wait_full(act, name)
                b, _ = bank(name)
                ins = fn(o)
                ins.then_inc(free[b], 1)

            n_mod = [0]

            def ada(layer, blk):
                m = n_mod[0]
                n_mod[0] += 1
                name = ("ada", layer, blk)
                o = wait_full(act, name)
                b, n = bank(name)
                if m >= 2:
                    act.wait_ge(mod_stored[m % 2], 16 * (m // 2))
                act.copy(stage(m), o[:, 0:P]).then_inc(free[b], 1)
                act.wait_ge(free[b], n)
                act.dma_start(scratch[layer, blk * 512:blk * 512 + 512].rearrange("(q n) -> q n", q=4),
                              stage(m)[0:P:32, :]).then_inc(mod_stored[m % 2], 16)

            act.wait_ge(c_landed, 16)
            act.activation(cact[:, :], ccol[:, :], ACT.Silu).then_inc(cact_made, 1)
            act.wait_ge(rope_args, 1)
            flat = rope[:, :, :, :].rearrange("p s a f -> p (s a f)")
            act.activation(flat, flat, ACT.Sin).then_inc(rope_ready, 1)
            for blk in range(4):
                ada(0, blk)

            for l in range(L):
                def evac(name, dst, sem_done, scale=None, src=None):
                    o = wait_full(act, name)
                    b, n = bank(name)
                    s = o if src is None else src(o)
                    ins = act.copy(dst, s) if scale is None else act.mul(dst, s, scale)
                    ins.then_inc(free[b], 1)
                    act.wait_ge(free[b], n)
                    act.sem_inc(sem_done, 1)

                def four(o):
                    return o.rearrange("p (k t) -> p k t", k=4)

                evac(("wT", l), cwT[:, :, :].rearrange("p j t -> p (j t)"), cw_ready,
                     src=lambda o: o[:, 0:CT * (TAPS + 1)])
                for t in range(2):
                    for q in range(2):
                        evac(("hT", l, t, q), hT[:, 4 * q:4 * q + 4, t * P:(t + 1) * P], hT_ready, src=four)
                def sigmoid(n, ct):
                    o = wait_full(act, ("cv", l, ct))
                    if CT * l + n >= 2:
                        act.wait_ge(glu_done, CT * l + n - 1)
                    act.activation(sig[:, n % 2, :], o[:, T:2 * T], ACT.Sigmoid).then_inc(sig_ready, 1)

                for n, ct in enumerate(CONV_ORDER):
                    sigmoid(n, ct)
                for t in range(2):
                    evac(("qi", l, t), pj[:, t, 3 * AW:4 * AW], proj_ready)
                for t in range(2):
                    o = wait_full(act, ("ki", l, t))
                    seq_(act.mul(wis[:, t, :], o[:, DH:DH + NI], float(NI) ** -0.5), wait=False)
                    evac(("ki", l, t), pjh[:, t, 32, :], proj_ready, src=lambda o: o[:, 0:DH])
                for i, name in enumerate(("q", "k", "v")):
                    for t in range(2):
                        evac((name, l, t), pj[:, t, i * AW:(i + 1) * AW], proj_ready)
                for t in range(2):
                    evac(("iT", l, t), qiT[:, :, t * P:(t + 1) * P], idxT_ready, src=four)
                evac(("kiT", l), kiT, idxT_ready, src=lambda o: o[:, 0:T])
                for n in range(6):
                    name = ("dot", l, n)
                    o = wait_full(act, name)
                    b, k = bank(name)
                    if n >= 2:
                        act.wait_ge(relu_used, 6 * l + n - 1)
                    act.activation(relu[:, n % 2, :], o, ACT.Relu, scale=float(DH) ** -0.5).then_inc(free[b], 1)
                    act.wait_ge(free[b], k)
                    act.sem_inc(relu_ready, 1)
                for t in range(2):
                    evac(("qT", l, t), qT[:, :, t * P:(t + 1) * P], qkT_ready, src=four)
                    evac(("kT", l, t), kT[:, :, t * P:(t + 1) * P], qkT_ready, src=four)
                for t in range(2):
                    act.wait_ge(silu_in, 2 * l + t + 1)
                    act.activation(hb[:, t, AW:D], hb[:, t, AW:D], ACT.Silu).then_inc(silu_done, 1)
                def take_mixed(t):
                    for q in range(2):
                        evac(("mT", l, t, q), hT[:, 4 * q:4 * q + 4, t * P:(t + 1) * P], mixedT_ready, src=four)

                def take_h2(t):
                    for q in range(2):
                        o = wait_full(act, ("h2T", l, t, q))
                        act.copy(h2hi[:, 4 * q:4 * q + 4, t * P:(t + 1) * P], four(o)).then_inc(act_hi, 1)
                        act.wait_ge(act_hi, 4 * l + 2 * t + q + 1)
                        evac(("h2T", l, t, q), hT[:, 4 * q:4 * q + 4, t * P:(t + 1) * P], h2T_ready, src=four)

                for n in range(6):
                    t, heads, nk = DOTS[n]
                    act.wait_ge(logits_ready, 6 * l + n + 1)
                    if n >= 2:
                        wait_full(act, ("PT", l, n - 2))
                    for i, h in enumerate(heads):
                        ins = act.activation(ex[:, n % 2, i * nk:(i + 1) * nk], lg[:, n % 2, i * nk:(i + 1) * nk],
                                             ACT.Exp, bias=negm[:, n % 2, i:i + 1], scale=float(DH) ** -0.5,
                                             accum_out=rsum[:, t, h:h + 1])
                        seq_(ins, sem=exp_part, wait=h == heads[-1])
                    act.sem_inc(exp_ready, 1)
                    if l == 0:
                        for a in ADA_ATTENTION[n]:
                            ada(*a)
                    if n >= 2:
                        act.wait_ge(pv_full, 6 * l + n - 1)
                    evac(("PT", l, n), pt[:, n % 2, :], ptT_ready)
                    if n == 3:
                        take_mixed(0)
                take_mixed(1)
                take_h2(0)
                for n in range(4):
                    evac(("skT", l, n), skT[:, 4 * n:4 * n + 4, :].rearrange("p g n -> p (g n)"), skT_ready)
                take_h2(1)

                def scores(blk):
                    for t in range(2):
                        evac(("s", l, blk, t), sc[:, t, 4 * blk:4 * blk + 4, :].rearrange("p g n -> p (g n)"), s_ready)

                for blk in range(4):
                    for s in range(2):
                        g = 4 * blk + 2 * s
                        evac(("qp", l, blk, s), qpT[:, g:g + 2, :].rearrange("p g t -> p (g t)"), qpT_ready)
                    if l == 0:
                        for a in ADA_MID[blk]:
                            ada(*a)
                    if blk:
                        scores(blk - 1)
                scores(3)
                if l == 0:
                    for a in ADA_TAIL:
                        ada(*a)
                for t in range(2):
                    act.wait_ge(gexp_in, 2 * l + t + 1)
                    g = seln[:, 2, :, :].rearrange("p h k -> p (h k)")
                    act.activation(g, g, ACT.Exp).then_inc(gexp_done, 1)
                    evac(("eT", l, t), selT[:, :, t * P:(t + 1) * P], selT_ready,
                         src=lambda o: o[:, 0:3 * P].rearrange("p (a t) -> p a t", a=3))

                if l == 0:
                    act.sem_inc(gate_stored, 4)

                def gate_batch(n, t0, k):
                    act.wait_ge(gate_mm, n + (l * NBATCH + 5))
                    src = ps[:, k % 4, :].rearrange("p (t i) -> p t i", i=P)
                    act.copy(gates[:, :, bass.ds(t0, BT)].rearrange("p i t -> p t i"), src).then_inc(gate_stored, 1)

                gate_batches(act, gate_batch)

                def split_uT(j, k):
                    jj = j + l * NSTEP
                    for q in range(2):
                        act.wait_ge(uT_turned, jj * 2 + (q + 1))
                        act.copy(uT_hi[:, 4 * q:4 * q + 4, :].rearrange("p k e -> p (k e)"),
                                 ps[:, q, :]).then_inc(uThi_done, 1)

                split_uT(0, 0)

                def step(j, k):
                    jj = j + l * NSTEP
                    act.wait_ge(v_landed[k % 2], loads(l, j, k))
                    if l or k >= 2:
                        act.wait_ge(y_mm, jj - 1)
                    act.copy(v_hi[:, k % 2, :], v_raw[:, k % 2, :]).then_inc(vhi_done, 1)
                    act.wait_ge(act_mm, jj + 1)
                    if k < NSTEP - 1:
                        split_uT(j + 1, k + 1)
                    if l or k >= 2:
                        act.wait_ge(c_done, jj - 1)
                    act.activation(gel[:, k % 2, :], ps[:, 2 + k % 2, 0:T], ACT.Gelu).then_inc(gelu_done, 1)

                if l == 0:
                    for i in range(2):
                        act.wait_ge(mod_stored[i], 16 * (len(mod_order) // 2))
                expert_steps(act, None, None, step)

        @block_ctx.vector
        def _(dve):
            seq_ = Chain(dve, dve_step)
            asked = [0]

            def rsqrt(last):
                seq_(last, rsqrt_asked, wait=False)
                asked[0] += 1
                dve.wait_ge(rsqrt_done, asked[0])

            def take(name):
                return wait_full(dve, name)

            def give(ins, name):
                b, n = bank(name)
                ins.then_inc(free[b], 1)
                dve.wait_ge(free[b], n)

            tt, ts, stt = dve.tensor_tensor, dve.tensor_scalar, dve.scalar_tensor_tensor

            dve.wait_ge(consts_made, 1)
            dve.wait_ge(pos_landed, 16)
            seq_(dve.tensor_copy(posf[:, :], posi[:, :]))
            for s in range(2):
                for t in range(2):
                    seq_(ts(rope[:, s, t, :], invf[:, :], posf[:, t:t + 1], None, ALU.mult))
            MAGIC = 1.5 * 2.0 ** 23
            C1, C2 = 6.28125, float(np.float32(2 * np.pi - 6.28125).view(np.uint32) and 0.0019350051879882812)
            C3 = 2 * np.pi - C1 - C2
            for s in range(2):
                seq_(ts(ropek[:, s], rope[:, s], 1.0 / (2 * np.pi), 0.25 * s, ALU.mult, ALU.add))
            kf = ropek[:, :, :, :].rearrange("p s a f -> p (s a f)")
            af = rope[:, :, :, :].rearrange("p s a f -> p (s a f)")
            seq_(ts(kf, kf, MAGIC, None, ALU.add))
            seq_(ts(kf, kf, -MAGIC, None, ALU.add))
            for cst in (C1, C2, C3):
                seq_(stt(af, kf, -cst, af, ALU.mult, ALU.add))
            seq_(ts(rope[:, 1], rope[:, 1], float(np.pi / 2), None, ALU.add))
            seq_(ts(af, af, 3.1415925, -3.1415925, ALU.min, ALU.max), rope_args)
            dve.wait_ge(x_landed, 16)

            def rms_stats(src, t, width, junk=None):
                return dve.tensor_tensor_reduce(out=hb[:, t, 0:width] if junk is None else junk, in0=src, in1=src,
                                                scale=1.0 / width, scalar=NORM_EPS, op0=ALU.mult, op1=ALU.add,
                                                accum_out=rs[:, t:t + 1])

            def modulated(l, mod, ready, landed):
                seq_(rms_stats(xs[:, 0, :], 0, D))
                rsqrt(rms_stats(xs[:, 1, :], 1, D))
                dve.wait_ge(landed, 32 * (l + 1))
                seq_(ts(mod[:, 1, :], mod[:, 1, :], 1.0, None, ALU.add))
                for t in range(2):
                    seq_(stt(hb[:, t, :], xs[:, t, :], rs[:, t:t + 1], mod[:, 1, :], ALU.mult, ALU.mult))
                    seq_(tt(hb[:, t, :], hb[:, t, :], mod[:, 0, :], ALU.add), ready)

            def rotate(t, h0, nh):
                v = pjh[:, t, h0:h0 + nh, 0:ROT].rearrange("p h (s f) -> p h s f", s=2)
                pc = rt[:, 0, 0:nh * ROT].rearrange("p (h s f) -> p h s f", s=2, f=HALF)
                pn = rt[:, 1, 0:nh * ROT].rearrange("p (h s f) -> p h s f", s=2, f=HALF)

                def spread(k):
                    return rope[:, k, t, :].unsqueeze(1).unsqueeze(1).to_broadcast([P, nh, 2, HALF])
                seq_(tt(pc, v, spread(1), ALU.mult))
                seq_(tt(pn, v, spread(0), ALU.mult))
                seq_(tt(v[:, :, 0, :], pc[:, :, 0, :], pn[:, :, 1, :], ALU.subtract))
                return tt(v[:, :, 1, :], pc[:, :, 1, :], pn[:, :, 0, :], ALU.add)

            def tap(ct, i):
                o = acc[:, ct, :]
                if i == 0:
                    return ts(o, hc[:, ct, 0:T], cwT[:, ct, 0:1], cwT[:, ct, TAPS:TAPS + 1], ALU.mult, ALU.add)
                return stt(o, hc[:, ct, i:i + T], cwT[:, ct, i:i + 1], o, ALU.mult, ALU.add)

            def conv_pair(a, b):
                for i in range(TAPS - 1):
                    seq_.lag(tap(a, i))
                    seq_.lag(tap(b, i))
                seq_(tap(a, TAPS - 1), conv_ready)
                seq_.settle()
                seq_(tap(b, TAPS - 1), conv_ready)

            def index_scores(l, t):
                nk = P * (t + 1)
                sv = score[:, t, 0:nk]
                first = True
                for n, (tile, heads, _) in enumerate(DOTS):
                    if tile != t:
                        continue
                    dve.wait_ge(relu_ready, 6 * l + n + 1)
                    for i, h in enumerate(heads):
                        r = relu[:, n % 2, i * nk:(i + 1) * nk]
                        last = relu_used if h == heads[-1] else None
                        if first:
                            seq_(ts(sv, r, wis[:, t, h:h + 1], 0.0, ALU.mult, ALU.add), last)
                            first = False
                        else:
                            seq_(stt(sv, r, wis[:, t, h:h + 1], sv, ALU.mult, ALU.add), last)
                seq_(tt(score[:, t, nk - P:nk], score[:, t, nk - P:nk], tri[:, :], ALU.add))

            def select():
                ab = [[score[:, t, 0:P * (t + 1)], work[:, t, 0:P * (t + 1)]] for t in range(2)]
                for i in range(SEL // 8):
                    for t in range(2):
                        seq_.lag(dve.max(m8[:, t, :], ab[t][0]))
                    for t in range(2):
                        seq_.lag(dve.match_replace(ab[t][1], m8[:, t, :], ab[t][0], TAKEN))
                    for t in range(2):
                        ab[t].reverse()
                for t in range(2):
                    nk = P * (t + 1)
                    seq_.lag(ts(bias[:, t, 0:nk], ab[t][0], 0.5 * TAKEN, NEG, ALU.is_gt, ALU.mult))
                seq_.settle()
                for t in range(2):
                    nk = P * (t + 1)
                    seq_(tt(bias[:, t, nk - P:nk], bias[:, t, nk - P:nk], tri[:, :], ALU.add))

            for l in range(L):
                modulated(l, moda, h_ready, mod1_landed)
                def glu(n):
                    ct = CONV_ORDER[n]
                    name = ("cv", l, ct)
                    dve.wait_ge(sig_ready, CT * l + n + 1)
                    o = take(name)
                    give(tt(hc[:, ct, TAPS - 1:HCW], o[:, 0:T], sig[:, n % 2, :], ALU.mult), name)
                    dve.sem_inc(glu_done, 1)

                dve.wait_ge(cw_ready, l + 1)
                glu(0)
                glu(1)
                for i in range(TAPS):
                    if i == TAPS // 2:
                        glu(2)
                        glu(3)
                    seq_(tap(CONV_ORDER[1], i), conv_ready if i == TAPS - 1 else None)
                conv_pair(*CONV_ORDER[2:])

                dve.wait_ge(small_landed, 16 * 6 * (l + 1))
                dve.wait_ge(proj_ready, 10 * l + 4)
                for t in range(2):
                    seq_(dve.bn_stats(bn6[:, t, :], pjh[:, t, 32, :]))
                    seq_(dve.bn_aggr(mv[:, t, :], bn6[:, t, :]))
                rsqrt(ts(rs[:, 0:2], mv[:, :, 1], NORM_EPS, None, ALU.add))
                for t in range(2):
                    seq_(ts(pjh[:, t, 32, :], pjh[:, t, 32, :], mv[:, t, 0:1], rs[:, t:t + 1], ALU.subtract, ALU.mult))
                ki = pjh[:, :, 32, :]
                seq_(tt(ki, ki, gain_small[:, 2, :].unsqueeze(1).to_broadcast([P, 2, DH]), ALU.mult))
                seq_(tt(ki, ki, gain_small[:, 3, :].unsqueeze(1).to_broadcast([P, 2, DH]), ALU.add))
                if l == 0:
                    dve.wait_ge(rope_ready, 1)
                for t in range(2):
                    seq_(rotate(t, 24, NI + 1))
                    seq_(dve.tensor_copy(pjh[:, t, 33, :], pjh[:, t, 32, :]), idx_ready)
                dve.wait_ge(proj_ready, 10 * l + 8)
                for t in range(2):
                    sq = hb[:, t, :].rearrange("p (h d) -> p h d", d=DH)
                    seq_(tt(sq, pjh[:, t, 0:16, :], pjh[:, t, 0:16, :], ALU.mult))
                    seq_(dve.tensor_reduce(rs[:, 16 * t:16 * t + 16], sq, AX.X, ALU.add))
                rsqrt(ts(rs[:, 0:32], rs[:, 0:32], 1.0 / DH, NORM_EPS, ALU.mult, ALU.add))
                for t in range(2):
                    v = pjh[:, t, 0:16, :]
                    r = rs[:, 16 * t:16 * t + 16].unsqueeze(2).to_broadcast([P, 16, DH])
                    seq_(tt(v, v, r, ALU.mult))
                    v4 = pj[:, t, 0:2 * AW].rearrange("p (s h d) -> p s h d", s=2, d=DH)
                    g = gain_small[:, 0:2, :].unsqueeze(2).to_broadcast([P, 2, NH, DH])
                    seq_(tt(v4, v4, g, ALU.mult))
                    seq_(rotate(t, 0, 16), qk_ready)

                index_scores(l, 0)
                index_scores(l, 1)
                select()

                for t in range(2):
                    o = take(("cT", l, t))
                    seq_(dve.bn_stats(bn6[:, t, :], o))
                    seq_(dve.bn_aggr(mv[:, t, :], bn6[:, t, :]))
                rsqrt(ts(rs[:, 0:2], mv[:, :, 1], NORM_EPS, None, ALU.add))
                dve.wait_ge(out_gains_landed, 64 * (l + 1))
                for t in range(2):
                    name = ("cT", l, t)
                    o = take(name)
                    hv = hb[:, t, AW:D]
                    give(ts(hv, o, mv[:, t, 0:1], rs[:, t:t + 1], ALU.subtract, ALU.mult), name)
                    seq_(tt(hv, hv, ln_gb[:, 0, :], ALU.mult))
                    seq_(tt(hv, hv, ln_gb[:, 1, :], ALU.add), silu_in)
                for t in range(2):
                    dve.wait_ge(silu_done, 2 * l + t + 1)
                    ins = rms_stats(hb[:, t, AW:D], t, CW)
                    if t:
                        rsqrt(ins)
                    else:
                        seq_(ins)
                for t in range(2):
                    seq_(stt(hb[:, t, AW:D], hb[:, t, AW:D], rs[:, t:t + 1], out_g[:, AW:D], ALU.mult, ALU.mult))

                def logits(n):
                    t, heads, nk = DOTS[n]
                    nh = len(heads)
                    name = ("S", l, n)
                    o = take(name).rearrange("p (h k) -> p h k", h=nh)
                    if n >= 2:
                        dve.wait_ge(exp_ready, 6 * l + n - 1)
                    v = lg[:, n % 2, :].rearrange("p (h k) -> p h k", h=nh)
                    give(tt(v, o, bias[:, t, 0:nk].unsqueeze(1).to_broadcast([P, nh, nk]), ALU.add), name)
                    seq_(dve.tensor_reduce(gmx[:, n % 2, 0:nh], v, AX.X, ALU.max))
                    seq_(ts(negm[:, n % 2, 0:nh], gmx[:, n % 2, 0:nh], -float(DH) ** -0.5, None, ALU.mult), logits_ready)

                def attended(t):
                    dve.wait_ge(pv_full, 6 * l + (2 if t == 0 else 6))
                    seq_(dve.reciprocal(rinv[:, t, :], rsum[:, t, :]))
                    o = ps[:, 7, :].rearrange("p (h d) -> p h d", d=DH)
                    seq_(tt(hb[:, t, 0:AW].rearrange("p (h d) -> p h d", d=DH), o,
                            rinv[:, t, :].unsqueeze(2).to_broadcast([P, NH, DH]), ALU.mult), pv_free)

                def mix(t):
                    attended(t)
                    rsqrt(dve.tensor_tensor_reduce(out=xtmp[:, 0, :], in0=hb[:, t, 0:AW], in1=hb[:, t, 0:AW],
                                                   scale=1.0 / AW, scalar=NORM_EPS, op0=ALU.mult, op1=ALU.add,
                                                   accum_out=rs[:, 0:1]))
                    seq_(stt(hb[:, t, 0:AW], hb[:, t, 0:AW], rs[:, 0:1], out_g[:, 0:AW], ALU.mult, ALU.mult),
                         mixed_ready)

                def add_branch(t):
                    if t == 0:
                        dve.wait_ge(gate_landed, 16 * (2 * l + 1))
                    for blk in range(2):
                        cols = slice(blk * 512, blk * 512 + 512)
                        name = ("out", l, blk, t)
                        o = take(name)
                        give(tt(xtmp[:, blk, :], o, gmod[:, cols], ALU.mult), name)
                        seq_(tt(xs[:, t, cols], xs[:, t, cols], xtmp[:, blk, :], ALU.add))

                def second_norm(t):
                    if t == 0:
                        dve.wait_ge(mod2_landed, 32 * (l + 1))
                        seq_(ts(modb[:, 1, :], modb[:, 1, :], 1.0, None, ALU.add))
                    rsqrt(dve.tensor_tensor_reduce(out=hb[:, t, :], in0=xs[:, t, :], in1=xs[:, t, :],
                                                   scale=1.0 / D, scalar=NORM_EPS, op0=ALU.mult, op1=ALU.add,
                                                   accum_out=rs[:, 0:1]))
                    seq_(stt(hb[:, t, :], xs[:, t, :], rs[:, 0:1], modb[:, 1, :], ALU.mult, ALU.mult))
                    seq_(tt(hb[:, t, :], hb[:, t, :], modb[:, 0, :], ALU.add), h2_ready)

                for n in range(4):
                    logits(n)
                mix(0)
                logits(4)
                logits(5)
                add_branch(0)
                mix(1)
                second_norm(0)
                add_branch(1)
                second_norm(1)
                for t in range(2):
                    for q in range(2):
                        dve.wait_ge(h2T_ready, 4 * l + 2 * t + q + 1)
                        a = (slice(None), slice(4 * q, 4 * q + 4), slice(t * P, (t + 1) * P))
                        seq_(tt(h2lo[a], hT[a], h2hi[a].bitcast(F32), ALU.subtract), h2lo_done)

                def best16(rows):
                    for s, v, i, w in rows:
                        seq_.lag(dve.max(v[:, 0:8], s))
                    for s, v, i, w in rows:
                        seq_.lag(dve.max_index(i[:, 0:8], v[:, 0:8], s))
                    for s, v, i, w in rows:
                        seq_.lag(dve.match_replace(w, v[:, 0:8], s, TAKEN))
                    for s, v, i, w in rows:
                        seq_.lag(dve.max(v[:, 8:16], w))
                    for s, v, i, w in rows:
                        seq_.lag(dve.max_index(i[:, 8:16], v[:, 8:16], w))
                    seq_.settle()

                for blk in range(4):
                    for t in range(2):
                        dve.wait_ge(s_ready, 8 * l + 2 * blk + t + 1)
                        for i in (0, 2):
                            best16([(sc[:, t, 4 * blk + j, :], v1[:, t, j, :], i1u[:, j, :],
                                     work1[:, (j - i) * NK:(j - i + 1) * NK]) for j in (i, i + 1)])
                        for r in range(2):
                            seq_(dve.tensor_copy(i1f[:, t, r, 2 * blk:2 * blk + 2, :],
                                                 i1u[:, 0:4, :].rearrange("p (h s) k -> p h s k", s=2)[:, :, r, :]))
                        cd = cand[:, t * 1024:t * 1024 + 512].rearrange("p (h a b) -> p h a b", a=16, b=16)
                        v = v1[:, t, 0:4, :].rearrange("p (h s) k -> p h s k", s=2)
                        for h in range(2):
                            seq_(tt(cd[:, h], v[:, h, 0, :].unsqueeze(2).to_broadcast([P, 16, 16]),
                                    v[:, h, 1, :].unsqueeze(1).to_broadcast([P, 16, 16]), ALU.add))
                        best16([(cand[:, t * 1024 + h * 256:t * 1024 + h * 256 + 256], topv[:, t, 2 * blk + h, :],
                                 posu[:, t, 2 * blk + h, :], (work1, bias[:, 0, :])[h]) for h in range(2)])

                for t in range(2):
                    if l or t:
                        wait_full(dve, ("eT", l, t - 1) if t else ("eT", l - 1, 1))
                    g = seln[:, 2, :, :]
                    seq_(tt(g, topv[:, t], topv[:, t, :, 0:1].to_broadcast([P, HP, 16]), ALU.subtract), gexp_in)
                    pu = pab.bitcast(U32)[:, 0:128]
                    pf = pab[:, 128:256]
                    flatpos = posu[:, t].rearrange("p h k -> p (h k)")
                    for r in range(2):
                        if r == 0:
                            seq_(ts(pu, flatpos, 4, None, ALU.logical_shift_right))
                        else:
                            seq_(ts(pu, flatpos, 15, None, ALU.bitwise_and))
                        seq_(dve.tensor_copy(pf, pu))
                        e = eq.rearrange("p (m a) -> p m a", a=16)
                        seq_(tt(e, pf.unsqueeze(2).to_broadcast([P, 128, 16]),
                                iota[:, 0:16].unsqueeze(1).to_broadcast([P, 128, 16]), ALU.is_equal))
                        e4 = eq.rearrange("p (h k a) -> p h k a", h=HP, a=16)
                        seq_(tt(e4, e4, i1f[:, t, r].unsqueeze(2).to_broadcast([P, HP, 16, 16]), ALU.mult))
                        seq_(dve.tensor_reduce(seln[:, r, :, :].rearrange("p h k -> p (h k)"), e, AX.X, ALU.add))
                    dve.wait_ge(gexp_done, 2 * l + t + 1)
                    seq_(dve.tensor_reduce(rs[:, 0:HP], g, AX.X, ALU.add))
                    seq_(dve.reciprocal(rs[:, 8:16], rs[:, 0:HP]))
                    seq_(tt(g, g, rs[:, 8:16].unsqueeze(2).to_broadcast([P, HP, 16]), ALU.mult), sel_ready)

                dve.wait_ge(selT_ready, 2 * (l + 1))
                ramp = iota[:, :].unsqueeze(1).to_broadcast([P, BT, P])

                def gate_batch(n, t0, k):
                    dve.wait_ge(gate_mm, n + (l * NBATCH + 1))
                    for r in range(2):
                        e = selT[:, r, bass.ds(t0, BT)].unsqueeze(2).to_broadcast([P, BT, P])
                        ins = tt(hot_rows(k)[:, r], ramp, e, ALU.is_equal)
                        if r == 0:
                            ins.then_inc(hot_ready, 1)
                        else:
                            ins.then_inc(hot2_ready, 1)

                gate_batches(dve, gate_batch)

                def split_uT(j, k):
                    jj = j + l * NSTEP
                    for q in range(2):
                        dve.wait_ge(uThi_done, jj * 2 + (q + 1))
                        hi = uT_hi[:, 4 * q:4 * q + 4, :].rearrange("p k e -> p (k e)")
                        lo = uT_lo[:, 4 * q:4 * q + 4, :].rearrange("p k e -> p (k e)")
                        tt(lo, ps[:, q, :], hi.bitcast(F32), ALU.subtract).then_inc(uTlo_done, 1)

                split_uT(0, 0)

                def step(j, k):
                    jj = j + l * NSTEP
                    s = k % 2
                    dve.wait_ge(vhi_done, jj + 1)
                    tt(v_lo[:, s, :], v_raw[:, s, :], v_hi[:, s, :].bitcast(F32), ALU.subtract).then_inc(vlo_done, 1)
                    if k < NSTEP - 1:
                        split_uT(j + 1, k + 1)
                    dve.wait_ge(gelu_done, jj + 1)
                    seq_(tt(gel[:, s, :], gel[:, s, :], gates[:, j, :] if isinstance(j, int)
                            else gates[:, bass.ds(j, 1), :].rearrange("p a t -> p (a t)"), ALU.mult))
                    seq_(dve.tensor_copy(c_hi[:, s, :], gel[:, s, :]))
                    tt(c_lo[:, s, :], gel[:, s, :], c_hi[:, s, :].bitcast(F32), ALU.subtract).then_inc(c_done, 1)

                expert_steps(dve, seq_, {dve_step: 8}, step)

                dve.wait_ge(y_mm, NSTEP * (l + 1))
                dve.wait_ge(gate_landed, 32 * (l + 1))
                for t in range(2):
                    for q in range(2):
                        cols = slice(q * 512, q * 512 + 512)
                        gy = gel[:, :, :].rearrange("p a n -> p (a n)")
                        seq_(tt(gy, ps[:, 4 + 2 * t + q, :], gmod[:, cols], ALU.mult))
                        seq_(tt(xs[:, t, cols], xs[:, t, cols], gy, ALU.add), x_done if q else None)


CONV_ORDER = (2, 3, 0, 1)

POOL_TAPS = (19, 24)

DOTS = [(0, (0, 2, 4, 6), 128), (0, (1, 3, 5, 7), 128),
        (1, (0, 2), 256), (1, (4, 6), 256), (1, (1, 3), 256), (1, (5, 7), 256)]

_INS = ["x", "c", "positions", "w_ada", "b_ada", "w_in", "q_norm_g", "k_norm_g", "idx_k_ln_g",
        "idx_k_ln_b", "conv_dw", "conv_b", "conv_ln_g", "conv_ln_b", "out_g_attn", "out_g_conv",
        "w_out", "peer_wq", "peer_sub_keys", "peer_u", "peer_v"]


def kernel(**inputs):
    import concourse.bacc as bacc
    from concourse.bass_utils import run_bass_kernel_spmd

    nc = bacc.Bacc("TRN2", target_bir_lowering=False, num_devices=1)
    arrays, args = {}, {}
    for name in _INS:
        a = np.ascontiguousarray(inputs[name])
        arrays[f"in_{name}"] = a
        args[name] = nc.dram_tensor(f"in_{name}", a.shape, mybir.dt.from_np(a.dtype), kind="ExternalInput").ap()
    o = nc.dram_tensor("out_x", inputs["x"].shape, F32, kind="ExternalOutput").ap()
    trunk(nc, out=o, **args)
    r = run_bass_kernel_spmd(nc, [arrays], core_ids=[0])
    return r.results[0]["out_x"]
```

```python
from contextlib import ExitStack

import numpy as np

import concourse.bass as bass
from concourse import mybir

F32 = mybir.dt.float32
F32R = mybir.dt.float32r
BF16 = mybir.dt.bfloat16
I32 = mybir.dt.int32
U32 = mybir.dt.uint32
ALU = mybir.AluOpType
ACT = mybir.ActivationFunctionType
AX = mybir.AxisListType

P = 128
NORM_EPS = 1e-6
ROPE_THETA = 500000.0
PEER_TOPK = 16
NEG = -1.0e30
TAKEN = -3.0e38
RING = 7
WSLOTS = 3


class Chain:

    def __init__(self, eng, step_sem):
        self.eng, self.step_sem, self.count = eng, step_sem, {}
        self.i, self.per, self.start = None, {}, {}

    def lag(self, ins):
        self(ins, wait=False)
        if self.count[self.step_sem] > 1:
            self.eng.wait_ge(self.step_sem, self.count[self.step_sem] - 1)

    def settle(self):
        self.eng.wait_ge(self.step_sem, self.count[self.step_sem])

    def __call__(self, ins, sem=None, wait=True):
        s = self.step_sem if sem is None else sem
        n = self.count.get(s, 0) + 1
        self.count[s] = n
        ins.then_inc(s, 1)
        if wait:
            self.eng.wait_ge(s, n if self.i is None else n + self.i * self.per[s])

    def enter(self, i, per):
        self.i, self.per, self.start = i, per, dict(self.count)

    def leave(self, iterations):
        for s, n in self.per.items():
            assert self.count.get(s, 0) - self.start.get(s, 0) == n
            self.count[s] = self.start.get(s, 0) + n * iterations
        self.i = None


def plan(depth):
    seq = []

    def block(*name):
        seq.append(("block", name))

    def job(*name):
        seq.append(("job", name))

    def ada(items):
        for layer, blk in items:
            block("ada", layer, blk)
            job("ada", layer, blk)

    def out_tile(l, t):
        for q in range(2):
            job("mT", l, t, q)
        for b in range(2):
            job("out", l, b, t)

    for l in range(depth):
        more = l == 0 and depth > 1
        if l == 0:
            ada([(0, b) for b in range(4)])
        job("wT", l)
        for t in range(2):
            for q in range(2):
                job("hT", l, t, q)
        block("cu1", l)
        job("cv", l, 2)
        job("cv", l, 3)
        block("cu0", l)
        job("cv", l, 0)
        job("cv", l, 1)
        for name in ("qi", "ki", "q", "k", "v"):
            block(name, l)
            for t in range(2):
                job(name, l, t)
        job("iT", l, 0)
        job("iT", l, 1)
        job("kiT", l)
        for n in range(6):
            job("dot", l, n)
        for t in range(2):
            for name in ("qT", "kT"):
                job(name, l, t)
        for t in range(2):
            job("cT", l, t)
        job("S", l, 0)
        for n in range(6):
            for m in LOGITS_AHEAD[n]:
                job("S", l, m)
            if l == 0:
                ada(ADA_ATTENTION[n])
            job("PT", l, n)
            if n == 3:
                block("out", l, 0)
                block("out", l, 1)
                out_tile(l, 0)
        out_tile(l, 1)
        for q in range(2):
            job("h2T", l, 0, q)
        block("sk", l)
        for n in range(4):
            job("skT", l, n)
        for q in range(2):
            job("h2T", l, 1, q)
        mid = ADA_MID if l == 0 else [[], [], [], []]
        for b in range(4):
            block("wq", l, b)
            job("qp", l, b, 0)
            job("qp", l, b, 1)
            ada(mid[b] if more or l else [])
            if b:
                job("s", l, b - 1, 0)
                job("s", l, b - 1, 1)
        job("s", l, 3, 0)
        job("s", l, 3, 1)
        if more:
            ada(ADA_TAIL)
        job("eT", l, 0)
        job("eT", l, 1)
    return seq


CAND_ROWS = [(0, 0, 1, 16), (16, 1, 3, 8), (40, 4, 4, 4), (56, 8, 8, 1)]
NCAND = 64
EARLY = (8, 20)
LOGITS_AHEAD = [[1], [2], [3], [4, 5], [], []]
ADA_ATTENTION = [[(0, 4), (0, 5)], [(0, 6), (0, 7)], [(0, 8)], [(0, 9)], [], []]
ADA_MID = [[(0, 10)], [(0, 11), (1, 0)], [(1, 1), (1, 2)], [(1, 3)]]
ADA_TAIL = [(1, b) for b in range(4, 12)]


def trunk(nc, x, c, positions, w_ada, b_ada, w_in, q_norm_g, k_norm_g, idx_k_ln_g, idx_k_ln_b,
          conv_dw, conv_b, conv_ln_g, conv_ln_b, out_g_attn, out_g_conv, w_out, peer_wq,
          peer_sub_keys, peer_u, peer_v, out):
    _, T, D = x.shape
    L = w_ada.shape[0]
    DH = q_norm_g.shape[1]
    TAPS, CW = conv_dw.shape[1:]
    AW = out_g_attn.shape[1]
    NH = AW // DH
    NI = NH
    ROT = DH // 4
    HALF = ROT // 2
    KT = D // P
    CT = CW // P
    HP = peer_sub_keys.shape[1]
    NK = peer_sub_keys.shape[3]
    SEL = min(256, T // 4)
    CU0 = 3 * AW + NI * DH + DH + NI
    assert (T, D, NH, DH, CW, NK, HP) == (256, 1024, 8, 64, 512, 128, 8) and L == 2

    seq = plan(L)
    blocks = [n for kind, n in seq if kind == "block"]
    jobs = [n for kind, n in seq if kind == "job"]
    job_at = {n: i for i, n in enumerate(jobs)}
    block_at = {n: i for i, n in enumerate(blocks)}
    last_job, cur = {}, None
    for kind, n in seq:
        if kind == "block":
            cur = n
        elif n[0] == "out":
            last_job[("out", n[1], n[2])] = n
        elif cur is not None and (n[0] == cur[0] or (cur[0][:2] == "cu" and n[0] == "cv")
                                  or (cur[0], n[0]) in (("sk", "skT"), ("wq", "qp"))):
            last_job[cur] = n

    scratch = nc.dram_tensor("mod_rows", [L, 6 * D], F32, kind="Internal").ap()

    with ExitStack() as ctx:
        def sb(name, shape, dt=F32):
            return ctx.enter_context(nc.sbuf_tensor(name, shape, dt))

        def sem(name):
            return ctx.enter_context(nc.semaphore(name))

        xs = sb("xs", [P, 2, D])
        h2hi = sb("h2hi", [P, KT, T], F32R)
        h2lo = sb("h2lo", [P, KT, T], F32R)
        u_raw = sb("u_raw", [P, 2, D])
        v_raw = sb("v_raw", [P, 2, D])
        uT_hi = sb("uT_hi", [P, KT, P], F32R)
        uT_lo = sb("uT_lo", [P, KT, P], F32R)
        v_hi = sb("v_hi", [P, 2, D], F32R)
        v_lo = sb("v_lo", [P, 2, D], F32R)
        c_hi = sb("c_hi", [P, 2, T], F32R)
        c_lo = sb("c_lo", [P, 2, T], F32R)
        gel = sb("gel", [P, 2, T])
        ident = sb("ident", [P, P])
        iota = sb("iota", [P, P])
        row_start = sb("row_start", [P, 16])
        tri = sb("tri", [P, P])
        pickT = sb("pickT", [P, 2, T], BF16)
        gateT = sb("gateT", [P, T])
        ramp = sb("ramp", [P, NK, 4], BF16)
        bias = sb("bias", [P, 2, T])
        cwT = sb("cwT", [P, CT, TAPS + 1])
        gain_small = sb("gain_small", [P, 4, DH])
        rope = sb("rope", [P, 2, 2, HALF])
        ropek = sb("ropek", [P, 2, 2, HALF])
        invf = sb("invf", [P, HALF])
        posi = sb("posi", [P, 2], I32)
        posf = sb("posf", [P, 2])
        ccol = sb("ccol", [P, KT])
        cact = sb("cact", [P, KT])
        wis = sb("wis", [P, 2, NI])
        rs = sb("rs", [P, 32])
        neghalf = sb("neghalf", [P, 32])
        bn6 = sb("bn6", [P, 2, 6])
        mv = sb("mv", [P, 2, 2])
        m8 = sb("m8", [P, 2, 8])
        negm = sb("negm", [P, 2, 4])
        rsum = sb("rsum", [P, 2, NH])
        rinv = sb("rinv", [P, 2, NH])
        gmx = sb("gmx", [P, 2, 4])

        arena = sb("arena", [P, P * T])
        gates = arena[:, :].rearrange("p (i t) -> p i t", t=T)
        top = [0]

        def cut(n, at=None):
            a = top[0] if at is None else at
            if at is None:
                top[0] = a + n
            assert a + n <= P * T
            return arena[:, a:a + n]

        wring = cut(WSLOTS * 8 * 512).rearrange("p (s n) -> p s n", s=WSLOTS)
        MODA = top[0]
        moda = cut(2 * D).rearrange("p (a n) -> p a n", a=2)
        ln_gb = moda[:, 0, :].rearrange("p (a n) -> p a n", a=2)
        out_g = moda[:, 1, :]
        eq = cut(2 * D, MODA)
        GM0 = top[0]
        gmod = cut(D)
        HT0 = top[0]
        hT = cut(KT * T).rearrange("p (k t) -> p k t", k=KT)
        HB0 = top[0]
        hb = cut(2 * D).rearrange("p (a n) -> p a n", a=2)
        cand = cut(2 * D, HB0)
        P0 = top[0]
        PW = 34 * DH
        pj = cut(2 * PW).rearrange("p (a n) -> p a n", a=2)
        pjh = pj.rearrange("p a (h d) -> p a h d", d=DH)
        sc = cut(2 * 16 * NK, P0).rearrange("p (a g n) -> p a g n", a=2, g=16)
        QK0 = top[0]
        qT = cut(4 * T).rearrange("p (j t) -> p j t", j=4)
        kT = cut(4 * T).rearrange("p (j t) -> p j t", j=4)
        qiT = cut(4 * T).rearrange("p (j t) -> p j t", j=4)
        kiT = cut(T)
        xtmp = qiT.rearrange("p j t -> p (j t)").rearrange("p (b n) -> p b n", b=2)
        skT = cut(16 * NK, QK0).rearrange("p (g n) -> p g n", g=16)
        CV0 = top[0]
        HCW = TAPS - 1 + T
        hc = cut(CT * HCW).rearrange("p (j t) -> p j t", j=CT)
        acc = cut(CT * T).rearrange("p (j t) -> p j t", j=CT)
        modb = cut(2 * D, CV0).rearrange("p (a n) -> p a n", a=2)
        AT0 = top[0]
        lg = cut(2 * 512).rearrange("p (b n) -> p b n", b=2)
        ex = cut(2 * 512).rearrange("p (b n) -> p b n", b=2)
        pt = cut(2 * 512).rearrange("p (b n) -> p b n", b=2)
        cw_raw = cut(CW, AT0)
        relu = lg
        score = ex[:, 0, :].rearrange("p (t n) -> p t n", t=2)
        work = ex[:, 1, :].rearrange("p (t n) -> p t n", t=2)
        tap_tmp = gmod.rearrange("p (b n) -> p b n", b=2)
        rt = pt[:, 0, :].rearrange("p (b n) -> p b n", b=2)
        sig = pt[:, 1, :].rearrange("p (b n) -> p b n", b=2)
        qpT = cut(16 * T, CV0).rearrange("p (g t) -> p g t", g=16)
        TK0 = CV0 + 16 * T
        v1 = cut(256, TK0).rearrange("p (a g k) -> p a g k", a=2, g=8)
        i1u = cut(256, TK0 + 256).bitcast(U32).rearrange("p (g k) -> p g k", k=16)
        work1 = cut(256, TK0 + 512)
        i1f = cut(512, GM0).rearrange("p (a r h k) -> p a r h k", a=2, r=2, h=HP)
        topv = cut(256, TK0 + 768).rearrange("p (a h k) -> p a h k", a=2, h=HP)
        posu = cut(256, TK0 + 1024).bitcast(U32).rearrange("p (a h k) -> p a h k", a=2, h=HP)
        seln = cut(768, TK0).rearrange("p (a r h k) -> p a r h k", a=2, r=3, h=HP)

        ps = ctx.enter_context(nc.psum_tensor("ps", [P, 8, 512], F32))

        full = [sem(f"bank{b}_full") for b in range(RING)]
        free = [sem(f"bank{b}_free") for b in range(RING)]
        w_in_slot = [sem(f"weights_landed{s}") for s in range(WSLOTS)]
        x_landed = sem("x_landed")
        c_landed = sem("c_landed")
        pos_landed = sem("pos_landed")
        small_landed = sem("small_landed")
        consts_made = sem("consts_made")
        pool_step = sem("pool_step")
        dve_step = sem("dve_step")
        act_step = sem("act_step")
        cact_made = sem("cact_made")
        mod_stored = [sem(f"mod_stored{i}") for i in range(2)]
        mod1_landed = sem("mod1_landed")
        out_gains_landed = sem("out_gains_landed")
        gate_landed = sem("gate_landed")
        mod2_landed = sem("mod2_landed")
        rsqrt_asked = sem("rsqrt_asked")
        rsqrt_done = sem("rsqrt_done")
        rope_ready = sem("rope_ready")
        rope_args = sem("rope_args")
        cw_ready = sem("cw_ready")
        h_ready = sem("h_ready")
        hT_ready = sem("hT_ready")
        proj_ready = sem("proj_ready")
        idx_ready = sem("idx_ready")
        idxT_ready = sem("idxT_ready")
        sig_ready = sem("sig_ready")
        glu_done = sem("glu_done")
        exp_part = sem("exp_part")
        act_hi = sem("act_hi")
        h2lo_done = sem("h2lo_done")
        relu_ready = sem("relu_ready")
        relu_used = sem("relu_used")
        conv_ready = sem("conv_ready")
        conv_pool = sem("conv_pool")
        qk_ready = sem("qk_ready")
        qkT_ready = sem("qkT_ready")
        logits_ready = sem("logits_ready")
        exp_ready = sem("exp_ready")
        ptT_ready = sem("ptT_ready")
        pv_full = sem("pv_full")
        pv_free = sem("pv_free")
        silu_in = sem("silu_in")
        silu_done = sem("silu_done")
        mixed_ready = sem("mixed_ready")
        mixedT_ready = sem("mixedT_ready")
        xmid_ready = sem("xmid_ready")
        skT_ready = sem("skT_ready")
        h2_ready = sem("h2_ready")
        h2T_ready = sem("h2T_ready")
        qpT_ready = sem("qpT_ready")
        s_ready = sem("s_ready")
        gexp_in = sem("gexp_in")
        gexp_done = sem("gexp_done")
        sel_ready = sem("sel_ready")
        selT_ready = sem("selT_ready")
        hot_ready = sem("hot_ready")
        hot2_ready = sem("hot2_ready")
        hot2_cast = sem("hot2_cast")
        gated = sem("gated")
        gate_mm = sem("gate_mm")
        gate_stored = sem("gate_stored")
        gate_scaled = sem("gate_scaled")
        u_landed = [sem(f"u_landed{s}") for s in range(2)]
        v_landed = [sem(f"v_landed{s}") for s in range(2)]
        uT_turned = sem("uT_turned")
        uThi_done = sem("uThi_done")
        uTlo_done = sem("uTlo_done")
        uT_copied = sem("uT_copied")
        vhi_done = sem("vhi_done")
        vlo_done = sem("vlo_done")
        act_mm = sem("act_mm")
        gelu_done = sem("gelu_done")
        c_done = sem("c_done")
        y_mm = sem("y_mm")
        x_done = sem("x_done")
        out_stored = sem("out_stored")

        def bank(name):
            n = job_at[name]
            return n % RING, n // RING + 1

        def wait_full(eng, name):
            b, n = bank(name)
            eng.wait_ge(full[b], n)
            return ps[:, b, :]

        cand_start = [at + (a - a0) * nb for at, a0, na, nb in CAND_ROWS for a in range(a0, a0 + na)]

        mod_order = [(n[1], n[2]) for n in blocks if n[0] == "ada"]
        BT = 4
        NBATCH = T // BT
        NSTEP = NK

        def tile_steps(eng, chain, per, step, first, last):
            step(first, first)
            step(first + 1, first + 1)
            with eng.Fori(0, (last - first - 4) // 4) as i:
                if chain is not None:
                    chain.enter(i, per)
                for u in range(4):
                    step(i * 4 + (first + 2 + u), first + 2 + u)
                if chain is not None:
                    chain.leave((last - first - 4) // 4)
            step(last - 2, last - 2)
            step(last - 1, last - 1)

        def early_steps(eng, l, step):
            for k in range(4):
                step(k, k)
            if EARLY[l] > 8:
                with eng.Fori(0, EARLY[l] // 4 - 2) as i:
                    for u in range(4):
                        step(i * 4 + (4 + u), 4 + u)
            for k in range(EARLY[l] - 4, EARLY[l]):
                step(k, k)

        def brow(n):
            s = n % WSLOTS
            return v_raw[0:1, s // 2, (s % 2) * 512:(s % 2) * 512 + 512]

        def stage(m):
            return gel[:, m % 2, 0:P]

        def loads(l, j, k):
            if isinstance(j, int):
                return 16 * ((l * NSTEP + j) // 2 + 1)
            return (j - k % 2) * 8 + 16 * (l * NSTEP // 2 + 1)

        scaled_before = [NBATCH * sum(e > 0 for e in EARLY[:l]) for l in range(L)]
        early_before = [sum(EARLY[:l]) for l in range(L)]

        def early_uT(buf, k, q):
            return buf[:, k % 2, q * 512:q * 512 + 512]

        def hot_rows(k):
            raw = (u_raw, v_raw)[k % 4 // 2]
            return raw[:, k % 2, :].rearrange("p (r t i) -> p r t i", r=2, t=BT)

        def hot_picks(k):
            return (gel, bias)[k % 2].rearrange("p a t -> p (a t)").bitcast(BF16).rearrange(
                "p (r i t) -> p r i t", r=2, t=BT)

        def lagged_batches(eng, ahead, after, lag):
            for k in range(lag):
                ahead(k, k * BT, k)
            with eng.Fori(0, NBATCH // 8 - 1) as i:
                for k in range(8):
                    ahead(i * 8 + (k + lag), i * (8 * BT) + (k + lag) * BT, k + lag)
                    after(i * 8 + k, i * (8 * BT) + k * BT, k)
            for k in range(NBATCH - 8, NBATCH):
                if k + lag < NBATCH:
                    ahead(k + lag, (k + lag) * BT, k + lag)
                after(k, k * BT, k)

        def gate_batches(eng, batch):
            with eng.Fori(0, NBATCH // 8) as i:
                for k in range(8):
                    batch(i * 8 + k, i * (8 * BT) + k * BT, k)

        block_ctx = ctx.enter_context(nc.Block())

        @block_ctx.sync
        def _(sp):
            sp.dma_start(ccol[:, :], c[0, :].rearrange("(p k) -> p k", k=KT)).then_inc(c_landed, 16)
            sp.dma_start(xs[:, :, :], x[0].rearrange("(a p) d -> p a d", p=P)).then_inc(x_landed, 16)

            def load_block(n):
                name = blocks[n]
                slot = n % WSLOTS
                if n >= WSLOTS:
                    b, k = bank(last_job[blocks[n - WSLOTS]])
                    sp.wait_ge(full[b], k)
                w = wring[:, slot, :].rearrange("p (k n) -> p k n", k=KT)
                l = name[1]
                got = w_in_slot[slot]
                win = w_in[l].rearrange("(k p) n -> p k n", p=P)
                if name[0] == "ada":
                    src = w_ada[l].rearrange("(p k) n -> p k n", k=KT)[:, :, name[2] * 512:name[2] * 512 + 512]
                    sp.dma_start(w, src).then_inc(got, 16)
                    sp.dma_start(brow(n), b_ada[l:l + 1, name[2] * 512:name[2] * 512 + 512]).then_inc(got, 16)
                    return
                if name[0] in ("q", "k", "v", "qi"):
                    a = {"q": 0, "k": 1, "v": 2, "qi": 3}[name[0]] * AW
                    pieces = [(w, win[:, :, a:a + 512])]
                elif name[0] == "ki":
                    pieces = [(w[:, :, 0:DH + NI], win[:, :, 4 * AW:CU0])]
                elif name[0] in ("cu0", "cu1"):
                    a = CU0 + 256 * int(name[0][2])
                    pieces = [(w[:, :, 0:256], win[:, :, a:a + 256]),
                              (w[:, :, 256:512], win[:, :, a + CW:a + CW + 256])]
                elif name[0] == "out":
                    pieces = [(w, w_out[l].rearrange("(k p) n -> p k n", p=P)[:, :, name[2] * 512:name[2] * 512 + 512])]
                elif name[0] == "wq":
                    pieces = [(w, peer_wq[l].rearrange("(k p) n -> p k n", p=P)[:, :, name[2] * 512:name[2] * 512 + 512])]
                else:
                    pieces = [(wring[:, slot, 0:16 * NK].rearrange("p (g n) -> p g n", g=16),
                               peer_sub_keys[l].rearrange("h s n k -> n (h s) k"))]
                for dst, src in pieces:
                    sp.dma_start(dst, src).then_inc(got, 16)

            n = 0
            for l in range(L):
                while n < len(blocks) and (blocks[n][1] == l or blocks[n][0] == "ada"):
                    if l and n == block_at[("cu1", l)]:
                        sp.wait_ge(c_done, l * NSTEP)
                    load_block(n)
                    n += 1

                def load_u(j, k):
                    if l or k >= 2:
                        sp.wait_ge(uT_turned, (j + l * NSTEP) * 2 - 2)
                    sp.dma_start(u_raw[:, k % 2, :],
                                 peer_u[l, bass.ds(j * P, P), :]).then_inc(u_landed[k % 2], 16)

                def load_v(j, k):
                    if l or k >= 2:
                        sp.wait_ge(vlo_done, j + (l * NSTEP - 1))
                    sp.dma_start(v_raw[:, k % 2, :],
                                 peer_v[l, bass.ds(j * P, P), :]).then_inc(v_landed[k % 2], 16)

                def load_experts(j, k):
                    if k != early or not early:
                        load_u(j, k)
                    load_v(j, k)

                early = EARLY[l]
                if early:
                    early_steps(sp, l, load_u)
                sp.wait_ge(gate_mm, (l + 1) * NBATCH + 4)
                if early:
                    load_u(early, early)
                    tile_steps(sp, None, None, load_v, 0, early)
                tile_steps(sp, None, None, load_experts, early, NSTEP)
            sp.wait_ge(x_done, 2 * L)
            sp.dma_start(out[0].rearrange("(a p) d -> p a d", p=P), xs[:, :, :]).then_inc(out_stored, 16)
            sp.wait_ge(out_stored, 16)

        @block_ctx.gpsimd
        def _(pool):
            seq_ = Chain(pool, pool_step)
            seq_(pool.memset(ident[:, :], 0.0))
            seq_(pool.affine_select(out=ident[:, :], in_=ident[:, :], compare_op=ALU.not_equal, fill=1.0,
                                    base=0, pattern=[[-1, P]], channel_multiplier=1))
            seq_(pool.iota(iota[:, :], [[1, P]], base=0, channel_multiplier=0,
                           allow_small_or_imprecise_dtypes=True))
            seq_(pool.memset(tri[:, :], 0.0))
            seq_(pool.affine_select(out=tri[:, :], in_=tri[:, :], compare_op=ALU.is_ge, fill=NEG,
                                    base=0, pattern=[[-1, P]], channel_multiplier=1))
            seq_(pool.memset(neghalf[:, :], -0.5))
            inv_freq = np.power(np.float32(ROPE_THETA), -np.arange(0, ROT, 2, dtype=np.float32) / ROT)
            for i, f in enumerate(inv_freq):
                seq_(pool.memset(invf[:, i:i + 1], float(f)))
            for i, first in enumerate(cand_start):
                seq_(pool.memset(row_start[:, i:i + 1], float(first)))
            seq_(pool.memset(hc[:, :, 0:TAPS - 1], 0.0))
            seq_(pool.memset(rs[:, :], 1.0), consts_made)
            pool.dma_start(posi[:, :], positions[0, :].rearrange("(a p) -> p a", p=P),
                           allow_slow_non_contiguous=True).then_inc(pos_landed, 16)

            asked = 0

            def rsqrt(width):
                nonlocal asked
                asked += 1
                pool.wait_ge(rsqrt_asked, asked)
                pool.tensor_tensor(rs[:, 0:width], rs[:, 0:width], neghalf[:, 0:width],
                                   ALU.pow).then_inc(rsqrt_done, 1)

            def mod_rows(l, first, last):
                m = mod_order.index((l, last))
                for i in range(2):
                    pool.wait_ge(mod_stored[i], 16 * ((m - i) // 2 + 1))

            def spread(dst, src, landed):
                pool.dma_start(dst, src).then_inc(landed, 16)

            for l in range(L):
                if l:
                    pool.wait_ge(c_done, l * NSTEP)
                    seq_(pool.memset(hc[:, :, 0:TAPS - 1], 0.0), consts_made)
                for i, g in enumerate((q_norm_g, k_norm_g, idx_k_ln_g, idx_k_ln_b)):
                    spread(gain_small[:, i, :], g[l, :].partition_broadcast(P), small_landed)
                spread(cw_raw[0:TAPS, :], conv_dw[l], small_landed)
                spread(cw_raw[TAPS:TAPS + 1, :], conv_b[l:l + 1, :], small_landed)
                mod_rows(l, 0, 3)
                if l:
                    pool.wait_ge(x_done, 2 * l)
                for i in range(2):
                    spread(moda[:, i, :], scratch[l, i * D:(i + 1) * D].partition_broadcast(P), mod1_landed)
                rsqrt(2)
                pool.wait_ge(h_ready, 2 * (l + 1))
                spread(ln_gb[:, 0, :], conv_ln_g[l, :].partition_broadcast(P), out_gains_landed)
                spread(ln_gb[:, 1, :], conv_ln_b[l, :].partition_broadcast(P), out_gains_landed)
                spread(out_g[:, 0:AW], out_g_attn[l, :].partition_broadcast(P), out_gains_landed)
                spread(out_g[:, AW:D], out_g_conv[l, :].partition_broadcast(P), out_gains_landed)
                ct = CONV_ORDER[0]
                pool.wait_ge(cw_ready, l + 1)
                pool.wait_ge(glu_done, CT * l + 1)
                o = acc[:, ct, :]
                seq_(pool.tensor_scalar(o, hc[:, ct, 0:T], cwT[:, ct, 0:1], cwT[:, ct, TAPS:TAPS + 1],
                                        ALU.mult, ALU.add))
                for i in range(1, TAPS):
                    p = tap_tmp[:, i % 2, 0:T]
                    seq_(pool.tensor_scalar(p, hc[:, ct, i:i + T], cwT[:, ct, i:i + 1], None, ALU.mult))
                    seq_(pool.tensor_tensor(o, o, p, ALU.add), conv_pool if i == TAPS - 1 else None)
                    if i == POOL_TAPS[0]:
                        rsqrt(2)
                    if i == POOL_TAPS[1]:
                        rsqrt(32)
                rsqrt(2)
                rsqrt(2)
                mod_rows(l, 4, 5)
                spread(gmod, scratch[l, 2 * D:3 * D].partition_broadcast(P), gate_landed)
                for t in range(2):
                    wait_full(pool, ("cT", l, t))
                mod_rows(l, 6, 9)
                for i in range(2):
                    spread(modb[:, i, :], scratch[l, (3 + i) * D:(4 + i) * D].partition_broadcast(P), mod2_landed)
                for t in range(2):
                    rsqrt(1)
                for t in range(2):
                    rsqrt(1)

                def early_lo(j, k):
                    jj = j + l * NSTEP
                    for q in range(2):
                        pool.wait_ge(uT_copied, j * 2 + (2 * early_before[l] + q + 1))
                        pool.tensor_tensor(early_uT(v_lo, k, q), early_uT(v_raw, k, q),
                                           early_uT(v_hi, k, q).bitcast(F32),
                                           ALU.subtract).then_inc(uTlo_done, 1)

                if EARLY[l]:
                    early_steps(pool, l, early_lo)

                if l == 0:
                    pool.sem_inc(gated, 2)

                def gate_batch(n, t0, k):
                    pool.wait_ge(hot_ready, n + (l * NBATCH + 1))
                    pool.wait_ge(gate_mm, n + (l * NBATCH + 1))
                    g = gateT[:, bass.ds(t0, BT)].unsqueeze(2).to_broadcast([P, BT, P])
                    pool.tensor_tensor(hot_rows(k)[:, 0], hot_picks(k)[:, 0].rearrange("p i t -> p t i"), g,
                                       ALU.mult).then_inc(gated, 1)

                gate_batches(pool, gate_batch)
                mod_rows(l, 10, 11)
                pool.wait_ge(c_done, (l + 1) * NSTEP)
                spread(gmod, scratch[l, 5 * D:6 * D].partition_broadcast(P), gate_landed)

        @block_ctx.tensor
        def _(pe):
            done = [0]
            state = {"block": -1}

            def next_is(kind, name):
                assert seq[done[0]] == (kind, name), (seq[done[0]], name)
                done[0] += 1

            landed_count = [0] * WSLOTS

            def use_block(*name):
                next_is("block", name)
                n = block_at[name]
                slot = n % WSLOTS
                landed_count[slot] += 2 if name[0] in ("ada", "cu0", "cu1") else 1
                pe.wait_ge(w_in_slot[slot], 16 * landed_count[slot])
                state["block"] = n
                return wring[:, slot, :].rearrange("p (k n) -> p k n", k=KT)

            def open_job(*name):
                next_is("job", name)
                b, n = bank(name)
                if n > 1:
                    pe.wait_ge(free[b], n - 1)
                return b, ps[:, b, :]

            def mm_all(o, pairs):
                for i, (a, b) in enumerate(pairs):
                    ins = pe.matmul(o, a, b, start=i == 0, stop=i == len(pairs) - 1)
                return ins

            def ada(layer, blk):
                w = use_block("ada", layer, blk)
                b, o = open_job("ada", layer, blk)
                for k in range(KT + 1):
                    for q in range(4):
                        cols = slice(q * P, (q + 1) * P)
                        if k < KT:
                            lhs, rhs = cact[:, k:k + 1].to_broadcast([P, 32]), w[:, k, cols]
                        else:
                            lhs, rhs = ident[0:1, 0:1].to_broadcast([1, 32]), brow(state["block"])[:, cols]
                        ins = pe.matmul(o[32 * q:32 * q + 32, 0:P], lhs, rhs, start=k == 0, stop=k == KT)
                ins.then_inc(full[b], 1)

            def turn4(name, srcs, width=P):
                b, o = open_job(*name)
                for i, s in enumerate(srcs):
                    n = s.shape[0]
                    ins = pe.transpose(o[:, i * n:(i + 1) * n], s, ident[0:n, 0:n])
                ins.then_inc(full[b], 1)

            def proj(w, name, lhs, width):
                b, o = open_job(*name)
                mm_all(o[:, 0:width], [(lhs[:, k, :], w[:, k, 0:width]) for k in range(KT)]).then_inc(full[b], 1)

            pe.wait_ge(consts_made, 1)
            pe.wait_ge(cact_made, 1)
            for blk in range(4):
                ada(0, blk)
            for l in range(L):
                if l:
                    pe.wait_ge(x_done, 2 * l)
                pe.wait_ge(small_landed, 16 * 6 * (l + 1))
                turn4(("wT", l), [cw_raw[0:TAPS + 1, j * P:(j + 1) * P] for j in range(CT)])
                for t in range(2):
                    pe.wait_ge(h_ready, 2 * l + t + 1)
                    for q in range(2):
                        turn4(("hT", l, t, q), [hb[:, t, (4 * q + i) * P:(4 * q + i + 1) * P] for i in range(4)])
                pe.wait_ge(hT_ready, 4 * (l + 1))
                def conv_proj(w, ct):
                    b, o = open_job("cv", l, ct)
                    for s in range(2):
                        col = s * 256 + (ct % 2) * P
                        ins = mm_all(o[:, s * T:(s + 1) * T],
                                     [(w[:, k, col:col + P], hT[:, k, :]) for k in range(KT)])
                    ins.then_inc(full[b], 1)

                for name, ct in (("cu1", 2), ("cu0", 0)):
                    w = use_block(name, l)
                    conv_proj(w, ct)
                    conv_proj(w, ct + 1)

                def token_proj(name, width=512):
                    w = use_block(name, l)
                    for t in range(2):
                        proj(w, (name, l, t), hT[:, :, t * P:(t + 1) * P], width)

                token_proj("qi")
                token_proj("ki", DH + NI)
                token_proj("q")
                token_proj("k")
                token_proj("v")
                for t in range(2):
                    pe.wait_ge(idx_ready, 2 * l + t + 1)
                    turn4(("iT", l, t), [pj[:, t, (12 + i) * P:(13 + i) * P] for i in range(4)])
                turn4(("kiT", l), [pj[:, t, 16 * P:17 * P] for t in range(2)])
                pe.wait_ge(idxT_ready, 3 * (l + 1))
                for n in range(6):
                    t, heads, nk = DOTS[n]
                    b, o = open_job("dot", l, n)
                    for i, h in enumerate(heads):
                        r = (h % 2) * DH
                        ins = pe.matmul(o[:, i * nk:(i + 1) * nk], qiT[r:r + DH, h // 2, t * P:(t + 1) * P],
                                        kiT[r:r + DH, 0:nk], start=True, stop=True)
                    ins.then_inc(full[b], 1)
                for t in range(2):
                    pe.wait_ge(qk_ready, 2 * l + t + 1)
                    turn4(("qT", l, t), [pj[:, t, i * P:(i + 1) * P] for i in range(4)])
                    turn4(("kT", l, t), [pj[:, t, (4 + i) * P:(5 + i) * P] for i in range(4)])
                pe.wait_ge(conv_ready, (CT - 1) * (l + 1))
                pe.wait_ge(conv_pool, l + 1)
                for t in range(2):
                    turn4(("cT", l, t), [acc[:, j, t * P:(t + 1) * P] for j in range(CT)])

                pe.wait_ge(qkT_ready, 4 * (l + 1))

                def logits(n):
                    t, heads, nk = DOTS[n]
                    b, o = open_job("S", l, n)
                    for i, h in enumerate(heads):
                        r = (h % 2) * DH
                        ins = pe.matmul(o[:, i * nk:(i + 1) * nk], qT[r:r + DH, h // 2, t * P:(t + 1) * P],
                                        kT[r:r + DH, h // 2, 0:nk], start=True, stop=True)
                    ins.then_inc(full[b], 1)

                def values(n):
                    t, heads, nk = DOTS[n]
                    pe.wait_ge(ptT_ready, 6 * l + n + 1)
                    if heads[0] == 0 and (l or t):
                        pe.wait_ge(pv_free, 2 * l + t)
                    for i, h in enumerate(heads):
                        for kb in range(nk // P):
                            ins = pe.matmul(ps[:, 7, h * DH:(h + 1) * DH],
                                            pt[:, n % 2, (i * (nk // P) + kb) * P:(i * (nk // P) + kb + 1) * P],
                                            pjh[:, kb, 16 + h, :], start=kb == 0, stop=kb == nk // P - 1)
                    ins.then_inc(pv_full, 1)

                pe.wait_ge(proj_ready, 10 * (l + 1))
                logits(0)
                w_out_blocks = []

                def out_tile(t):
                    pe.wait_ge(mixed_ready, 2 * l + t + 1)
                    for q in range(2):
                        turn4(("mT", l, t, q), [hb[:, t, (4 * q + i) * P:(4 * q + i + 1) * P] for i in range(4)])
                    pe.wait_ge(mixedT_ready, 4 * l + 2 * (t + 1))
                    for blk in range(2):
                        proj(w_out_blocks[blk], ("out", l, blk, t), hT[:, :, t * P:(t + 1) * P], 512)

                def turn_h2(t):
                    pe.wait_ge(h2_ready, 2 * l + t + 1)
                    for q in range(2):
                        turn4(("h2T", l, t, q), [hb[:, t, (4 * q + i) * P:(4 * q + i + 1) * P] for i in range(4)])

                for n in range(6):
                    for m in LOGITS_AHEAD[n]:
                        logits(m)
                    if n:
                        values(n - 1)
                    if l == 0:
                        for a in ADA_ATTENTION[n]:
                            ada(*a)
                    pe.wait_ge(exp_ready, 6 * l + n + 1)
                    turn4(("PT", l, n), [ex[:, n % 2, i * P:(i + 1) * P] for i in range(4)])
                    if n == 3:
                        for blk in range(2):
                            w_out_blocks.append(use_block("out", l, blk))
                        out_tile(0)
                values(5)
                out_tile(1)
                turn_h2(0)
                use_block("sk", l)
                raw = wring[:, block_at[("sk", l)] % WSLOTS, 0:16 * NK].rearrange("p (g n) -> p g n", g=16)
                for n in range(4):
                    turn4(("skT", l, n), [raw[:, 4 * n + i, :] for i in range(4)])
                turn_h2(1)
                pe.wait_ge(h2T_ready, 4 * (l + 1))
                pe.wait_ge(skT_ready, 4 * (l + 1))

                def subkeys(blk):
                    pe.wait_ge(qpT_ready, 2 * (4 * l + blk + 1))
                    for t in range(2):
                        b, o = open_job("s", l, blk, t)
                        for i in range(4):
                            g = 4 * blk + i
                            ins = pe.matmul(o[:, i * NK:(i + 1) * NK], qpT[:, g, t * P:(t + 1) * P], skT[:, g, :],
                                            start=True, stop=True)
                        ins.then_inc(full[b], 1)

                for blk in range(4):
                    w = use_block("wq", l, blk)
                    for s in range(2):
                        b, o = open_job("qp", l, blk, s)
                        for i in range(2):
                            col = (2 * s + i) * P
                            ins = mm_all(o[:, i * T:(i + 1) * T],
                                         [(w[:, k, col:col + P], hT[:, k, :]) for k in range(KT)])
                        ins.then_inc(full[b], 1)
                    if l == 0:
                        for a in ADA_MID[blk]:
                            ada(*a)
                    if blk:
                        subkeys(blk - 1)
                subkeys(3)
                if l == 0:
                    for a in ADA_TAIL:
                        ada(*a)
                if EARLY[l]:
                    def ring_consumed(name):
                        for m in jobs[:job_at[name] + 1][-RING:]:
                            b, n = bank(m)
                            pe.wait_ge(free[b], n)

                    def early_turn(j, k):
                        pe.wait_ge(u_landed[k % 2], loads(l, j, k))
                        for q in range(2):
                            for i in range(4):
                                d = 4 * q + i
                                ins = pe.transpose(ps[:, 2 * (k % 2) + q, i * P:(i + 1) * P],
                                                   u_raw[:, k % 2, d * P:(d + 1) * P], ident[:, :])
                            ins.then_inc(uT_turned, 1)

                    def early_activations(j, k):
                        jj = j + l * NSTEP
                        if l or k >= 2:
                            pe.wait_ge(gelu_done, jj - 1)
                        o = ps[:, 4 + k % 2, 0:T]
                        for q in range(2):
                            pe.wait_ge(uTlo_done, jj * 2 + (q + 1))
                            hi = early_uT(v_hi, k, q).rearrange("p (d e) -> p d e", e=P)
                            lo = early_uT(v_lo, k, q).rearrange("p (d e) -> p d e", e=P)
                            for i in range(4):
                                d = 4 * q + i
                                pe.matmul(o, hi[:, i], h2hi[:, d, :], start=d == 0, stop=False)
                                pe.matmul(o, hi[:, i], h2lo[:, d, :], start=False, stop=False)
                                ins = pe.matmul(o, lo[:, i], h2hi[:, d, :], start=False, stop=d == KT - 1)
                        ins.then_inc(act_mm, 1)

                    ring_consumed(jobs[job_at[("eT", l, 0)] - 1])
                    pe.wait_ge(h2lo_done, 4 * (l + 1))
                    early_turn(0, 0)
                    early_turn(1, 1)

                    def early_step(j, k):
                        early_activations(j, k)
                        if k < EARLY[l] - 2:
                            early_turn(j + 2, k + 2)

                    early_steps(pe, l, early_step)
                    pe.wait_ge(gelu_done, l * NSTEP + EARLY[l])
                for t in range(2):
                    pe.wait_ge(sel_ready, 2 * l + t + 1)
                    b, o = open_job("eT", l, t)
                    for i in range(3):
                        ins = pe.transpose(o[:, i * P:(i + 1) * P], seln[:, t, i, :, :].rearrange("p h k -> p (h k)"),
                                           ident[:, :])
                    ins.then_inc(full[b], 1)

                last_jobs = jobs[:job_at[("eT", l, 1)] + 1][-RING:]
                for name in last_jobs:
                    b, n = bank(name)
                    pe.wait_ge(free[b], n)

                if l == 0:
                    pe.sem_inc(gate_mm, 4)

                def gate_batch(n, t0, k):
                    pe.wait_ge(gated, n + (l * NBATCH + 3))
                    pe.wait_ge(hot2_cast, n + (l * NBATCH + 3))
                    pe.wait_ge(gate_stored, n + (l * NBATCH + 1))
                    if EARLY[l]:
                        pe.wait_ge(gate_scaled, n + (scaled_before[l] + 1))
                    hot = hot_rows(k)
                    for t in range(BT):
                        ins = pe.matmul(ps[:, k % 4, t * P:(t + 1) * P], hot[:, 1, t, :], hot[:, 0, t, :],
                                        start=True, stop=True)
                    ins.then_inc(gate_mm, 1)

                gate_batches(pe, gate_batch)

                def turn(j, k):
                    pe.wait_ge(u_landed[k % 2], loads(l, j, k))
                    for q in range(2):
                        for i in range(4):
                            d = 4 * q + i
                            ins = pe.transpose(ps[:, q, i * P:(i + 1) * P], u_raw[:, k % 2, d * P:(d + 1) * P],
                                               ident[:, :])
                        ins.then_inc(uT_turned, 1)

                def activations(j, k):
                    jj = j + l * NSTEP
                    pe.wait_ge(uThi_done, jj * 2 + 2)
                    pe.wait_ge(uTlo_done, jj * 2 + 2)
                    o = ps[:, 2 + k % 2, 0:T]
                    for d in range(KT):
                        pe.matmul(o, uT_hi[:, d, :], h2hi[:, d, :], start=d == 0, stop=False)
                        pe.matmul(o, uT_hi[:, d, :], h2lo[:, d, :], start=False, stop=False)
                        ins = pe.matmul(o, uT_lo[:, d, :], h2hi[:, d, :], start=False, stop=d == KT - 1)
                    ins.then_inc(act_mm, 1)

                def outputs(j, k):
                    jj = j + l * NSTEP
                    pe.wait_ge(c_done, jj + 1)
                    pe.wait_ge(vlo_done, jj + 1)
                    s = k % 2
                    for t in range(2):
                        for q in range(2):
                            o = ps[:, 4 + 2 * t + q, :]
                            ts, qs = slice(t * P, (t + 1) * P), slice(q * 512, (q + 1) * 512)
                            pe.matmul(o, c_hi[:, s, ts], v_hi[:, s, qs], start=k == 0, stop=False)
                            pe.matmul(o, c_hi[:, s, ts], v_lo[:, s, qs], start=False, stop=False)
                            ins = pe.matmul(o, c_lo[:, s, ts], v_hi[:, s, qs], start=False, stop=k == NSTEP - 1)
                    ins.then_inc(y_mm, 1)

                pe.wait_ge(h2lo_done, 4 * (l + 1))
                pe.wait_ge(gate_stored, NBATCH * (l + 1) + 4)
                early = EARLY[l]
                if early:
                    pe.wait_ge(gate_scaled, scaled_before[l] + NBATCH + 4)
                turn(early, early)

                def step(j, k):
                    activations(j, k)
                    if k < NSTEP - 1:
                        turn(j + 1, k + 1)
                    if k > 0:
                        outputs(j - 1, k - 1)

                def early_outputs(j, k):
                    if k < early - 1:
                        outputs(j, k)

                if early:
                    tile_steps(pe, None, None, early_outputs, 0, early)
                tile_steps(pe, None, None, step, early, NSTEP)
                outputs(NSTEP - 1, NSTEP - 1)
            assert done[0] == len(seq)

        @block_ctx.scalar
        def _(act):
            seq_ = Chain(act, act_step)

            n_mod = [0]

            def ada(layer, blk):
                m = n_mod[0]
                n_mod[0] += 1
                name = ("ada", layer, blk)
                o = wait_full(act, name)
                b, n = bank(name)
                if m >= 2:
                    act.wait_ge(mod_stored[m % 2], 16 * (m // 2))
                act.copy(stage(m), o[:, 0:P]).then_inc(free[b], 1)
                act.wait_ge(free[b], n)
                act.dma_start(scratch[layer, blk * 512:blk * 512 + 512].rearrange("(q n) -> q n", q=4),
                              stage(m)[0:P:32, :]).then_inc(mod_stored[m % 2], 16)

            act.wait_ge(c_landed, 16)
            act.activation(cact[:, :], ccol[:, :], ACT.Silu).then_inc(cact_made, 1)
            act.wait_ge(rope_args, 1)
            flat = rope[:, :, :, :].rearrange("p s a f -> p (s a f)")
            act.activation(flat, flat, ACT.Sin).then_inc(rope_ready, 1)
            for blk in range(4):
                ada(0, blk)

            for l in range(L):
                def evac(name, dst, sem_done, scale=None, src=None):
                    o = wait_full(act, name)
                    b, n = bank(name)
                    s = o if src is None else src(o)
                    ins = act.copy(dst, s) if scale is None else act.mul(dst, s, scale)
                    ins.then_inc(free[b], 1)
                    act.wait_ge(free[b], n)
                    act.sem_inc(sem_done, 1)

                def four(o):
                    return o.rearrange("p (k t) -> p k t", k=4)

                evac(("wT", l), cwT[:, :, :].rearrange("p j t -> p (j t)"), cw_ready,
                     src=lambda o: o[:, 0:CT * (TAPS + 1)])
                for t in range(2):
                    for q in range(2):
                        evac(("hT", l, t, q), hT[:, 4 * q:4 * q + 4, t * P:(t + 1) * P], hT_ready, src=four)
                def sigmoid(n, ct):
                    o = wait_full(act, ("cv", l, ct))
                    if CT * l + n >= 2:
                        act.wait_ge(glu_done, CT * l + n - 1)
                    act.activation(sig[:, n % 2, :], o[:, T:2 * T], ACT.Sigmoid).then_inc(sig_ready, 1)

                for n, ct in enumerate(CONV_ORDER):
                    sigmoid(n, ct)
                for t in range(2):
                    evac(("qi", l, t), pj[:, t, 3 * AW:4 * AW], proj_ready)
                for t in range(2):
                    o = wait_full(act, ("ki", l, t))
                    seq_(act.mul(wis[:, t, :], o[:, DH:DH + NI], float(NI) ** -0.5), wait=False)
                    evac(("ki", l, t), pjh[:, t, 32, :], proj_ready, src=lambda o: o[:, 0:DH])
                for i, name in enumerate(("q", "k", "v")):
                    for t in range(2):
                        evac((name, l, t), pj[:, t, i * AW:(i + 1) * AW], proj_ready)
                for t in range(2):
                    evac(("iT", l, t), qiT[:, :, t * P:(t + 1) * P], idxT_ready, src=four)
                evac(("kiT", l), kiT, idxT_ready, src=lambda o: o[:, 0:T])
                for n in range(6):
                    name = ("dot", l, n)
                    o = wait_full(act, name)
                    b, k = bank(name)
                    if n >= 2:
                        act.wait_ge(relu_used, 6 * l + n - 1)
                    act.activation(relu[:, n % 2, :], o, ACT.Relu, scale=float(DH) ** -0.5).then_inc(free[b], 1)
                    act.wait_ge(free[b], k)
                    act.sem_inc(relu_ready, 1)
                for t in range(2):
                    evac(("qT", l, t), qT[:, :, t * P:(t + 1) * P], qkT_ready, src=four)
                    evac(("kT", l, t), kT[:, :, t * P:(t + 1) * P], qkT_ready, src=four)
                for t in range(2):
                    act.wait_ge(silu_in, 2 * l + t + 1)
                    act.activation(hb[:, t, AW:D], hb[:, t, AW:D], ACT.Silu).then_inc(silu_done, 1)
                def take_mixed(t):
                    for q in range(2):
                        evac(("mT", l, t, q), hT[:, 4 * q:4 * q + 4, t * P:(t + 1) * P], mixedT_ready, src=four)

                def take_h2(t):
                    for q in range(2):
                        o = wait_full(act, ("h2T", l, t, q))
                        act.copy(h2hi[:, 4 * q:4 * q + 4, t * P:(t + 1) * P], four(o)).then_inc(act_hi, 1)
                        act.wait_ge(act_hi, 4 * l + 2 * t + q + 1)
                        evac(("h2T", l, t, q), hT[:, 4 * q:4 * q + 4, t * P:(t + 1) * P], h2T_ready, src=four)

                for n in range(6):
                    t, heads, nk = DOTS[n]
                    act.wait_ge(logits_ready, 6 * l + n + 1)
                    if n >= 2:
                        wait_full(act, ("PT", l, n - 2))
                    for i, h in enumerate(heads):
                        ins = act.activation(ex[:, n % 2, i * nk:(i + 1) * nk], lg[:, n % 2, i * nk:(i + 1) * nk],
                                             ACT.Exp, bias=negm[:, n % 2, i:i + 1], scale=float(DH) ** -0.5,
                                             accum_out=rsum[:, t, h:h + 1])
                        seq_(ins, sem=exp_part, wait=h == heads[-1])
                    act.sem_inc(exp_ready, 1)
                    if l == 0:
                        for a in ADA_ATTENTION[n]:
                            ada(*a)
                    if n >= 2:
                        act.wait_ge(pv_full, 6 * l + n - 1)
                    evac(("PT", l, n), pt[:, n % 2, :], ptT_ready)
                    if n == 3:
                        take_mixed(0)
                take_mixed(1)
                take_h2(0)
                for n in range(4):
                    evac(("skT", l, n), skT[:, 4 * n:4 * n + 4, :].rearrange("p g n -> p (g n)"), skT_ready)
                take_h2(1)

                def scores(blk):
                    for t in range(2):
                        evac(("s", l, blk, t), sc[:, t, 4 * blk:4 * blk + 4, :].rearrange("p g n -> p (g n)"), s_ready)

                for blk in range(4):
                    for s in range(2):
                        g = 4 * blk + 2 * s
                        evac(("qp", l, blk, s), qpT[:, g:g + 2, :].rearrange("p g t -> p (g t)"), qpT_ready)
                    if l == 0:
                        for a in ADA_MID[blk]:
                            ada(*a)
                    if blk:
                        scores(blk - 1)
                scores(3)
                if l == 0:
                    for a in ADA_TAIL:
                        ada(*a)
                if EARLY[l]:
                    def early_split(j, k):
                        for q in range(2):
                            act.wait_ge(uT_turned, (j + l * NSTEP) * 2 + (q + 1))
                            src = ps[:, 2 * (k % 2) + q, :]
                            act.copy(early_uT(v_hi, k, q), src).then_inc(uThi_done, 1)
                            act.copy(early_uT(v_raw, k, q), src).then_inc(uT_copied, 1)

                    if l:
                        act.wait_ge(y_mm, l * NSTEP)
                    early_split(0, 0)
                    early_split(1, 1)

                    def early_step(j, k):
                        act.wait_ge(act_mm, j + (l * NSTEP + 1))
                        row = gates[:, j, :] if isinstance(j, int) else \
                            gates[:, bass.ds(j, 1), :].rearrange("p a t -> p (a t)")
                        act.activation(row, ps[:, 4 + k % 2, 0:T], ACT.Gelu).then_inc(gelu_done, 1)
                        if k < EARLY[l] - 2:
                            early_split(j + 2, k + 2)

                    early_steps(act, l, early_step)
                for t in range(2):
                    act.wait_ge(gexp_in, 2 * l + t + 1)
                    g = seln[:, t, 2, :, :].rearrange("p h k -> p (h k)")
                    act.activation(g, g, ACT.Exp).then_inc(gexp_done, 1)
                    o = wait_full(act, ("eT", l, t))
                    seq_(act.copy(gateT[:, t * P:(t + 1) * P], o[:, 2 * P:3 * P]), wait=False)
                    evac(("eT", l, t), pickT[:, :, t * P:(t + 1) * P], selT_ready,
                         src=lambda o: o[:, 0:2 * P].rearrange("p (a t) -> p a t", a=2))
                seq_.settle()

                if l == 0:
                    act.sem_inc(gate_stored, 4)

                    act.sem_inc(hot2_cast, 2)

                def hot2_batch(n, t0, k):
                    act.wait_ge(hot2_ready, n + (l * NBATCH + 1))
                    act.wait_ge(gate_mm, n + (l * NBATCH + 1))
                    act.copy(hot_rows(k)[:, 1], hot_picks(k)[:, 1].rearrange("p i t -> p t i")).then_inc(hot2_cast, 1)

                def gate_batch(n, t0, k):
                    act.wait_ge(gate_mm, n + (l * NBATCH + 5))
                    src = ps[:, k % 4, :].rearrange("p (t i) -> p t i", i=P)[:, :, EARLY[l]:P]
                    act.copy(gates[:, EARLY[l]:P, bass.ds(t0, BT)].rearrange("p i t -> p t i"),
                             src).then_inc(gate_stored, 1)

                lagged_batches(act, hot2_batch, gate_batch, 2)

                def split_uT(j, k):
                    jj = j + l * NSTEP
                    for q in range(2):
                        act.wait_ge(uT_turned, jj * 2 + (q + 1))
                        act.copy(uT_hi[:, 4 * q:4 * q + 4, :].rearrange("p k e -> p (k e)"),
                                 ps[:, q, :]).then_inc(uThi_done, 1)

                split_uT(EARLY[l], EARLY[l])

                def split_v(j, k):
                    act.wait_ge(v_landed[k % 2], loads(l, j, k))
                    if l or k >= 2:
                        act.wait_ge(y_mm, j + (l * NSTEP - 1))
                    act.copy(v_hi[:, k % 2, :], v_raw[:, k % 2, :]).then_inc(vhi_done, 1)

                def step(j, k):
                    jj = j + l * NSTEP
                    split_v(j, k)
                    act.wait_ge(act_mm, jj + 1)
                    if k < NSTEP - 1:
                        split_uT(j + 1, k + 1)
                    if l or k >= 2:
                        act.wait_ge(c_done, jj - 1)
                    act.activation(gel[:, k % 2, :], ps[:, 2 + k % 2, 0:T], ACT.Gelu).then_inc(gelu_done, 1)

                if l == 0:
                    for i in range(2):
                        act.wait_ge(mod_stored[i], 16 * (len(mod_order) // 2))
                if EARLY[l]:
                    tile_steps(act, None, None, split_v, 0, EARLY[l])
                tile_steps(act, None, None, step, EARLY[l], NSTEP)

        @block_ctx.vector
        def _(dve):
            seq_ = Chain(dve, dve_step)
            asked = [0]

            def rsqrt(last):
                seq_(last, rsqrt_asked, wait=False)
                asked[0] += 1
                dve.wait_ge(rsqrt_done, asked[0])

            def take(name):
                return wait_full(dve, name)

            def give(ins, name):
                b, n = bank(name)
                ins.then_inc(free[b], 1)
                dve.wait_ge(free[b], n)

            tt, ts, stt = dve.tensor_tensor, dve.tensor_scalar, dve.scalar_tensor_tensor

            dve.wait_ge(consts_made, 1)
            seq_(dve.tensor_copy(ramp[:, :, :], iota[:, :].unsqueeze(2).to_broadcast([P, NK, 4])))

            dve.wait_ge(pos_landed, 16)
            seq_(dve.tensor_copy(posf[:, :], posi[:, :]))
            for s in range(2):
                for t in range(2):
                    seq_(ts(rope[:, s, t, :], invf[:, :], posf[:, t:t + 1], None, ALU.mult))
            MAGIC = 1.5 * 2.0 ** 23
            C1, C2 = 6.28125, 0.0019350051879882812
            C3 = 2 * np.pi - C1 - C2
            for s in range(2):
                seq_(ts(ropek[:, s], rope[:, s], 1.0 / (2 * np.pi), 0.25 * s, ALU.mult, ALU.add))
            kf = ropek[:, :, :, :].rearrange("p s a f -> p (s a f)")
            af = rope[:, :, :, :].rearrange("p s a f -> p (s a f)")
            seq_(ts(kf, kf, MAGIC, None, ALU.add))
            seq_(ts(kf, kf, -MAGIC, None, ALU.add))
            for cst in (C1, C2, C3):
                seq_(stt(af, kf, -cst, af, ALU.mult, ALU.add))
            seq_(ts(rope[:, 1], rope[:, 1], float(np.pi / 2), None, ALU.add))
            seq_(ts(af, af, 3.1415925, -3.1415925, ALU.min, ALU.max), rope_args)
            dve.wait_ge(x_landed, 16)

            def rms_stats(src, t, width, junk=None):
                return dve.tensor_tensor_reduce(out=hb[:, t, 0:width] if junk is None else junk, in0=src, in1=src,
                                                scale=1.0 / width, scalar=NORM_EPS, op0=ALU.mult, op1=ALU.add,
                                                accum_out=rs[:, t:t + 1])

            def modulated(l, mod, ready, landed):
                seq_(rms_stats(xs[:, 0, :], 0, D))
                rsqrt(rms_stats(xs[:, 1, :], 1, D))
                dve.wait_ge(landed, 32 * (l + 1))
                seq_(ts(mod[:, 1, :], mod[:, 1, :], 1.0, None, ALU.add))
                for t in range(2):
                    seq_(stt(hb[:, t, :], xs[:, t, :], rs[:, t:t + 1], mod[:, 1, :], ALU.mult, ALU.mult))
                    seq_(tt(hb[:, t, :], hb[:, t, :], mod[:, 0, :], ALU.add), ready)

            def rotate(t, h0, nh):
                v = pjh[:, t, h0:h0 + nh, 0:ROT].rearrange("p h (s f) -> p h s f", s=2)
                pc = rt[:, 0, 0:nh * ROT].rearrange("p (h s f) -> p h s f", s=2, f=HALF)
                pn = rt[:, 1, 0:nh * ROT].rearrange("p (h s f) -> p h s f", s=2, f=HALF)

                def spread(k):
                    return rope[:, k, t, :].unsqueeze(1).unsqueeze(1).to_broadcast([P, nh, 2, HALF])
                seq_(tt(pc, v, spread(1), ALU.mult))
                seq_(tt(pn, v, spread(0), ALU.mult))
                seq_(tt(v[:, :, 0, :], pc[:, :, 0, :], pn[:, :, 1, :], ALU.subtract))
                return tt(v[:, :, 1, :], pc[:, :, 1, :], pn[:, :, 0, :], ALU.add)

            def tap(ct, i):
                o = acc[:, ct, :]
                if i == 0:
                    return ts(o, hc[:, ct, 0:T], cwT[:, ct, 0:1], cwT[:, ct, TAPS:TAPS + 1], ALU.mult, ALU.add)
                return stt(o, hc[:, ct, i:i + T], cwT[:, ct, i:i + 1], o, ALU.mult, ALU.add)

            def conv_pair(a, b):
                for i in range(TAPS - 1):
                    seq_.lag(tap(a, i))
                    seq_.lag(tap(b, i))
                seq_(tap(a, TAPS - 1), conv_ready)
                seq_.settle()
                seq_(tap(b, TAPS - 1), conv_ready)

            def index_scores(l, t):
                nk = P * (t + 1)
                sv = score[:, t, 0:nk]
                first = True
                for n, (tile, heads, _) in enumerate(DOTS):
                    if tile != t:
                        continue
                    dve.wait_ge(relu_ready, 6 * l + n + 1)
                    for i, h in enumerate(heads):
                        r = relu[:, n % 2, i * nk:(i + 1) * nk]
                        last = relu_used if h == heads[-1] else None
                        if first:
                            seq_(ts(sv, r, wis[:, t, h:h + 1], 0.0, ALU.mult, ALU.add), last)
                            first = False
                        else:
                            seq_(stt(sv, r, wis[:, t, h:h + 1], sv, ALU.mult, ALU.add), last)
                seq_(tt(score[:, t, nk - P:nk], score[:, t, nk - P:nk], tri[:, :], ALU.add))

            def select():
                ab = [[score[:, t, 0:P * (t + 1)], work[:, t, 0:P * (t + 1)]] for t in range(2)]
                for i in range(SEL // 8):
                    for t in range(2):
                        seq_.lag(dve.max(m8[:, t, :], ab[t][0]))
                    for t in range(2):
                        seq_.lag(dve.match_replace(ab[t][1], m8[:, t, :], ab[t][0], TAKEN))
                    for t in range(2):
                        ab[t].reverse()
                for t in range(2):
                    nk = P * (t + 1)
                    seq_.lag(ts(bias[:, t, 0:nk], ab[t][0], 0.5 * TAKEN, NEG, ALU.is_gt, ALU.mult))
                seq_.settle()
                for t in range(2):
                    nk = P * (t + 1)
                    seq_(tt(bias[:, t, nk - P:nk], bias[:, t, nk - P:nk], tri[:, :], ALU.add))

            for l in range(L):
                modulated(l, moda, h_ready, mod1_landed)
                def glu(n):
                    ct = CONV_ORDER[n]
                    name = ("cv", l, ct)
                    dve.wait_ge(sig_ready, CT * l + n + 1)
                    o = take(name)
                    give(tt(hc[:, ct, TAPS - 1:HCW], o[:, 0:T], sig[:, n % 2, :], ALU.mult), name)
                    dve.sem_inc(glu_done, 1)

                dve.wait_ge(cw_ready, l + 1)
                glu(0)
                glu(1)
                for i in range(TAPS):
                    if i == TAPS // 2:
                        glu(2)
                        glu(3)
                    seq_(tap(CONV_ORDER[1], i), conv_ready if i == TAPS - 1 else None)
                conv_pair(*CONV_ORDER[2:])

                dve.wait_ge(small_landed, 16 * 6 * (l + 1))
                dve.wait_ge(proj_ready, 10 * l + 4)
                for t in range(2):
                    seq_(dve.bn_stats(bn6[:, t, :], pjh[:, t, 32, :]))
                    seq_(dve.bn_aggr(mv[:, t, :], bn6[:, t, :]))
                rsqrt(ts(rs[:, 0:2], mv[:, :, 1], NORM_EPS, None, ALU.add))
                for t in range(2):
                    seq_(ts(pjh[:, t, 32, :], pjh[:, t, 32, :], mv[:, t, 0:1], rs[:, t:t + 1], ALU.subtract, ALU.mult))
                ki = pjh[:, :, 32, :]
                seq_(tt(ki, ki, gain_small[:, 2, :].unsqueeze(1).to_broadcast([P, 2, DH]), ALU.mult))
                seq_(tt(ki, ki, gain_small[:, 3, :].unsqueeze(1).to_broadcast([P, 2, DH]), ALU.add))
                if l == 0:
                    dve.wait_ge(rope_ready, 1)
                for t in range(2):
                    seq_(rotate(t, 24, NI + 1))
                    seq_(dve.tensor_copy(pjh[:, t, 33, :], pjh[:, t, 32, :]), idx_ready)
                dve.wait_ge(proj_ready, 10 * l + 8)
                for t in range(2):
                    sq = hb[:, t, :].rearrange("p (h d) -> p h d", d=DH)
                    seq_(tt(sq, pjh[:, t, 0:16, :], pjh[:, t, 0:16, :], ALU.mult))
                    seq_(dve.tensor_reduce(rs[:, 16 * t:16 * t + 16], sq, AX.X, ALU.add))
                rsqrt(ts(rs[:, 0:32], rs[:, 0:32], 1.0 / DH, NORM_EPS, ALU.mult, ALU.add))
                for t in range(2):
                    v = pjh[:, t, 0:16, :]
                    r = rs[:, 16 * t:16 * t + 16].unsqueeze(2).to_broadcast([P, 16, DH])
                    seq_(tt(v, v, r, ALU.mult))
                    v4 = pj[:, t, 0:2 * AW].rearrange("p (s h d) -> p s h d", s=2, d=DH)
                    g = gain_small[:, 0:2, :].unsqueeze(2).to_broadcast([P, 2, NH, DH])
                    seq_(tt(v4, v4, g, ALU.mult))
                    seq_(rotate(t, 0, 16), qk_ready)

                index_scores(l, 0)
                index_scores(l, 1)
                select()

                for t in range(2):
                    o = take(("cT", l, t))
                    seq_(dve.bn_stats(bn6[:, t, :], o))
                    seq_(dve.bn_aggr(mv[:, t, :], bn6[:, t, :]))
                rsqrt(ts(rs[:, 0:2], mv[:, :, 1], NORM_EPS, None, ALU.add))
                dve.wait_ge(out_gains_landed, 64 * (l + 1))
                for t in range(2):
                    name = ("cT", l, t)
                    o = take(name)
                    hv = hb[:, t, AW:D]
                    give(ts(hv, o, mv[:, t, 0:1], rs[:, t:t + 1], ALU.subtract, ALU.mult), name)
                    seq_(tt(hv, hv, ln_gb[:, 0, :], ALU.mult))
                    seq_(tt(hv, hv, ln_gb[:, 1, :], ALU.add), silu_in)
                for t in range(2):
                    dve.wait_ge(silu_done, 2 * l + t + 1)
                    ins = rms_stats(hb[:, t, AW:D], t, CW)
                    if t:
                        rsqrt(ins)
                    else:
                        seq_(ins)
                for t in range(2):
                    seq_(stt(hb[:, t, AW:D], hb[:, t, AW:D], rs[:, t:t + 1], out_g[:, AW:D], ALU.mult, ALU.mult))

                def logits(n):
                    t, heads, nk = DOTS[n]
                    nh = len(heads)
                    name = ("S", l, n)
                    o = take(name).rearrange("p (h k) -> p h k", h=nh)
                    if n >= 2:
                        dve.wait_ge(exp_ready, 6 * l + n - 1)
                    v = lg[:, n % 2, :].rearrange("p (h k) -> p h k", h=nh)
                    give(tt(v, o, bias[:, t, 0:nk].unsqueeze(1).to_broadcast([P, nh, nk]), ALU.add), name)
                    seq_(dve.tensor_reduce(gmx[:, n % 2, 0:nh], v, AX.X, ALU.max))
                    seq_(ts(negm[:, n % 2, 0:nh], gmx[:, n % 2, 0:nh], -float(DH) ** -0.5, None, ALU.mult), logits_ready)

                def attended(t):
                    dve.wait_ge(pv_full, 6 * l + (2 if t == 0 else 6))
                    seq_(dve.reciprocal(rinv[:, t, :], rsum[:, t, :]))
                    o = ps[:, 7, :].rearrange("p (h d) -> p h d", d=DH)
                    seq_(tt(hb[:, t, 0:AW].rearrange("p (h d) -> p h d", d=DH), o,
                            rinv[:, t, :].unsqueeze(2).to_broadcast([P, NH, DH]), ALU.mult), pv_free)

                def mix(t):
                    attended(t)
                    rsqrt(dve.tensor_tensor_reduce(out=xtmp[:, 0, :], in0=hb[:, t, 0:AW], in1=hb[:, t, 0:AW],
                                                   scale=1.0 / AW, scalar=NORM_EPS, op0=ALU.mult, op1=ALU.add,
                                                   accum_out=rs[:, 0:1]))
                    seq_(stt(hb[:, t, 0:AW], hb[:, t, 0:AW], rs[:, 0:1], out_g[:, 0:AW], ALU.mult, ALU.mult),
                         mixed_ready)

                def add_branch(t):
                    if t == 0:
                        dve.wait_ge(gate_landed, 16 * (2 * l + 1))
                    for blk in range(2):
                        cols = slice(blk * 512, blk * 512 + 512)
                        name = ("out", l, blk, t)
                        o = take(name)
                        give(tt(xtmp[:, blk, :], o, gmod[:, cols], ALU.mult), name)
                        seq_(tt(xs[:, t, cols], xs[:, t, cols], xtmp[:, blk, :], ALU.add))

                def second_norm(t):
                    if t == 0:
                        dve.wait_ge(mod2_landed, 32 * (l + 1))
                        seq_(ts(modb[:, 1, :], modb[:, 1, :], 1.0, None, ALU.add))
                    rsqrt(dve.tensor_tensor_reduce(out=hb[:, t, :], in0=xs[:, t, :], in1=xs[:, t, :],
                                                   scale=1.0 / D, scalar=NORM_EPS, op0=ALU.mult, op1=ALU.add,
                                                   accum_out=rs[:, 0:1]))
                    seq_(stt(hb[:, t, :], xs[:, t, :], rs[:, 0:1], modb[:, 1, :], ALU.mult, ALU.mult))
                    seq_(tt(hb[:, t, :], hb[:, t, :], modb[:, 0, :], ALU.add), h2_ready)

                for n in range(4):
                    logits(n)
                mix(0)
                logits(4)
                logits(5)
                add_branch(0)
                mix(1)
                second_norm(0)
                add_branch(1)
                second_norm(1)
                for t in range(2):
                    for q in range(2):
                        dve.wait_ge(h2T_ready, 4 * l + 2 * t + q + 1)
                        a = (slice(None), slice(4 * q, 4 * q + 4), slice(t * P, (t + 1) * P))
                        seq_(tt(h2lo[a], hT[a], h2hi[a].bitcast(F32), ALU.subtract), h2lo_done)

                def best16(rows):
                    for s, v, i, w in rows:
                        seq_.lag(dve.max(v[:, 0:8], s))
                    for s, v, i, w in rows:
                        seq_.lag(dve.max_index(i[:, 0:8], v[:, 0:8], s))
                    for s, v, i, w in rows:
                        seq_.lag(dve.match_replace(w, v[:, 0:8], s, TAKEN))
                    for s, v, i, w in rows:
                        seq_.lag(dve.max(v[:, 8:16], w))
                    for s, v, i, w in rows:
                        seq_.lag(dve.max_index(i[:, 8:16], v[:, 8:16], w))
                    seq_.settle()

                for blk in range(4):
                    for t in range(2):
                        dve.wait_ge(s_ready, 8 * l + 2 * blk + t + 1)
                        for i in (0, 2):
                            best16([(sc[:, t, 4 * blk + j, :], v1[:, t, j, :], i1u[:, j, :],
                                     work1[:, (j - i) * NK:(j - i + 1) * NK]) for j in (i, i + 1)])
                        for r in range(2):
                            seq_(dve.tensor_copy(i1f[:, t, r, 2 * blk:2 * blk + 2, :],
                                                 i1u[:, 0:4, :].rearrange("p (h s) k -> p h s k", s=2)[:, :, r, :]))
                        cd = cand[:, t * D:t * D + 2 * NCAND].rearrange("p (h n) -> p h n", h=2)
                        v = v1[:, t, 0:4, :].rearrange("p (h s) k -> p h s k", s=2)
                        for at, a0, na, nb in CAND_ROWS:
                            for h in range(2):
                                seq_.lag(tt(cd[:, h, at:at + na * nb].rearrange("p (a b) -> p a b", b=nb),
                                            v[:, h, 0, a0:a0 + na].unsqueeze(2).to_broadcast([P, na, nb]),
                                            v[:, h, 1, 0:nb].unsqueeze(1).to_broadcast([P, na, nb]), ALU.add))
                        seq_.settle()
                        best16([(cd[:, h, :], topv[:, t, 2 * blk + h, :], posu[:, t, 2 * blk + h, :],
                                 work1[:, h * NCAND:(h + 1) * NCAND]) for h in range(2)])

                for t in range(2):
                    if l:
                        wait_full(dve, ("eT", l - 1, t))
                    seq_(tt(seln[:, t, 2], topv[:, t], topv[:, t, :, 0:1].to_broadcast([P, HP, 16]), ALU.subtract),
                         gexp_in)
                for t in range(2):
                    pf, code, pu, start, code_step = (cand[:, (2 + i) * P:(3 + i) * P] for i in range(5))
                    pu = pu.bitcast(U32)
                    heads = "p (h k) -> p h k"
                    e = eq.rearrange("p (m a) -> p m a", a=16)
                    e4 = eq.rearrange("p (h k a) -> p h k a", h=HP, a=16)
                    seq_(stt(code.rearrange(heads, h=HP), i1f[:, t, 0], float(NCAND),
                             row_start[:, :].unsqueeze(1).to_broadcast([P, HP, 16]), ALU.mult, ALU.add))
                    c3, s3 = code.rearrange(heads, h=HP), code_step.rearrange(heads, h=HP)
                    seq_.lag(dve.tensor_copy(s3[:, :, 0], c3[:, :, 0]))
                    seq_.lag(tt(s3[:, :, 1:16], c3[:, :, 1:16], c3[:, :, 0:15], ALU.subtract))
                    seq_(dve.tensor_copy(pf, posu[:, t].rearrange("p h k -> p (h k)")))
                    seq_(tt(e, pf.unsqueeze(2).to_broadcast([P, 128, 16]),
                            row_start[:, :].unsqueeze(1).to_broadcast([P, 128, 16]), ALU.is_ge))
                    seq_(tt(e4, e4, s3.unsqueeze(2).to_broadcast([P, HP, 16, 16]), ALU.mult))
                    seq_(dve.tensor_reduce(code, e, AX.X, ALU.add))
                    seq_(dve.tensor_copy(pu, code))
                    seq_(ts(pu, pu, NCAND - 1, None, ALU.bitwise_and))
                    seq_(dve.tensor_copy(start, pu))
                    seq_.lag(tt(pf, pf, start, ALU.subtract))
                    seq_.lag(tt(code, code, start, ALU.subtract))
                    seq_.settle()
                    seq_.lag(ts(seln[:, t, 0, :, :].rearrange("p h k -> p (h k)"), code, 1.0 / NCAND, None, ALU.mult))
                    seq_.lag(tt(e, pf.unsqueeze(2).to_broadcast([P, 128, 16]),
                                iota[:, 0:16].unsqueeze(1).to_broadcast([P, 128, 16]), ALU.is_equal))
                    seq_.settle()
                    seq_(tt(e4, e4, i1f[:, t, 1].unsqueeze(2).to_broadcast([P, HP, 16, 16]), ALU.mult))
                    seq_(dve.tensor_reduce(seln[:, t, 1, :, :].rearrange("p h k -> p (h k)"), e, AX.X, ALU.add))
                for t in range(2):
                    g = seln[:, t, 2]
                    dve.wait_ge(gexp_done, 2 * l + t + 1)
                    seq_(dve.tensor_reduce(rs[:, 0:HP], g, AX.X, ALU.add))
                    seq_(dve.reciprocal(rs[:, 8:16], rs[:, 0:HP]))
                    seq_(tt(g, g, rs[:, 8:16].unsqueeze(2).to_broadcast([P, HP, 16]), ALU.mult), sel_ready)

                dve.wait_ge(selT_ready, 2 * (l + 1))
                if l == 0:
                    for i in range(2):
                        dve.wait_ge(mod_stored[i], 16 * (len(mod_order) // 2))

                def hot_batch(n, t0, k):
                    dve.wait_ge(gated, n + (l * NBATCH + 1))
                    dve.wait_ge(hot2_cast, n + (l * NBATCH + 1))
                    for r in range(2):
                        e = pickT[:, r, bass.ds(t0, BT)].unsqueeze(1).to_broadcast([P, NK, BT])
                        ins = tt(hot_picks(k)[:, r], ramp[:, :, :], e, ALU.is_equal)
                        if r == 0:
                            ins.then_inc(hot_ready, 1)
                        else:
                            ins.then_inc(hot2_ready, 1)

                def scale_batch(n, t0, k):
                    dve.wait_ge(gate_stored, n + (l * NBATCH + 5))
                    a = gates[:, 0:EARLY[l], bass.ds(t0, BT)].rearrange("p i t -> p t i")
                    g = ps[:, k % 4, :].rearrange("p (t i) -> p t i", i=P)[:, :, 0:EARLY[l]]
                    tt(a, a, g, ALU.mult).then_inc(gate_scaled, 1)

                if EARLY[l]:
                    if not scaled_before[l]:
                        dve.sem_inc(gate_scaled, 4)
                    dve.wait_ge(gelu_done, l * NSTEP + EARLY[l])
                    lagged_batches(dve, hot_batch, scale_batch, 4)
                    dve.wait_ge(gate_scaled, scaled_before[l] + NBATCH + 4)
                else:
                    gate_batches(dve, hot_batch)

                def split_uT(j, k):
                    jj = j + l * NSTEP
                    for q in range(2):
                        dve.wait_ge(uThi_done, jj * 2 + (q + 1))
                        hi = uT_hi[:, 4 * q:4 * q + 4, :].rearrange("p k e -> p (k e)")
                        lo = uT_lo[:, 4 * q:4 * q + 4, :].rearrange("p k e -> p (k e)")
                        tt(lo, ps[:, q, :], hi.bitcast(F32), ALU.subtract).then_inc(uTlo_done, 1)

                split_uT(EARLY[l], EARLY[l])

                def split_v(j, k):
                    s = k % 2
                    dve.wait_ge(vhi_done, j + (l * NSTEP + 1))
                    tt(v_lo[:, s, :], v_raw[:, s, :], v_hi[:, s, :].bitcast(F32), ALU.subtract).then_inc(vlo_done, 1)

                def gate_row(j):
                    return gates[:, j, :] if isinstance(j, int) else \
                        gates[:, bass.ds(j, 1), :].rearrange("p a t -> p (a t)")

                def early_step(j, k):
                    s = k % 2
                    split_v(j, k)
                    seq_(dve.tensor_copy(c_hi[:, s, :], gate_row(j)))
                    tt(c_lo[:, s, :], gate_row(j), c_hi[:, s, :].bitcast(F32), ALU.subtract).then_inc(c_done, 1)

                def step(j, k):
                    jj = j + l * NSTEP
                    s = k % 2
                    split_v(j, k)
                    if k < NSTEP - 1:
                        split_uT(j + 1, k + 1)
                    dve.wait_ge(gelu_done, jj + 1)
                    seq_(tt(gel[:, s, :], gel[:, s, :], gate_row(j), ALU.mult))
                    seq_(dve.tensor_copy(c_hi[:, s, :], gel[:, s, :]))
                    tt(c_lo[:, s, :], gel[:, s, :], c_hi[:, s, :].bitcast(F32), ALU.subtract).then_inc(c_done, 1)

                if EARLY[l]:
                    tile_steps(dve, seq_, {dve_step: 4}, early_step, 0, EARLY[l])
                tile_steps(dve, seq_, {dve_step: 8}, step, EARLY[l], NSTEP)

                dve.wait_ge(y_mm, NSTEP * (l + 1))
                dve.wait_ge(gate_landed, 32 * (l + 1))
                for t in range(2):
                    for q in range(2):
                        cols = slice(q * 512, q * 512 + 512)
                        gy = gel[:, :, :].rearrange("p a n -> p (a n)")
                        seq_(tt(gy, ps[:, 4 + 2 * t + q, :], gmod[:, cols], ALU.mult))
                        seq_(tt(xs[:, t, cols], xs[:, t, cols], gy, ALU.add), x_done if q else None)


CONV_ORDER = (2, 3, 0, 1)

POOL_TAPS = (19, 24)

DOTS = [(0, (0, 2, 4, 6), 128), (0, (1, 3, 5, 7), 128),
        (1, (0, 2), 256), (1, (4, 6), 256), (1, (1, 3), 256), (1, (5, 7), 256)]

_INS = ["x", "c", "positions", "w_ada", "b_ada", "w_in", "q_norm_g", "k_norm_g", "idx_k_ln_g",
        "idx_k_ln_b", "conv_dw", "conv_b", "conv_ln_g", "conv_ln_b", "out_g_attn", "out_g_conv",
        "w_out", "peer_wq", "peer_sub_keys", "peer_u", "peer_v"]


def kernel(**inputs):
    import concourse.bacc as bacc
    from concourse.bass_utils import run_bass_kernel_spmd

    nc = bacc.Bacc("TRN2", target_bir_lowering=False, num_devices=1)
    arrays, args = {}, {}
    for name in _INS:
        a = np.ascontiguousarray(inputs[name])
        arrays[f"in_{name}"] = a
        args[name] = nc.dram_tensor(f"in_{name}", a.shape, mybir.dt.from_np(a.dtype), kind="ExternalInput").ap()
    o = nc.dram_tensor("out_x", inputs["x"].shape, F32, kind="ExternalOutput").ap()
    trunk(nc, out=o, **args)
    r = run_bass_kernel_spmd(nc, [arrays], core_ids=[0])
    return r.results[0]["out_x"]
```
